# Optimizing a Trainium2 kernel written in Bass

```python
import jax, jax.numpy as jnp
from jax import lax
import numpy as np
import math

D_MODEL = 1024
BATCH = 1
SEQ = 512
DEPTH = 2

N_A_LAYERS = DEPTH // 2
N_B_LAYERS = DEPTH - N_A_LAYERS

HEAD_DIM = 64
EPS = 1e-6
ROPE_THETA = 10000.0

MLSTM_HEADS = 4
MLSTM_DV = (3 * D_MODEL // 4) // MLSTM_HEADS
MLSTM_DQK = MLSTM_DV // 2
MLSTM_QK_W = MLSTM_HEADS * MLSTM_DQK
MLSTM_V_W = MLSTM_HEADS * MLSTM_DV
MLSTM_CHUNK = 64
GATE_SOFTCAP = 15.0
M_INIT = -1e30

SWA_Q_HEADS = (3 * D_MODEL // 4) // HEAD_DIM
SWA_KV_HEADS = 4
SWA_Q_W = SWA_Q_HEADS * HEAD_DIM
SWA_KV_W = SWA_KV_HEADS * HEAD_DIM
SWA_WINDOW = 128

MEM_TOKENS = 256
MEM_HEADS = 4
MEM_HEAD_DIM = (D_MODEL // 4) // MEM_HEADS
MEM_W = MEM_HEADS * MEM_HEAD_DIM

A_IN_W = 2 * MLSTM_QK_W + 2 * MLSTM_V_W + 2 * MLSTM_HEADS + MEM_W
B_IN_W = SWA_Q_W + MEM_W
MIX_W = MLSTM_V_W + MEM_W

D_FF = ((8 * D_MODEL // 3 + 255) // 256) * 256


def rmsnorm(x, g):
    xf = x.astype(jnp.float32)
    y = xf * lax.rsqrt(jnp.mean(xf * xf, axis=-1, keepdims=True) + EPS)
    return (y * g.astype(jnp.float32)).astype(x.dtype)

def rope_tables(positions):
    inv = 1.0 / (ROPE_THETA ** (jnp.arange(0, HEAD_DIM, 2, dtype=jnp.float32) / HEAD_DIM))
    ang = positions.astype(jnp.float32)[..., None] * inv
    return jnp.cos(ang), jnp.sin(ang)

def apply_rope(t, cos, sin):
    t1, t2 = jnp.split(t.astype(jnp.float32), 2, axis=-1)
    c = cos[:, :, None, :]
    s = sin[:, :, None, :]
    return jnp.concatenate([t1 * c - t2 * s, t2 * c + t1 * s], axis=-1).astype(t.dtype)

def mlstm_chunkwise(q, k, v, i_pre, f_pre):
    f32 = jnp.float32
    B_, S_, H, dqk = q.shape
    L = MLSTM_CHUNK
    NC = S_ // L

    def chunks(t):
        return t.astype(f32).reshape(B_, NC, L, H, -1).transpose(0, 3, 1, 2, 4)

    qc = chunks(q)
    kc = chunks(k) * (dqk ** -0.5)
    vc = chunks(v)
    ig = i_pre.astype(f32).reshape(B_, NC, L, H).transpose(0, 3, 1, 2)
    logf = jax.nn.log_sigmoid(f_pre.astype(f32)).reshape(B_, NC, L, H).transpose(0, 3, 1, 2)
    b = jnp.cumsum(logf, axis=-1)
    g = b[..., -1]
    a = g[..., None] - b + ig

    def step(carry, inp):
        C, n, m = carry
        g_c, a_c, k_c, v_c = inp
        m_new = jnp.maximum(g_c + m, jnp.max(a_c, axis=-1))
        decay = jnp.exp(g_c + m - m_new)
        w = jnp.exp(a_c - m_new[..., None])
        C_new = decay[..., None, None] * C + jnp.einsum('bhl,bhlv,bhlk->bhvk', w, v_c, k_c)
        n_new = decay[..., None] * n + jnp.einsum('bhl,bhlk->bhk', w, k_c)
        return (C_new, n_new, m_new), (C, n, m)

    dv = v.shape[-1]
    init = (jnp.zeros((B_, H, dv, dqk), f32), jnp.zeros((B_, H, dqk), f32), jnp.full((B_, H), M_INIT, f32))
    xs = (g.transpose(2, 0, 1), a.transpose(2, 0, 1, 3), kc.transpose(2, 0, 1, 3, 4), vc.transpose(2, 0, 1, 3, 4))
    _, (C_st, n_st, m_st) = lax.scan(step, init, xs)
    C_st = C_st.transpose(1, 2, 0, 3, 4)
    n_st = n_st.transpose(1, 2, 0, 3)
    m_st = m_st.transpose(1, 2, 0)

    causal = jnp.tril(jnp.ones((L, L), dtype=bool))
    dmat = jnp.where(causal, b[..., :, None] - b[..., None, :] + ig[..., None, :], -jnp.inf)
    inter_log = b + m_st[..., None]
    m_row = jnp.maximum(inter_log, jnp.max(dmat, axis=-1))
    scores = jnp.einsum('bhcjd,bhcsd->bhcjs', qc, kc) * jnp.exp(dmat - m_row[..., None])
    inter_w = jnp.exp(inter_log - m_row)
    num = (jnp.einsum('bhcjs,bhcsv->bhcjv', scores, vc)
           + inter_w[..., None] * jnp.einsum('bhcjk,bhcvk->bhcjv', qc, C_st))
    den = jnp.sum(scores, axis=-1) + inter_w * jnp.einsum('bhcjk,bhck->bhcj', qc, n_st)
    h = num / jnp.maximum(jnp.abs(den), jnp.exp(-m_row))[..., None]
    return h.transpose(0, 2, 3, 1, 4).reshape(B_, S_, H, dv)

def mlstm_mixer(h, w_in, b_gates, g_out):
    B_, S_, _ = h.shape
    p = h @ w_in
    q, k, v, o, gates, mq = jnp.split(
        p, [MLSTM_QK_W, 2 * MLSTM_QK_W, 2 * MLSTM_QK_W + MLSTM_V_W, 2 * MLSTM_QK_W + 2 * MLSTM_V_W,
            2 * MLSTM_QK_W + 2 * MLSTM_V_W + 2 * MLSTM_HEADS], axis=-1)
    gates = gates.astype(jnp.float32) + b_gates.astype(jnp.float32)
    gates = GATE_SOFTCAP * jnp.tanh(gates / GATE_SOFTCAP)
    i_pre, f_pre = jnp.split(gates, 2, axis=-1)
    hm = mlstm_chunkwise(q.reshape(B_, S_, MLSTM_HEADS, MLSTM_DQK), k.reshape(B_, S_, MLSTM_HEADS, MLSTM_DQK),
                         v.reshape(B_, S_, MLSTM_HEADS, MLSTM_DV), i_pre, f_pre)
    hm = hm * lax.rsqrt(jnp.mean(hm * hm, axis=-1, keepdims=True) + EPS)
    hm = hm * g_out.astype(jnp.float32).reshape(MLSTM_HEADS, MLSTM_DV)
    hm = jax.nn.sigmoid(o.astype(jnp.float32)) * hm.reshape(B_, S_, MLSTM_V_W)
    return hm.astype(h.dtype), mq.reshape(B_, S_, MEM_HEADS, MEM_HEAD_DIM)

def swa_sink_attention(q, k, v, sinks):
    B_, S_, Hq, dh = q.shape
    Hkv = k.shape[2]
    G = Hq // Hkv
    W = SWA_WINDOW
    NB = S_ // W
    qb = q.reshape(B_, NB, W, Hkv, G, dh)

    def band(t):
        tb = jnp.pad(t, ((0, 0), (W, 0), (0, 0), (0, 0))).reshape(B_, NB + 1, W, Hkv, dh)
        return jnp.concatenate([tb[:, :-1], tb[:, 1:]], axis=2)

    kband = band(k)
    vband = band(v)
    s = jnp.einsum('bnqhgd,bnkhd->bnhgqk', qb, kband).astype(jnp.float32) * (dh ** -0.5)
    qpos = jnp.arange(W)[:, None] + W
    kpos = jnp.arange(2 * W)[None, :]
    diff = qpos - kpos
    in_band = (diff >= 0) & (diff < W)
    blk = jnp.arange(NB)[:, None, None]
    valid = in_band[None] & (blk * W + kpos[None] - W >= 0)
    s = jnp.where(valid[None, :, None, None, :, :], s, -jnp.inf)
    sink = sinks.astype(jnp.float32).reshape(Hkv, G)[None, None, :, :, None, None]
    m = jnp.maximum(jnp.max(s, axis=-1, keepdims=True), sink)
    p = jnp.exp(s - m)
    p = p / (jnp.sum(p, axis=-1, keepdims=True) + jnp.exp(sink - m))
    o = jnp.einsum('bnhgqk,bnkhd->bnqhgd', p.astype(v.dtype), vband)
    return o.reshape(B_, S_, Hq * dh)

def swa_mixer(h, w_in, sinks, k_sh, v_sh, cos, sin):
    B_, S_, _ = h.shape
    p = h @ w_in
    q, mq = jnp.split(p, [SWA_Q_W], axis=-1)
    q = apply_rope(q.reshape(B_, S_, SWA_Q_HEADS, HEAD_DIM), cos, sin)
    o = swa_sink_attention(q, k_sh, v_sh, sinks)
    return o, mq.reshape(B_, S_, MEM_HEADS, MEM_HEAD_DIM)

def memory_attention(mq, mk, mv):
    B_, S_, Hm, dh = mq.shape
    s = jnp.einsum('bqhd,bmhd->bhqm', mq, mk).astype(jnp.float32) * (dh ** -0.5)
    p = jax.nn.softmax(s, axis=-1)
    o = jnp.einsum('bhqm,bmhd->bqhd', p.astype(mv.dtype), mv)
    return o.reshape(B_, S_, Hm * dh)

def shared_kv(x, g_kv, w_kv, cos, sin):
    B_, S_, _ = x.shape
    kv = rmsnorm(x, g_kv) @ w_kv
    k, v = jnp.split(kv, 2, axis=-1)
    k = apply_rope(k.reshape(B_, S_, SWA_KV_HEADS, HEAD_DIM), cos, sin)
    return k, v.reshape(B_, S_, SWA_KV_HEADS, HEAD_DIM)

def swiglu(h, w_in, w_out):
    gate, up = jnp.split(h @ w_in, 2, axis=-1)
    return (jax.nn.silu(gate) * up) @ w_out

def first_inputs(seed: int = 0) -> dict:
    key = jax.random.key(seed)
    ks = jax.random.split(key, 24)
    f32 = jnp.float32

    def w(k, shape, fan_in):
        return jax.random.normal(k, shape, f32) * (fan_in ** -0.5)

    def gain(k, shape):
        return 1.0 + 0.05 * jax.random.normal(k, shape, f32)

    x = jax.random.normal(ks[0], (BATCH, SEQ, D_MODEL), f32)
    mem = jax.random.normal(ks[1], (BATCH, MEM_TOKENS, D_MODEL), f32)
    offset = jax.random.randint(ks[2], (BATCH,), 0, 1024, dtype=jnp.int32)
    positions = (offset[:, None] + jnp.arange(SEQ, dtype=jnp.int32)[None, :]).astype(jnp.int32)

    i_bias = 0.1 * jax.random.normal(ks[3], (N_A_LAYERS, MLSTM_HEADS), f32)
    f_bias = 3.0 + 3.0 * jax.random.uniform(ks[4], (N_A_LAYERS, MLSTM_HEADS), f32)
    return {
        "x": x,
        "mem": mem,
        "positions": positions,
        "g_mix_pre": gain(ks[5], (DEPTH, D_MODEL)),
        "g_mix_post": gain(ks[6], (DEPTH, D_MODEL)),
        "g_ffn_pre": gain(ks[7], (DEPTH, D_MODEL)),
        "g_ffn_post": gain(ks[8], (DEPTH, D_MODEL)),
        "g_mem": gain(ks[9], (DEPTH, D_MODEL)),
        "w_mem_kv": w(ks[10], (DEPTH, D_MODEL, 2 * MEM_W), D_MODEL),
        "w_out": w(ks[11], (DEPTH, MIX_W, D_MODEL), MIX_W),
        "w_ffn_in": w(ks[12], (DEPTH, D_MODEL, 2 * D_FF), D_MODEL),
        "w_ffn_out": w(ks[13], (DEPTH, D_FF, D_MODEL), D_FF),
        "w_in_a": w(ks[14], (N_A_LAYERS, D_MODEL, A_IN_W), D_MODEL),
        "b_gates_a": jnp.concatenate([i_bias, f_bias], axis=-1),
        "g_mlstm_out": gain(ks[15], (N_A_LAYERS, MLSTM_V_W)),
        "g_kv": gain(ks[16], (D_MODEL,)),
        "w_kv": w(ks[17], (D_MODEL, 2 * SWA_KV_W), D_MODEL),
        "w_in_b": w(ks[18], (N_B_LAYERS, D_MODEL, B_IN_W), D_MODEL),
        "sinks_b": 0.5 * jax.random.normal(ks[19], (N_B_LAYERS, SWA_Q_HEADS), f32),
    }

def first_block(x, mem, positions, g_mix_pre, g_mix_post, g_ffn_pre, g_ffn_post, g_mem, w_mem_kv, w_out,
              w_ffn_in, w_ffn_out, w_in_a, b_gates_a, g_mlstm_out, g_kv, w_kv, w_in_b, sinks_b):
    B_ = x.shape[0]
    cos, sin = rope_tables(positions)
    k_sh = None
    v_sh = None
    for l in range(DEPTH):
        h = rmsnorm(x, g_mix_pre[l])
        mk, mv = jnp.split(rmsnorm(mem, g_mem[l]) @ w_mem_kv[l], 2, axis=-1)
        mk = mk.reshape(B_, MEM_TOKENS, MEM_HEADS, MEM_HEAD_DIM)
        mv = mv.reshape(B_, MEM_TOKENS, MEM_HEADS, MEM_HEAD_DIM)
        if l < N_A_LAYERS:
            main, mq = mlstm_mixer(h, w_in_a[l], b_gates_a[l], g_mlstm_out[l])
        else:
            j = l - N_A_LAYERS
            main, mq = swa_mixer(h, w_in_b[j], sinks_b[j], k_sh, v_sh, cos, sin)
        mo = memory_attention(mq, mk, mv)
        mix = jnp.concatenate([main, mo], axis=-1) @ w_out[l]
        x = x + rmsnorm(mix, g_mix_post[l])
        x = x + rmsnorm(swiglu(rmsnorm(x, g_ffn_pre[l]), w_ffn_in[l], w_ffn_out[l]), g_ffn_post[l])
        if l == N_A_LAYERS - 1:
            k_sh, v_sh = shared_kv(x, g_kv, w_kv, cos, sin)
    return x


CHUNK = 64
Q_BLOCK = 128
N_MIXERS = 2
HEAD_DIM_2 = 128
N_MEM = 256
MEM_WIDTH = MEM_HEADS * HEAD_DIM_2
MIX_WIDTH = 2 * D_MODEL
CONV_WIDTH = MIX_WIDTH - MEM_WIDTH
CONV_KERNEL = 31
ATT_HEADS = (MIX_WIDTH - MEM_WIDTH) // HEAD_DIM_2
ATT_WIDTH = ATT_HEADS * HEAD_DIM_2
IDX_HEADS = 8
IDX_DIM = 64
TOPK_MAX = 256
ALPHA = (2 * DEPTH) ** 0.25
BETA = (8 * DEPTH) ** -0.25
LN_EPS = 1e-5
NEG = -1e30

A_SIZES = (2 * CONV_WIDTH, MEM_WIDTH, MIX_WIDTH)
B_SIZES = (ATT_WIDTH, HEAD_DIM_2, HEAD_DIM_2, IDX_HEADS * IDX_DIM, IDX_DIM, IDX_HEADS, MEM_WIDTH, MIX_WIDTH)
A_IN = sum(A_SIZES)
B_IN = sum(B_SIZES)


def split_cols(h, sizes):
    return jnp.split(h, [int(c) for c in np.cumsum(sizes)[:-1]], axis=-1)

def layer_norm(x, g, b):
    xf = x.astype(jnp.float32)
    mu = xf.mean(-1, keepdims=True)
    var = jnp.square(xf - mu).mean(-1, keepdims=True)
    return ((xf - mu) * lax.rsqrt(var + LN_EPS) * g.astype(jnp.float32) + b.astype(jnp.float32)).astype(x.dtype)

def alibi_slopes(n):
    p = 2 ** int(math.floor(math.log2(n)))
    base = [2.0 ** (-8.0 * (i + 1) / p) for i in range(p)]
    extra = [2.0 ** (-4.0 * (2 * i + 1) / p) for i in range(n - p)]
    return jnp.asarray(base + extra, dtype=jnp.float32)

def mem_cross_attention(q, mem_n, w_mkv):
    B, T, _ = q.shape
    k, v = jnp.split(mem_n @ w_mkv, 2, axis=-1)
    q = q.reshape(B, T, MEM_HEADS, HEAD_DIM_2)
    k = k.reshape(B, -1, MEM_HEADS, HEAD_DIM_2)
    v = v.reshape(B, -1, MEM_HEADS, HEAD_DIM_2)
    s = jnp.einsum('bthd,bnhd->bhtn', q, k).astype(jnp.float32) * (HEAD_DIM_2 ** -0.5)
    p = jax.nn.softmax(s, axis=-1).astype(v.dtype)
    return jnp.einsum('bhtn,bnhd->bthd', p, v).reshape(B, T, MEM_WIDTH)

def conformer_conv(u, conv_w, conv_b, g, b):
    a, gl = jnp.split(u, 2, axis=-1)
    h = a * jax.nn.sigmoid(gl)
    h = jnp.pad(h, ((0, 0), (CONV_KERNEL - 1, 0), (0, 0)))
    h = lax.conv_general_dilated(h, conv_w[:, None, :].astype(h.dtype), (1,), 'VALID',
                                 dimension_numbers=('NWC', 'WIO', 'NWC'),
                                 feature_group_count=CONV_WIDTH) + conv_b
    return jax.nn.silu(layer_norm(h, g, b))

def dsa_attention(q, k, v, q_idx, k_idx, w_idx):
    B, T = q.shape[:2]
    topk = min(TOPK_MAX, T // 4)
    nb = T // Q_BLOCK
    slopes = alibi_slopes(ATT_HEADS)
    key_chunk = jnp.arange(T, dtype=jnp.int32) // CHUNK
    scale = HEAD_DIM_2 ** -0.5

    def to_blocks(a):
        return jnp.moveaxis(a.reshape(B, nb, Q_BLOCK, *a.shape[2:]), 1, 0)

    def block(args):
        qb, qib, wb, start = args
        qpos = start + jnp.arange(Q_BLOCK, dtype=jnp.int32)
        qchunk = qpos // CHUNK
        admiss = key_chunk[None, :] <= qchunk[:, None]
        iscore = jax.nn.relu(jnp.einsum('bqhd,bsd->bqhs', qib, k_idx).astype(jnp.float32))
        iscore = jnp.einsum('bqh,bqhs->bqs', wb.astype(jnp.float32), iscore)
        iscore = jnp.where(admiss[None], iscore, NEG)
        _, sel = lax.top_k(iscore, topk)
        valid = key_chunk[sel] <= qchunk[None, :, None]
        kg = jax.vmap(lambda kb, ib: kb[ib])(k, sel)
        vg = jax.vmap(lambda vb, ib: vb[ib])(v, sel)
        dist = jnp.abs(qpos[None, :, None] - sel).astype(jnp.float32)
        logits = jnp.einsum('bqhd,bqkd->bqhk', qb, kg).astype(jnp.float32) * scale
        logits = logits - slopes[None, None, :, None] * dist[:, :, None, :]
        logits = jnp.where(valid[:, :, None, :], logits, NEG)
        p = jax.nn.softmax(logits, axis=-1).astype(vg.dtype)
        return jnp.einsum('bqhk,bqkd->bqhd', p, vg)

    starts = jnp.arange(nb, dtype=jnp.int32) * Q_BLOCK
    out = lax.map(block, (to_blocks(q), to_blocks(q_idx), to_blocks(w_idx), starts))
    return jnp.moveaxis(out, 0, 1).reshape(B, T, ATT_WIDTH)

def second_inputs(seed: int = 0) -> dict:
    key = jax.random.key(seed)
    ks = jax.random.split(key, 24)
    n_a = (DEPTH + 1) // 2
    n_b = DEPTH // 2
    nrm = lambda k, shape, s: jax.random.normal(k, shape, jnp.float32) * s
    return {
        "x": nrm(ks[0], (BATCH, SEQ, D_MODEL), 1.0),
        "mem": nrm(ks[1], (BATCH, N_MEM, D_MODEL), 1.0),
        "mem_ln_g": 1.0 + nrm(ks[2], (D_MODEL,), 0.05),
        "mem_ln_b": nrm(ks[3], (D_MODEL,), 0.01),
        "a_w_in": nrm(ks[4], (n_a, D_MODEL, A_IN), D_MODEL ** -0.5),
        "a_conv_w": nrm(ks[5], (n_a, CONV_KERNEL, CONV_WIDTH), CONV_KERNEL ** -0.5),
        "a_conv_b": nrm(ks[6], (n_a, CONV_WIDTH), 0.01),
        "a_ln_g": 1.0 + nrm(ks[7], (n_a, CONV_WIDTH), 0.05),
        "a_ln_b": nrm(ks[8], (n_a, CONV_WIDTH), 0.01),
        "a_w_mkv": nrm(ks[9], (n_a, D_MODEL, 2 * MEM_WIDTH), D_MODEL ** -0.5),
        "a_w_out": nrm(ks[10], (n_a, MIX_WIDTH, D_MODEL), BETA * MIX_WIDTH ** -0.5),
        "a_post_g": 1.0 + nrm(ks[11], (n_a, D_MODEL), 0.05),
        "a_post_b": nrm(ks[12], (n_a, D_MODEL), 0.01),
        "b_w_in": nrm(ks[13], (n_b, D_MODEL, B_IN), D_MODEL ** -0.5),
        "b_w_mkv": nrm(ks[14], (n_b, D_MODEL, 2 * MEM_WIDTH), D_MODEL ** -0.5),
        "b_w_out": nrm(ks[15], (n_b, MIX_WIDTH, D_MODEL), BETA * MIX_WIDTH ** -0.5),
        "b_post_g": 1.0 + nrm(ks[16], (n_b, D_MODEL), 0.05),
        "b_post_b": nrm(ks[17], (n_b, D_MODEL), 0.01),
    }

def second_block(x, mem, mem_ln_g, mem_ln_b, a_w_in, a_conv_w, a_conv_b, a_ln_g, a_ln_b,
              a_w_mkv, a_w_out, a_post_g, a_post_b, b_w_in, b_w_mkv, b_w_out,
              b_post_g, b_post_b):
    B, T, _ = x.shape
    mem_n = layer_norm(mem, mem_ln_g, mem_ln_b)
    for i in range(DEPTH):
        j = i // N_MIXERS
        if i % N_MIXERS == 0:
            u, qm, gate = split_cols(x @ a_w_in[j], A_SIZES)
            y_mix = conformer_conv(u, a_conv_w[j], a_conv_b[j], a_ln_g[j], a_ln_b[j])
            w_mkv, w_out, pg, pb = a_w_mkv[j], a_w_out[j], a_post_g[j], a_post_b[j]
        else:
            q, k, v, qi, ki, wi, qm, gate = split_cols(x @ b_w_in[j], B_SIZES)
            y_mix = dsa_attention(q.reshape(B, T, ATT_HEADS, HEAD_DIM_2), k, v,
                                  qi.reshape(B, T, IDX_HEADS, IDX_DIM), ki, wi)
            w_mkv, w_out, pg, pb = b_w_mkv[j], b_w_out[j], b_post_g[j], b_post_b[j]
        y_mem = mem_cross_attention(qm, mem_n, w_mkv)
        y = jnp.concatenate([y_mix, y_mem], axis=-1) * jax.nn.silu(gate)
        x = layer_norm(ALPHA * x + y @ w_out, pg, pb)
    return x


def setup_inputs(seed=0):
    out = dict(first_inputs(seed))
    for name, value in second_inputs(seed + 1).items():
        if name != "x":
            out[name + "_2"] = value
    return out


def reference(
    x, mem, positions, g_mix_pre, g_mix_post, g_ffn_pre, g_ffn_post, g_mem, w_mem_kv, w_out,
    w_ffn_in, w_ffn_out, w_in_a, b_gates_a, g_mlstm_out, g_kv, w_kv, w_in_b, sinks_b, mem_2,
    mem_ln_g_2, mem_ln_b_2, a_w_in_2, a_conv_w_2, a_conv_b_2, a_ln_g_2, a_ln_b_2, a_w_mkv_2,
    a_w_out_2, a_post_g_2, a_post_b_2, b_w_in_2, b_w_mkv_2, b_w_out_2, b_post_g_2, b_post_b_2,
):
    x = first_block(
        x, mem, positions, g_mix_pre, g_mix_post, g_ffn_pre, g_ffn_post, g_mem, w_mem_kv, w_out,
        w_ffn_in, w_ffn_out, w_in_a, b_gates_a, g_mlstm_out, g_kv, w_kv, w_in_b, sinks_b,
    )
    return second_block(
        x, mem_2, mem_ln_g_2, mem_ln_b_2, a_w_in_2, a_conv_w_2, a_conv_b_2, a_ln_g_2, a_ln_b_2,
        a_w_mkv_2, a_w_out_2, a_post_g_2, a_post_b_2, b_w_in_2, b_w_mkv_2, b_w_out_2,
        b_post_g_2, b_post_b_2,
    )


_drawn_inputs = setup_inputs


def setup_inputs(seed=0):
    import zlib

    import numpy as np

    out = dict(_drawn_inputs(seed))
    spreads = {}
    factors = {'sinks_b': 6.921,
     'mem_ln_g_2': 7.032,
     'mem_ln_b_2': 8.0,
     'a_conv_b_2': 8.0,
     'a_ln_g_2': 6.067,
     'a_ln_b_2': 8.0,
     'a_post_b_2': 3.908,
     'b_w_mkv_2': 4.938,
     'b_post_b_2': 5.681}
    for name, (base, spread) in spreads.items():
        noise = np.random.default_rng([zlib.crc32(name.encode()), seed]).standard_normal(out[name].shape)
        drawn = base * np.exp(spread * noise) if base else spread * noise
        out[name] = __import__('jax').numpy.asarray(drawn.astype(out[name].dtype))
    for name, factor in factors.items():
        out[name] = (out[name] * factor).astype(out[name].dtype)
    return out
```

```python
import math
from contextlib import contextmanager

import numpy as np

import concourse.bass as bass
from concourse import mybir

F32 = mybir.dt.float32
F32R = mybir.dt.float32r
I32 = mybir.dt.int32
ALU = mybir.AluOpType
ACT = mybir.ActivationFunctionType
AX = mybir.AxisListType
ENG = mybir.EngineType

P = 128
D = 1024
KB = D // P
SEQ = 512
NT = SEQ // P
MEMT = 2
MEM = MEMT * P
EPS = 1e-6
LN_EPS = 1e-5
NEG = -1e30
UNIT = 2048

LH, LQK, LV = 4, 96, 192
A_IN = 2 * LH * LQK + 2 * LH * LV + 2 * LH + 256
A_CHUNK = A_IN // 6
COL_V, COL_O = 2 * LH * LQK, 2 * LH * LQK + LH * LV
COL_GATE = COL_O + LH * LV
COL_MQ = COL_GATE + 2 * LH
SOFTCAP = 15.0
SH, SKV, HD = 12, 4, 64
DFF = 2816
FB = DFF // P

CONVW, TAPS = 1536, 31
CB = CONVW // P
AH = 12
IH, IHD = 8, 64
TOPK = SEQ // 4
MIXB = 2048 // P
ALPHA = 4.0 ** 0.25

GC_MIX, GC_FFN, GC_KV, GC_MEM, GC_LNG, GC_LNB = (0, 8), (16, 24), 32, (40, 48), 56, 64
GC_TAP = 72
GC_CB = GC_TAP + CB * TAPS
GC_CG, GC_CBETA = GC_CB + CB, GC_CB + 2 * CB
N_COLS = GC_CB + 3 * CB

R_MIXPOST, R_FFNPOST = (0, 2048), (1024, 3072)
R_APG, R_APB, R_BPG, R_BPB = 4096, 5120, 6144, 7168
R_MLSTM = 8192
R_GATE = R_MLSTM + LH * LV
R_SINK = R_GATE + 2 * LH
N_ROWS = R_SINK + SH

K_ID, K_ONE, K_TRI, K_SWA, K_CAUS, K_ADM, K_DIST, K_INV, K_SLOPE = (
    0, 128, 256, 384, 640, 1152, 1280, 1792, 1824)
N_CONST = K_SLOPE + AH


def alibi_slopes(n):
    p = 2 ** int(math.floor(math.log2(n)))
    return [2.0 ** (-8.0 * (i + 1) / p) for i in range(p)] + \
           [2.0 ** (-4.0 * (2 * i + 1) / p) for i in range(n - p)]


def constants():
    c = np.zeros((P, N_CONST), np.float32)
    q = np.arange(P)[:, None]
    k = np.arange(P)[None, :]
    c[:, K_ID:K_ID + P] = np.eye(P)
    c[:, K_ONE:K_ONE + P] = 1.0
    c[:, K_TRI:K_TRI + P] = q <= k
    causal = np.where(k <= q, 0.0, NEG)
    c[:, K_SWA:K_SWA + P] = np.where(k > q, 0.0, NEG)
    c[:, K_SWA + P:K_SWA + 2 * P] = causal
    c[:, K_CAUS + 384:K_CAUS + 512] = causal
    c[:, K_ADM:K_ADM + P] = np.where((k >= 64) & (q < 64), NEG, 0.0)
    c[:, K_DIST:K_DIST + 512] = np.abs(q - np.arange(512)[None, :] + 384)
    inv = np.float32(1.0) / np.power(np.float32(10000.0), np.arange(0, 64, 2, dtype=np.float32) / np.float32(64))
    c[:, K_INV:K_INV + 32] = inv[None, :]
    c[:, K_SLOPE:K_SLOPE + AH] = -np.asarray(alibi_slopes(AH), np.float32)[None, :] * P ** 0.5
    return c


class Signal:

    every = []

    def __init__(self, nc, name):
        self.sem, self.n, self.trip = nc.alloc_semaphore(name), 0, None
        Signal.every.append(self)

    def value(self, more=0):
        n = self.n + more
        return n if self.trip is None else self.trip + n

    def now(self, more=0):
        return self.sem, self.value(more)

    def mark(self, ins, by=1):
        ins.then_inc(self.sem, by)
        return self.expect(by)

    def expect(self, by):
        self.n += by
        return self.now()


@contextmanager
def loop(nc, trips, engines, per_trip):
    before = {s: s.n for s in Signal.every}
    with nc.Fori(0, trips, engines=engines) as i:
        for s, by in per_trip.items():
            s.trip = i * by
        yield i
    real = {s: s.n - before[s] for s in Signal.every if s.n != before[s]}
    assert real == {s: b for s, b in per_trip.items() if b}, {s.sem.name: b for s, b in real.items()}
    for s, by in per_trip.items():
        s.trip, s.n = None, before[s] + trips * by


def wait(engine, *tokens):
    for sem, value in tokens:
        if isinstance(value, int) and value <= 0:
            continue
        engine.wait_ge(sem, value)


def build(nc, x_in, mem_in, mem2_in, pos_in, cols_in, rows_in, const_in, weights_in, out):
    pe, act, dve, pool, sp = nc.tensor, nc.scalar, nc.vector, nc.gpsimd, nc.sync
    Signal.every = []
    sig = lambda name: Signal(nc, name)
    loaded = sig("loaded")
    pooled = sig("pool_loads")
    rows = sig("rows")
    raw = [sig("raw_even"), sig("raw_odd")]
    hi, lo = sig("split_hi"), sig("split_lo")
    used = sig("unit_used")
    full = sig("group_full")
    free = [sig(f"bank{b}_read") for b in range(8)]
    A, V, G = sig("act_done"), sig("dve_done"), sig("pool_done")
    n_units = weights_in.shape[0]

    at = [16512]

    def place(name, shape, dtype=F32, offset=None):
        size = 4 * int(np.prod(shape[1:]))
        if offset is None:
            offset, at[0] = at[0], at[0] + (size + 31) // 32 * 32
        return nc.alloc_sbuf_tensor_at(name, shape, dtype, offset=offset)

    const = place("const", [P, N_CONST])
    cols = place("cols", [P, N_COLS])
    row_a = place("row_a", [P, D])
    row_b = place("row_b", [P, D])
    small = place("small", [P, 256])
    rotary = place("rotary", [P, 2, NT, 32])
    minus_half = small[:, 240:256]
    small_rows = place("small_rows", [P, 32])
    x_res = place("x_res", [P, NT, D])
    x_base = at[0]
    XH = place("XH", [P, KB, SEQ], F32R)
    XL = place("XL", [P, KB, SEQ], F32R)
    RAW = [place(f"RAW{j}", [P, UNIT]) for j in range(2)]
    WH = [place(f"WH{j}", [P, UNIT], F32R) for j in range(2)]
    WL = [place(f"WL{j}", [P, UNIT], F32R) for j in range(2)]
    big = at[0]
    BIG = (229344 - big) // 32 * 32
    assert BIG >= 2 * FB * SEQ * 4, BIG
    S_buf = [place(f"S{j}", [P, SEQ], offset=x_base + 2048 * j) for j in range(4)]
    T_buf = [place(f"T{j}", [P, SEQ], offset=x_base + 8192 + 2048 * j) for j in range(4)]
    scratch = [S_buf, T_buf]
    c_row = place("c_row", [P, LH, SEQ], offset=x_base + 16384)
    scr = place("scr", [P, 2048], offset=x_base + 24576)
    mix_x = place("mix_x", [P, NT, D], offset=x_base)
    HH = place("HH", [P, FB, SEQ], F32R, offset=big)
    HL = place("HL", [P, FB, SEQ], F32R, offset=big + FB * SEQ * 4)
    xn = place("xn", [P, NT, D], offset=big + BIG - 16384)
    mix_b = place("mix_b", [P, NT, D], offset=big)
    proj = place("proj", [P, NT, A_IN], offset=big)
    mem_kv1 = place("mem_kv1", [P, 2, 2, 256], offset=big + 41088)
    qkT = place("qkT", [P, 2 * LH, SEQ], offset=big + 45184)
    mixed = place("mixed", [P, NT, D], offset=big + 61568)
    mqT = place("mqT", [P, 2, SEQ], offset=big + 77952)
    q_tok = place("q_tok", [P, NT, D], offset=big)
    kv_tok = place("kv_tok", [P, NT, 2 * SKV * HD], offset=big + 16384)
    kT = place("kT", [P, 2, SEQ], offset=big + 24576)
    kT_swapped = place("kT_swapped", [P, 2, SEQ], offset=big + 28672)
    qT = place("qT", [P, KB, SEQ], offset=big + 45184)
    Y = place("Y", [P, MIXB, SEQ], offset=big)
    gate = place("gate", [P, MIXB, SEQ], offset=big + 32768)
    S_gate = [place(f"Sg{j}", [P, SEQ], offset=big + 32768 + 2048 * j) for j in range(4)]
    T_gate = [place(f"Tg{j}", [P, SEQ], offset=big + 40960 + 2048 * j) for j in range(4)]
    YH = place("YH", [P, KB, SEQ], F32R, offset=big + 32768)
    YL = place("YL", [P, KB, SEQ], F32R, offset=big + 49152)
    misc = big + 65536
    mk2 = place("mk2", [P, 4, MEM], offset=misc)
    mv2 = place("mv2", [P, MEMT, 4 * P], offset=misc + 4096)
    PAD = TAPS - 1
    conv_in = place("conv_in", [P, CB, SEQ + PAD], offset=misc)
    assert 65536 + 4 * CB * (SEQ + PAD) <= BIG
    dkT = place("dkT", [P, SEQ], offset=misc)
    dvT = place("dvT", [P, SEQ], offset=misc + 2048)
    d_val = place("d_val", [P, NT, P], offset=misc + 4096)
    qiT = place("qiT", [P, 4, SEQ], offset=misc + 6144)
    kiT = place("kiT", [P, SEQ], offset=misc + 14336)
    wiT = place("wiT", [P, SEQ], offset=misc + 16384)
    sel_at = [0, 128, 384, 768]
    sel = place("sel", [P, 1280], offset=misc + 18432)
    wi = place("wi", [P, NT, IH], offset=misc + 23552)
    top8 = place("top8", [P, 8], offset=misc + 23680)

    bank = [nc.alloc_psum_tensor(f"bank{b}", [P, SEQ], F32) for b in range(8)]
    ring = [0, 0]

    def product_bank():
        b = ring[0] % 4
        ring[0] += 1
        wait(pe, free[b].now())
        return b

    def spare_bank():
        b = 4 + ring[1] % 4
        ring[1] += 1
        wait(pe, free[b].now())
        return b

    ident = const[:, K_ID:K_ID + P]
    ones = const[:, K_ONE:K_ONE + P]

    def col(base, k):
        return cols[:, base + k:base + k + 1]

    wait(pool, G.mark(pool.memset(minus_half, -0.5)))

    loaded.mark(sp.dma_start(const[:, :], const_in), 16)
    loaded.mark(sp.dma_start(cols[:, :], cols_in), 16)
    pos = place("pos", [P, NT], I32, offset=x_base)
    t_pos = loaded.mark(sp.dma_start(pos[:, :], pos_in), 16)
    mem_tok = place("mem_tok", [P, MEMT, D], offset=big + BIG - 32768)
    t_mem = loaded.mark(sp.dma_start(mem_tok[:, :, :], mem_in[0].rearrange("(t p) d -> p t d", p=P)), 16)
    t_x = loaded.mark(act.dma_start(x_res[:, :, :], x_in[0].rearrange("(t p) d -> p t d", p=P)), 16)
    t_loaded = loaded.now()
    t_rows = pooled.mark(pool.dma_start(
        small_rows[:, 0:2 * LH + SH],
        rows_in[R_GATE:N_ROWS].rearrange("(a n) -> a n", a=1).partition_broadcast(P)), 16)

    def quiet():
        return [s.now() for s in (A, V, G, full, used, lo, *free)]

    def load_row(dst, start, n=D):
        wait(pool, *quiet())
        src = rows_in[start:start + n].rearrange("(a n) -> a n", a=1).partition_broadcast(P)
        return rows.mark(pool.dma_start(dst[:, 0:n], src), 16)

    for j in range(2):
        sp.dma_start(RAW[j][:, :], weights_in[j]).then_inc(raw[j].sem, 16)
    with nc.Fori(1, n_units // 2, engines=[ENG.SP]) as i:
        for j in range(2):
            sp.wait_ge(lo.sem, i * 2 + (j - 1))
            sp.dma_start(RAW[j][:, :], weights_in[i * 2 + j]).then_inc(raw[j].sem, 16)

    def split_next():
        j = hi.n % 2
        if hi.trip is None and hi.n >= n_units:
            return
        wait(act, raw[j].expect(16), used.now())
        t = hi.mark(act.activation(WH[j][:, :], RAW[j][:, :], ACT.Copy))
        wait(dve, t)
        lo.mark(dve.tensor_tensor(WL[j][:, :], RAW[j][:, :], WH[j][:, :].bitcast(F32), ALU.subtract))

    def three_passes(ps, ah, al, bh, bl, first, last):
        pe.matmul(ps, ah, bh, start=first, stop=False)
        pe.matmul(ps, ah, bl, start=False, stop=False)
        return pe.matmul(ps, al, bh, start=False, stop=last)

    def unit_features(n, epilogue, widths=(P, P), tokens_h=XH, tokens_l=XL):
        j = used.n % 2
        wait(pe, (lo.sem, used.value(1)))
        results = []
        at_col = 0
        for c, w in enumerate(widths):
            b = product_bank()
            for kb in range(KB):
                s = slice(kb * 256 + at_col, kb * 256 + at_col + w)
                mm = three_passes(bank[b][0:w, 0:n], WH[j][:, s], WL[j][:, s],
                                  tokens_h[:, kb, 0:n], tokens_l[:, kb, 0:n], kb == 0, kb == KB - 1)
            results.append((b, (used if c == len(widths) - 1 else full).mark(mm)))
            at_col += w
        epilogue(results)
        split_next()

    def chunk_tokens(n, k_blocks, tiles, tokens, epilogue, per_unit=4):
        banks, results = [], []
        for k0 in range(0, k_blocks, per_unit):
            ks = range(k0, min(k0 + per_unit, k_blocks))
            end = ks[-1] == k_blocks - 1
            j = used.n % 2
            wait(pe, (lo.sem, used.value(1)))
            for t in range(tiles):
                if k0 == 0:
                    banks.append(product_bank())
                for kb in ks:
                    th, tl, k = tokens(kb)
                    tt = slice(t * P, (t + 1) * P)
                    s = slice((kb - k0) * n, (kb - k0 + 1) * n)
                    mm = three_passes(bank[banks[t]][:, 0:n], th[:, k, tt], tl[:, k, tt],
                                      WH[j][:, s], WL[j][:, s], kb == 0, kb == k_blocks - 1)
                if t == tiles - 1:
                    token = used.mark(mm)
                elif end:
                    token = full.mark(mm)
                if end:
                    results.append((banks[t], token))
            if end:
                epilogue(results)
            split_next()

    from_x = lambda kb: (XH, XL, kb)
    from_y = lambda kb: (XH, XL, kb) if kb < KB else (YH, YL, kb - KB)
    from_h = lambda kb: (HH, HL, kb)

    def inverse_root(v, eps):
        t = V.mark(dve.tensor_scalar(v, v, eps, None, ALU.add))
        wait(pool, t)
        t = G.mark(pool.tensor_tensor(v, v, minus_half[:, 0:v.shape[-1]], ALU.pow))
        wait(dve, t)

    def rms_scale(src, tiles, ready):
        wait(act, *ready)
        wait(dve, *ready)
        for t in range(tiles):
            if t % 2:
                A.mark(act.activation(scr[:, 0:D], src[:, t, :], ACT.Square, scale=1.0 / 32,
                                      accum_out=small[:, t:t + 1]))
            else:
                V.mark(dve.tensor_tensor_reduce(scr[:, D:2 * D], src[:, t, :], src[:, t, :], 1.0 / D, 0.0,
                                                ALU.mult, ALU.add, small[:, t:t + 1]))
            wait(act, A.now())
            wait(dve, V.now())
        wait(dve, A.now())
        inverse_root(small[:, 0:tiles], EPS)

    def turn_split(src, tiles, ready, g=None, b=None):
        n = tiles * P
        wait(pe, *ready)
        for kb in range(KB):
            k = spare_bank()
            for t in range(tiles):
                mm = pe.transpose(bank[k][:, t * P:(t + 1) * P], src[:, t, kb * P:(kb + 1) * P], ident)
            token = full.mark(mm)
            ps = bank[k][:, 0:n]
            wait(act, token)
            wait(dve, token)
            if b is not None:
                u = V.mark(dve.tensor_scalar(scr2[kb % 2][:, 0:n], ps, col(g, kb), col(b, kb), ALU.mult, ALU.add))
                wait(act, u)
                h = A.mark(act.activation(XH[:, kb, 0:n], scr2[kb % 2][:, 0:n], ACT.Copy))
                wait(dve, h)
                free[k].mark(dve.tensor_tensor(XL[:, kb, 0:n], scr2[kb % 2][:, 0:n],
                                               XH[:, kb, 0:n].bitcast(F32), ALU.subtract))
            else:
                scale = 1.0 if g is None else col(g, kb)
                h = A.mark(act.activation(XH[:, kb, 0:n], ps, ACT.Copy, scale=scale))
                wait(dve, h)
                free[k].mark(dve.scalar_tensor_tensor(out=XL[:, kb, 0:n], in0=ps, scalar=scale,
                                                      in1=XH[:, kb, 0:n].bitcast(F32),
                                                      op0=ALU.mult, op1=ALU.subtract))
        wait(pe, *[f.now() for f in free[4:]])

    scr2 = [place(f"scr2_{j}", [P, MEM], offset=big + BIG - 32768 - 1024 * (2 - j)) for j in range(2)]

    def rms_turn(src, g, ready):
        rms_scale(src, NT, ready)
        for t in range(NT):
            token = V.mark(dve.tensor_scalar(xn[:, t, :], src[:, t, :], small[:, t:t + 1], None, ALU.mult))
        turn_split(xn, NT, [token], g=g)

    def post_norm_add(mix, ready, row):
        rms_scale(mix, NT, ready)
        wait(dve, row)
        for t in range(NT):
            token = V.mark(dve.scalar_tensor_tensor(out=mix[:, t, :], in0=mix[:, t, :], scalar=small[:, t:t + 1],
                                                    in1=row_a[:, :], op0=ALU.mult, op1=ALU.mult))
            wait(dve, token)
            token = V.mark(dve.tensor_tensor(x_res[:, t, :], x_res[:, t, :], mix[:, t, :], ALU.add))
        return token

    def copy_out(dst):
        def epilogue(results):
            for t, (b, token) in enumerate(results):
                wait(act, token)
                free[b].mark(act.activation(dst(t), bank[b][:, 0:dst(t).shape[-1]], ACT.Copy))
        return epilogue

    compute = [ENG.PE, ENG.Activation, ENG.DVE]

    def weights_per_trip(units, more):
        per = {hi: units, lo: units, used: units, raw[0]: 8 * units, raw[1]: 8 * units}
        for s, by in more.items():
            per[s] = per.get(s, 0) + by
        return per

    def chunks(count, n, k_blocks, tokens, dst, per_unit=4, rolled=True):
        units = -(-k_blocks // per_unit)
        if rolled:
            with loop(nc, count, compute, weights_per_trip(
                    units, {full: NT - 1, free[0]: 1, free[1]: 1, free[2]: 1, free[3]: 1})) as i:
                chunk_tokens(n, k_blocks, NT, tokens, copy_out(lambda t: dst(t, i * n)), per_unit)
        else:
            for i in range(count):
                chunk_tokens(n, k_blocks, NT, tokens, copy_out(lambda t: dst(t, i * n)), per_unit)

    bank_tokens = lambda: [f.now() for f in free]

    def pipeline(jobs, stages, distance=1):
        for step in range(len(jobs) + distance * (len(stages) - 1)):
            for s, stage in enumerate(stages):
                i = step - s * distance
                if 0 <= i < len(jobs):
                    stage(i, jobs[i])

    stat = lambda kind, i: small[:, 16 + 8 * kind + i % 8:17 + 8 * kind + i % 8]

    def turn_probabilities(i, width, ready):
        wait(pe, ready)
        k = spare_bank()
        for c in range(width // P):
            mm = pe.transpose(bank[k][:, c * P:(c + 1) * P], scratch[0][i % 4][:, c * P:(c + 1) * P], ident)
        token = full.mark(mm)
        wait(act, token)
        return free[k].mark(act.activation(scratch[1][i % 4][:, 0:width], bank[k][:, 0:width], ACT.Copy))

    def softmax(i, k, width, scale, token, mask=None, sink=None, normal=False):
        S = scratch[0][i % 4][:, 0:width]
        ps = bank[k][:, 0:width]
        wait(dve, token)
        if mask is not None:
            start = NEG if sink is None else sink
            v = free[k].mark(dve.tensor_tensor_reduce(S, ps, mask, scale, start, ALU.add, ALU.max, stat(0, i)))
        else:
            v = V.mark(dve.tensor_reduce(stat(0, i), ps, AX.X, ALU.max))
        wait(dve, v)
        v = V.mark(dve.tensor_scalar(stat(1, i), stat(0, i), -1.0 if mask is not None else -scale, None, ALU.mult))
        wait(act, v)
        if mask is not None:
            a = A.mark(act.activation(S, S, ACT.Exp, bias=stat(1, i), accum_out=stat(2, i)))
        else:
            a = free[k].mark(act.activation(S, ps, ACT.Exp, bias=stat(1, i), scale=scale, accum_out=stat(2, i)))
        if sink is not None:
            a = A.mark(act.activation(stat(3, i), sink, ACT.Exp, bias=stat(1, i)))
            wait(dve, a)
            v = V.mark(dve.tensor_tensor(stat(2, i), stat(2, i), stat(3, i), ALU.add))
            wait(dve, v)
        wait(dve, a)
        v = V.mark(dve.reciprocal(stat(4, i), stat(2, i)))
        if normal:
            wait(dve, v)
            return V.mark(dve.tensor_scalar(S, S, stat(4, i), None, ALU.mult))
        return a, v

    def memory_first(qb, ready):
        wait(pe, *ready)
        jobs = [(t, h) for t in range(NT) for h in range(4)]
        got = {}

        def scores(i, job):
            t, h = job
            r = slice(64 * (h % 2), 64 * (h % 2) + 64)
            k = spare_bank()
            mm = pe.matmul(bank[k][:, 0:MEM], qb(h // 2)[r, t * P:(t + 1) * P], mem_kv1[r, 0, h // 2, :],
                           start=True, stop=True)
            got[i] = softmax(i, k, MEM, HD ** -0.5, full.mark(mm))

        def turn(i, job):
            got[i] = got[i][1], turn_probabilities(i, MEM, got[i][0])

        def values(i, job):
            t, h = job
            recip, token = got[i]
            wait(pe, token)
            k = spare_bank()
            for c in range(MEMT):
                mm = pe.matmul(bank[k][:, 0:64], scratch[1][i % 4][:, c * P:(c + 1) * P],
                               mem_kv1[:, 1, c, h * 64:(h + 1) * 64], start=c == 0, stop=c == MEMT - 1)
            wait(dve, full.mark(mm), recip)
            free[k].mark(dve.tensor_scalar(mixed[:, t, 768 + h * 64:832 + h * 64], bank[k][:, 0:64],
                                           stat(4, i), None, ALU.mult))

        pipeline(jobs, [scores, turn, values])

    def memory_second(ready):
        wait(pe, *ready)
        jobs = [(t, h) for t in range(NT) for h in range(4)]
        got = {}

        def scores(i, job):
            t, h = job
            k = spare_bank()
            mm = pe.matmul(bank[k][:, 0:MEM], Y[:, AH + h, t * P:(t + 1) * P], mk2[:, h, :], start=True, stop=True)
            got[i] = softmax(i, k, MEM, P ** -0.5, full.mark(mm), normal=True)

        def turn(i, job):
            got[i] = turn_probabilities(i, MEM, got[i])

        def values(i, job):
            t, h = job
            wait(pe, got[i])
            k = spare_bank()
            for c in range(MEMT):
                mm = pe.matmul(bank[k][:, 0:P], mv2[:, c, h * P:(h + 1) * P], scratch[1][i % 4][:, c * P:(c + 1) * P],
                               start=c == 0, stop=c == MEMT - 1)
            wait(act, full.mark(mm))
            free[k].mark(act.activation(Y[:, AH + h, t * P:(t + 1) * P], bank[k][:, 0:P], ACT.Copy))

        pipeline(jobs, [scores, turn, values])

    def memory_keys_first(layer, ready):
        rms_scale(mem_tok, MEMT, ready)
        for t in range(MEMT):
            token = V.mark(dve.tensor_scalar(mem_tok[:, t, :], mem_tok[:, t, :], small[:, t:t + 1], None, ALU.mult))
        turn_split(mem_tok, MEMT, [token], g=GC_MEM[layer])

        def keys(results):
            for c, (b, token) in enumerate(results):
                wait(act, token)
                free[b].mark(act.activation(mem_kv1[:, 0, c, :], bank[b][:, 0:MEM], ACT.Copy))
        unit_features(MEM, keys)
        chunk_tokens(256, KB, MEMT, from_x, copy_out(lambda t: mem_kv1[:, 1, t, :]), per_unit=8)

    def memory_keys_second(ready):
        wait(dve, *ready)
        for t in range(MEMT):
            layer_norm_stats(mem_tok[:, t, :], t)
            token = V.mark(dve.tensor_scalar(mem_tok[:, t, :], mem_tok[:, t, :], small[:, 100 + 2 * t:101 + 2 * t],
                                             small[:, 101 + 2 * t:102 + 2 * t], ALU.subtract, ALU.mult))
        turn_split(mem_tok, MEMT, [token], g=GC_LNG, b=GC_LNB)
        for u in range(2):
            def keys(results):
                for c, (b, token) in enumerate(results):
                    wait(act, token)
                    free[b].mark(act.activation(mk2[:, 2 * u + c, :], bank[b][:, 0:MEM], ACT.Copy))
            unit_features(MEM, keys)
        chunk_tokens(512, KB, MEMT, from_x, copy_out(lambda t: mv2[:, t, :]))

    def layer_norm_stats(src, t):
        for c in range(2):
            v = V.mark(dve.bn_stats(small[:, 108 + 12 * t + 6 * c:114 + 12 * t + 6 * c], src[:, 512 * c:512 * c + 512]))
        wait(dve, v)
        v = V.mark(dve.bn_aggr(small[:, 100 + 2 * t:102 + 2 * t], small[:, 108 + 12 * t:120 + 12 * t]))
        wait(dve, v)
        inverse_root(small[:, 101 + 2 * t:102 + 2 * t], LN_EPS)

    def mlstm():
        wait(dve, *bank_tokens())
        gates = scr[:, 0:32].rearrange("p (t g) -> p t g", g=8)
        nlf = scr[:, 64:80].rearrange("p (t h) -> p t h", h=4)
        nb = scr[:, 96:112].rearrange("p (t h) -> p t h", h=4)
        cc = scr[:, 128:144].rearrange("p (t h) -> p t h", h=4)
        e_f = scr[:, 160:176].rearrange("p (t h) -> p t h", h=4)
        for t in range(NT):
            v = V.mark(dve.tensor_tensor(gates[:, t, :], proj[:, t, COL_GATE:COL_GATE + 8], small_rows[:, 0:8], ALU.add))
        wait(act, v)
        a = A.mark(act.activation(gates, gates, ACT.Tanh, scale=1.0 / SOFTCAP))
        wait(act, a)
        a = A.mark(act.activation(e_f, gates[:, :, 4:8], ACT.Exp, scale=-SOFTCAP))
        wait(act, a)
        a = A.mark(act.activation(nlf, e_f, ACT.Ln, bias=1.0))
        wait(pe, a)
        k = spare_bank()
        for t in range(NT):
            for s in range(t + 1):
                mm = pe.matmul(bank[k][:, t * 4:t * 4 + 4], const[:, K_TRI:K_TRI + P] if s == t else ones,
                               nlf[:, s, :], start=s == 0, stop=s == t)
        wait(dve, full.mark(mm))
        v = free[k].mark(dve.tensor_copy(scr[:, 96:112], bank[k][:, 0:16]))
        wait(dve, v)
        v = V.mark(dve.scalar_tensor_tensor(out=cc, in0=gates[:, :, 0:4], scalar=SOFTCAP, in1=nb,
                                            op0=ALU.mult, op1=ALU.add))
        wait(dve, v)
        diag = scr[:, 512:2048].rearrange("p (j s) -> p j s", j=3)
        for h in range(LH):
            if h:
                wait(dve, full.now())
            for t in range(NT):
                v = V.mark(dve.tensor_scalar(diag[:, h % 3, t * P:(t + 1) * P], ident, cc[:, t, h:h + 1], None, ALU.mult))
            wait(pe, v)
            k = spare_bank()
            token = full.mark(pe.matmul(bank[k][:, :], ones, diag[:, h % 3, :], start=True, stop=True))
            wait(act, token)
            free[k].mark(act.activation(c_row[:, h, :], bank[k][:, :], ACT.Copy))
        for h in range(2 * LH):
            k = spare_bank()
            for t in range(NT):
                mm = pe.transpose(bank[k][0:LQK, t * P:(t + 1) * P], proj[:, t, h * LQK:(h + 1) * LQK], ident)
            wait(act, full.mark(mm))
            free[k].mark(act.activation(qkT[0:LQK, h, :], bank[k][0:LQK, :], ACT.Copy,
                                        scale=1.0 if h < LH else LQK ** -0.5))
        for c in range(2):
            k = spare_bank()
            for t in range(NT):
                mm = pe.transpose(bank[k][:, t * P:(t + 1) * P],
                                  proj[:, t, COL_MQ + c * P:COL_MQ + (c + 1) * P], ident)
            wait(act, full.mark(mm))
            free[k].mark(act.activation(mqT[:, c, :], bank[k][:, :], ACT.Copy))
        wait(dve, *bank_tokens())
        wait(pe, *bank_tokens())
        jobs = [(t, h) for t in range(NT) for h in range(LH)]
        got = {}

        def scores(i, job):
            t, h = job
            w = (t + 1) * P
            E = scratch[1][i % 4][:, 0:w]
            k = spare_bank()
            token = full.mark(pe.matmul(bank[k][:, 0:w], qkT[0:LQK, h, t * P:(t + 1) * P], qkT[0:LQK, LH + h, 0:w],
                                        start=True, stop=True))
            wait(dve, full.now())
            v = V.mark(dve.tensor_tensor_reduce(E, c_row[:, h, 0:w], const[:, K_CAUS + 512 - w:K_CAUS + 512],
                                                1.0, NEG, ALU.add, ALU.max, stat(0, i)))
            wait(dve, v)
            v = V.mark(dve.tensor_scalar(stat(1, i), stat(0, i), -1.0, None, ALU.mult))
            wait(act, v)
            A.mark(act.activation(E, E, ACT.Exp, bias=stat(1, i)))
            a = A.mark(act.activation(stat(3, i), nb[:, t, h:h + 1], ACT.Exp, bias=stat(1, i)))
            wait(dve, a, token)
            v = free[k].mark(dve.tensor_tensor_reduce(scratch[0][i % 4][:, 0:w], bank[k][:, 0:w], E, 1.0, 0.0,
                                                      ALU.mult, ALU.add, stat(2, i)))
            wait(dve, v)
            d = V.mark(dve.scalar_tensor_tensor(out=stat(2, i), in0=stat(2, i), scalar=-1.0, in1=stat(2, i),
                                                op0=ALU.mult, op1=ALU.max))
            wait(dve, d)
            d = V.mark(dve.tensor_scalar(stat(2, i), stat(2, i), stat(3, i), None, ALU.max))
            wait(dve, d)
            r = V.mark(dve.reciprocal(stat(4, i), stat(2, i)))
            got[i] = v, r

        def turn(i, job):
            got[i] = got[i][1], turn_probabilities(i, (job[0] + 1) * P, got[i][0])

        def values(i, job):
            t, h = job
            recip, token = got[i]
            wait(pe, token)
            k = spare_bank()
            for s in range(t + 1):
                mm = pe.matmul(bank[k][:, 0:LV], scratch[1][i % 4][:, s * P:(s + 1) * P],
                               proj[:, s, COL_V + h * LV:COL_V + (h + 1) * LV], start=s == 0, stop=s == t)
            wait(act, full.mark(mm), recip)
            m = free[k].mark(act.activation(mixed[:, t, h * LV:(h + 1) * LV], bank[k][:, 0:LV], ACT.Copy,
                                            scale=stat(4, i)))

        pipeline(jobs, [scores, turn, values])
        wait(act, *bank_tokens())
        for i, (t, h) in enumerate(jobs):
            a = A.mark(act.activation(scr[:, 512:512 + LV], mixed[:, t, h * LV:(h + 1) * LV], ACT.Square,
                                      scale=LV ** -0.5, accum_out=small[:, 64 + i:65 + i]))
            wait(act, a)
        wait(dve, a, rows.now())
        inverse_root(small[:, 64:80], EPS)
        for t in range(NT):
            a = A.mark(act.activation(proj[:, t, COL_O:COL_O + 768], proj[:, t, COL_O:COL_O + 768], ACT.Sigmoid))
            for h in range(LH):
                s = slice(h * LV, (h + 1) * LV)
                v = V.mark(dve.scalar_tensor_tensor(out=mixed[:, t, s], in0=mixed[:, t, s],
                                                    scalar=small[:, 64 + 4 * t + h:65 + 4 * t + h],
                                                    in1=row_b[:, s], op0=ALU.mult, op1=ALU.mult))
            wait(dve, v, a)
            V.mark(dve.tensor_tensor(mixed[:, t, 0:768], mixed[:, t, 0:768], proj[:, t, COL_O:COL_O + 768], ALU.mult))

    def rotary_tables():
        two_pi = 2 * math.pi
        c1 = float(np.float32(6.28125))
        c2 = float(np.float32(two_pi - c1))
        c3 = float(two_pi - c1 - c2)
        magic = 12582912.0
        ang, turns, r = scr[:, 0:128], scr[:, 128:256], scr[:, 256:384]
        pf = small[:, 8:12]
        wait(dve, t_loaded)
        v = V.mark(dve.tensor_copy(pf, pos[:, :]))
        wait(dve, v)
        for t in range(NT):
            v = V.mark(dve.tensor_scalar(ang[:, t * 32:(t + 1) * 32], const[:, K_INV:K_INV + 32], pf[:, t:t + 1],
                                         None, ALU.mult))
        for kind, shift in ((1, 0.0), (0, 0.25)):
            wait(dve, v)
            v = V.mark(dve.tensor_scalar(turns, ang, 1.0 / two_pi, shift, ALU.mult, ALU.add))
            wait(dve, v)
            v = V.mark(dve.tensor_scalar(turns, turns, magic, None, ALU.add))
            wait(dve, v)
            v = V.mark(dve.tensor_scalar(turns, turns, -magic, None, ALU.add))
            src = ang
            for c in (c1, c2, c3):
                wait(dve, v)
                v = V.mark(dve.scalar_tensor_tensor(out=r, in0=turns, scalar=-c, in1=src, op0=ALU.mult, op1=ALU.add))
                src = r
            wait(dve, v)
            v = V.mark(dve.tensor_scalar(r, r, shift * two_pi, math.pi, ALU.add, ALU.min))
            wait(dve, v)
            v = V.mark(dve.tensor_scalar(r, r, -math.pi, None, ALU.max))
            wait(act, v)
            a = A.mark(act.activation(rotary[:, kind, :, :], r.rearrange("p (t f) -> p t f", t=NT), ACT.Sin))
            wait(dve, a)

    def rotate(buf, heads, ready):
        wait(dve, *ready)
        n = heads * 32
        for t in range(NT):
            v4 = buf[:, t, 0:heads * HD].rearrange("p (h two f) -> p h two f", two=2, f=32)
            x1, x2 = v4[:, :, 0, :], v4[:, :, 1, :]
            cos = rotary[:, 0, t, :].rearrange("p (a f) -> p a f", a=1).to_broadcast([P, heads, 32])
            sin = rotary[:, 1, t, :].rearrange("p (a f) -> p a f", a=1).to_broadcast([P, heads, 32])
            s1 = scr[:, 0:n].rearrange("p (h f) -> p h f", f=32)
            s2 = scr[:, 512:512 + n].rearrange("p (h f) -> p h f", f=32)
            V.mark(dve.tensor_tensor(s1, x1, sin, ALU.mult))
            v = V.mark(dve.tensor_tensor(s2, x2, sin, ALU.mult))
            wait(dve, v)
            V.mark(dve.tensor_tensor(x1, x1, cos, ALU.mult))
            v = V.mark(dve.tensor_tensor(x2, x2, cos, ALU.mult))
            wait(dve, v)
            V.mark(dve.tensor_tensor(x1, x1, s2, ALU.subtract))
            v = V.mark(dve.tensor_tensor(x2, x2, s1, ALU.add))
            wait(dve, v)

    def sliding():
        rotate(q_tok, SH, bank_tokens())
        wait(pe, V.now(), *bank_tokens())
        for src, blocks, dst in ((q_tok, KB, qT), (kv_tok, 2, kT)):
            for c in range(blocks):
                k = spare_bank()
                for t in range(NT):
                    mm = pe.transpose(bank[k][:, t * P:(t + 1) * P], src[:, t, c * P:(c + 1) * P], ident)
                wait(act, full.mark(mm))
                free[k].mark(act.activation(dst[:, c, :], bank[k][:, :], ACT.Copy))
        wait(pe, *bank_tokens())
        wait(dve, *bank_tokens())
        for c in range(2):
            for r in range(2):
                v = V.mark(dve.tensor_copy(kT_swapped[64 * r:64 * r + 64, c, :], kT[64 - 64 * r:128 - 64 * r, c, :]))
        wait(pe, v)
        jobs = [(t, h) for t in range(NT) for h in range(SH)]
        got = {}

        def scores(i, job):
            t, h = job
            g = h // 3
            r = slice(64 * (h % 2), 64 * (h % 2) + 64)
            keys = kT if h % 2 == g % 2 else kT_swapped
            w = P if t == 0 else 2 * P
            k = spare_bank()
            mm = pe.matmul(bank[k][:, 0:w], qT[r, h // 2, t * P:(t + 1) * P],
                           keys[r, g // 2, (t + 1) * P - w:(t + 1) * P], start=True, stop=True)
            got[i] = softmax(i, k, w, HD ** -0.5, full.mark(mm), mask=const[:, K_SWA + 256 - w:K_SWA + 256],
                             sink=small_rows[:, 8 + h:9 + h])

        def turn(i, job):
            got[i] = got[i][1], turn_probabilities(i, P if job[0] == 0 else 2 * P, got[i][0])

        def values(i, job):
            t, h = job
            recip, token = got[i]
            wait(pe, token)
            k = spare_bank()
            n = 1 if t == 0 else 2
            for c in range(n):
                mm = pe.matmul(bank[k][:, 0:HD], scratch[1][i % 4][:, c * P:(c + 1) * P],
                               kv_tok[:, t - n + 1 + c, 256 + (h // 3) * HD:256 + (h // 3 + 1) * HD],
                               start=c == 0, stop=c == n - 1)
            wait(dve, full.mark(mm), recip)
            free[k].mark(dve.tensor_scalar(mixed[:, t, h * HD:(h + 1) * HD], bank[k][:, 0:HD],
                                           stat(4, i), None, ALU.mult))

        pipeline(jobs, [scores, turn, values])

    silu = [row_b[:, 0:512], row_b[:, 512:1024]]

    def feed_forward(layer):
        rms_turn(x_res, GC_FFN[layer], [V.now()])
        row = load_row(row_a, R_FFNPOST[layer])
        per = weights_per_trip(2, {A: 2, V: 2, full: 2, free[0]: 1, free[1]: 1, free[2]: 1, free[3]: 1})
        with loop(nc, FB // 2, compute, per) as i:
            for j in range(2):
                def hidden(results):
                    (bg, tg), (bu, tu) = results
                    wait(act, tg, V.now())
                    a = free[bg].mark(act.activation(silu[j], bank[bg][:, :], ACT.Silu))
                    wait(dve, a, tu, A.now())
                    v = free[bu].mark(dve.tensor_tensor(silu[j], silu[j], bank[bu][:, :], ALU.mult))
                    wait(act, v)
                    a = A.mark(act.activation(HH[:, i * 2 + j, :], silu[j], ACT.Copy))
                    wait(dve, a)
                    V.mark(dve.tensor_tensor(HL[:, i * 2 + j, :], silu[j],
                                             HH[:, i * 2 + j, :].bitcast(F32), ALU.subtract))
                unit_features(SEQ, hidden)
        wait(pe, V.now(), A.now())
        chunks(2, 512, FB, from_h, lambda t, c: mix_x[:, t, bass.ds(c, 512)])
        return post_norm_add(mix_x, bank_tokens(), row)

    def out_first(layer, row):
        turn_split(mixed, NT, [V.now(), A.now(), *bank_tokens()])
        chunks(2, 512, KB, from_x, lambda t, c: mix_b[:, t, bass.ds(c, 512)])
        return post_norm_add(mix_b, bank_tokens(), row)

    split_next()
    split_next()
    for e in (pe, act, dve):
        wait(e, t_loaded, t_rows)
    rotary_tables()
    memory_keys_first(0, [t_loaded, V.now(), A.now()])

    rms_turn(x_res, GC_MIX[0], [V.now(), A.now()])
    chunks(6, A_CHUNK, KB, from_x, lambda t, c: proj[:, t, bass.ds(c, A_CHUNK)])
    load_row(row_b, R_MLSTM, LH * LV)
    row = load_row(row_a, R_MIXPOST[0])
    mlstm()
    wait(act, V.now())
    memory_first(lambda c: mqT[:, c, :], bank_tokens())
    out_first(0, row)
    feed_forward(0)

    rms_turn(x_res, GC_KV, [V.now()])
    chunk_tokens(512, KB, NT, from_x, copy_out(lambda t: kv_tok[:, t, :]))
    rotate(kv_tok, SKV, bank_tokens())

    wait(pool, *quiet())
    t_mem = pooled.mark(pool.dma_start(mem_tok[:, :, :], mem_in[0].rearrange("(t p) d -> p t d", p=P)), 16)
    memory_keys_first(1, [t_mem, V.now()])
    rms_turn(x_res, GC_MIX[1], [V.now()])
    chunks(2, 512, KB, from_x, lambda t, c: q_tok[:, t, bass.ds(c, 512)])
    row = load_row(row_a, R_MIXPOST[1])
    sliding()
    memory_first(lambda c: qT[:, 6 + c, :], bank_tokens())
    out_first(1, row)
    feed_forward(1)

    def feature_units(units, epilogue_of, more, pairs=True):
        per = weights_per_trip(2, {full: 2, free[0]: 1, free[1]: 1, free[2]: 1, free[3]: 1, **more})
        with loop(nc, units // 2, compute, per) as i:
            for j in range(2):
                unit_features(SEQ, epilogue_of(i * 2 + j))

    def to_feature(dst, first, func=ACT.Copy):
        def of(unit):
            def epilogue(results):
                for c, (b, token) in enumerate(results):
                    wait(act, token)
                    free[b].mark(act.activation(dst[:, unit * 2 + (first + c), :], bank[b][:, :], func))
            return epilogue
        return of

    def second_out(last, g_row, b_row):
        wait(dve, V.now(), A.now(), *bank_tokens())
        for c in range(MIXB):
            V.mark(dve.tensor_tensor(Y[:, c, :], Y[:, c, :], gate[:, c, :], ALU.mult))
        wait(act, V.now())
        for c in range(MIXB):
            h, l, k = (XH, XL, c) if c < KB else (YH, YL, c - KB)
            a = A.mark(act.activation(h[:, k, :], Y[:, c, :], ACT.Copy))
            wait(dve, a)
            V.mark(dve.tensor_tensor(l[:, k, :], Y[:, c, :], h[:, k, :].bitcast(F32), ALU.subtract))
        wait(pe, V.now())
        load_row(row_a, g_row)
        row = load_row(row_b, b_row)
        wait(act, V.now())
        chunks(2, 512, MIXB, from_y, lambda t, c: mix_b[:, t, bass.ds(c, 512)] if not isinstance(c, int)
               else mix_b[:, t, c:c + 512], rolled=not last)
        wait(dve, *bank_tokens(), row)
        for t in range(NT):
            v = V.mark(dve.scalar_tensor_tensor(out=x_res[:, t, :], in0=x_res[:, t, :], scalar=ALPHA,
                                                in1=mix_b[:, t, :], op0=ALU.mult, op1=ALU.add))
            wait(dve, v)
            layer_norm_stats(x_res[:, t, :], t)
            v = V.mark(dve.tensor_scalar(x_res[:, t, :], x_res[:, t, :], small[:, 100 + 2 * t:101 + 2 * t],
                                         small[:, 101 + 2 * t:102 + 2 * t], ALU.subtract, ALU.mult))
            wait(dve, v)
            v = V.mark(dve.tensor_tensor(x_res[:, t, :], x_res[:, t, :], row_a[:, :], ALU.mult))
            wait(dve, v)
            v = V.mark(dve.tensor_tensor(x_res[:, t, :], x_res[:, t, :], row_b[:, :], ALU.add))

    def load_mem2():
        wait(pool, *quiet())
        return pooled.mark(pool.dma_start(mem_tok[:, :, :], mem2_in[0].rearrange("(t p) d -> p t d", p=P)), 16)

    def memory_part():
        unit_features(SEQ, to_feature(Y, AH)(0))
        unit_features(SEQ, to_feature(Y, AH + 2)(0))
        scratch[:] = [S_gate, T_gate]
        wait(dve, *quiet())
        wait(act, *quiet())
        memory_second(quiet())
        scratch[:] = [S_buf, T_buf]

    memory_keys_second([load_mem2(), *quiet()])
    wait(act, *quiet())
    turn_split(x_res, NT, quiet())
    memory_part()
    wait(dve, *quiet())
    v = V.mark(dve.memset(conv_in[:, :, 0:PAD], 0.0))

    def glu(unit):
        def epilogue(results):
            (ba, ta), (bg, tg) = results
            wait(act, tg, lo.now())
            a = free[bg].mark(act.activation(silu[1], bank[bg][:, :], ACT.Sigmoid))
            wait(dve, a, ta)
            free[ba].mark(dve.tensor_tensor(conv_in[:, unit, PAD:PAD + SEQ], silu[1], bank[ba][:, :], ALU.mult))
        return epilogue

    feature_units(CB, glu, {})
    feature_units(MIXB // 2, to_feature(gate, 0, ACT.Silu), {})

    wait(dve, *quiet())
    with loop(nc, CB // 2, [ENG.DVE], {V: 2 * TAPS}) as i:
        for k in range(TAPS):
            wait(dve, V.now())
            for j in range(2):
                c = i * 2 + j
                tap = cols[:, bass.ds(c * TAPS + (GC_TAP + k), 1)]
                src = conv_in[:, c, k:k + SEQ]
                if k == 0:
                    V.mark(dve.tensor_scalar(Y[:, c, :], src, tap, cols[:, bass.ds(c + GC_CB, 1)], ALU.mult, ALU.add))
                else:
                    V.mark(dve.scalar_tensor_tensor(out=Y[:, c, :], in0=src, scalar=tap, in1=Y[:, c, :],
                                                    op0=ALU.mult, op1=ALU.add))

    mean, dev = scr[:, 0:SEQ], scr[:, SEQ:2 * SEQ]
    wait(pe, V.now())
    k = spare_bank()
    for c in range(CB):
        mm = pe.matmul(bank[k][:, :], ones, Y[:, c, :], start=c == 0, stop=c == CB - 1)
    wait(dve, full.mark(mm))
    v = free[k].mark(dve.tensor_scalar(mean, bank[k][:, :], 1.0 / CONVW, None, ALU.mult))
    wait(dve, v)
    k = spare_bank()
    for c in range(CB):
        v = V.mark(dve.tensor_tensor(Y[:, c, :], Y[:, c, :], mean, ALU.subtract))
        wait(act, v)
        if c >= 4:
            wait(act, squares[c - 4])
        else:
            squares = {} if c == 0 else squares
        a = A.mark(act.activation(S_buf[c % 4][:, :], Y[:, c, :], ACT.Square))
        wait(pe, a)
        squares[c] = full.mark(pe.matmul(bank[k][:, :], ones, S_buf[c % 4][:, :], start=c == 0, stop=c == CB - 1))
    wait(dve, squares[CB - 1])
    v = free[k].mark(dve.tensor_scalar(dev, bank[k][:, :], 1.0 / CONVW, LN_EPS, ALU.mult, ALU.add))
    wait(dve, v)
    wait(act, v)
    a = A.mark(act.activation(dev, dev, ACT.Sqrt))
    wait(dve, a)
    v = V.mark(dve.reciprocal(dev, dev))
    wait(dve, v, A.now())
    for c in range(CB):
        v = V.mark(dve.tensor_tensor(Y[:, c, :], Y[:, c, :], dev, ALU.mult))
        wait(act, v)
        A.mark(act.activation(Y[:, c, :], Y[:, c, :], ACT.Silu, scale=col(GC_CG, c), bias=col(GC_CBETA, c)))
    second_out(False, R_APG, R_APB)

    memory_keys_second([load_mem2(), *quiet()])
    wait(act, *quiet())
    turn_split(x_res, NT, quiet())
    memory_part()
    wait(act, *quiet())
    feature_units(AH // 2, to_feature(Y, 0), {})

    def into(targets):
        def epilogue(results):
            for (dst, w), (b, token) in zip(targets, results):
                wait(act, token)
                free[b].mark(act.activation(dst, bank[b][0:w, :], ACT.Copy))
        return epilogue

    unit_features(SEQ, into([(dkT[:, :], P), (dvT[:, :], P)]))
    for u in range(2):
        unit_features(SEQ, into([(qiT[:, 2 * u, :], P), (qiT[:, 2 * u + 1, :], P)]))
    unit_features(SEQ, into([(kiT[0:IHD, :], IHD), (wiT[0:IH, :], IH)]), widths=(IHD, IH))
    feature_units(MIXB // 2, to_feature(gate, 0, ACT.Silu), {})

    wait(pe, *quiet())
    wait(dve, *quiet())
    wait(act, *quiet())
    k = spare_bank()
    for t in range(NT):
        mm = pe.transpose(bank[k][:, t * P:(t + 1) * P], dvT[:, t * P:(t + 1) * P], ident)
    wait(act, full.mark(mm))
    free[k].mark(act.activation(d_val[:, :, :], bank[k][:, :].rearrange("p (t d) -> p t d", t=NT), ACT.Copy))
    k = spare_bank()
    for t in range(NT):
        mm = pe.transpose(bank[k][:, t * IH:(t + 1) * IH], wiT[0:IH, t * P:(t + 1) * P], const[0:IH, K_ID:K_ID + IH])
    wait(dve, full.mark(mm))
    free[k].mark(dve.tensor_copy(wi[:, :, :], bank[k][:, 0:NT * IH].rearrange("p (t h) -> p t h", t=NT)))
    v = V.mark(dve.tensor_copy(kiT[IHD:2 * IHD, :], kiT[0:IHD, :]))
    wait(pe, v)
    wait(dve, v, *bank_tokens())

    def select(t):
        w = (t + 1) * P
        s = sel[:, sel_at[t]:sel_at[t] + w]
        diagonal = sel[:, sel_at[t] + t * P:sel_at[t] + w]
        if t == 0:
            V.mark(dve.tensor_copy(s, const[:, K_ADM:K_ADM + P]))
            return
        for h in range(IH):
            r = slice(IHD * (h % 2), IHD * (h % 2) + IHD)
            k = spare_bank()
            token = full.mark(pe.matmul(bank[k][:, 0:w], qiT[r, h // 2, t * P:(t + 1) * P], kiT[r, 0:w],
                                        start=True, stop=True))
            wait(act, token, V.now())
            a = free[k].mark(act.activation(S_buf[h % 2][:, 0:w], bank[k][:, 0:w], ACT.Relu))
            wait(dve, a)
            weight = wi[:, t, h:h + 1]
            if h == 0:
                v = V.mark(dve.tensor_scalar(s, S_buf[0][:, 0:w], weight, None, ALU.mult))
            else:
                v = V.mark(dve.scalar_tensor_tensor(out=s, in0=S_buf[h % 2][:, 0:w], scalar=weight, in1=s,
                                                    op0=ALU.mult, op1=ALU.add))
            wait(dve, v)
        v = V.mark(dve.tensor_tensor(diagonal, diagonal, const[:, K_ADM:K_ADM + P], ALU.add))
        for _ in range(TOPK // 8):
            wait(dve, v)
            v = V.mark(dve.max(top8[:, :], s))
            wait(dve, v)
            v = V.mark(dve.match_replace(s, top8[:, :], s, -3e38))
        wait(dve, v)
        V.mark(dve.tensor_scalar(s, s, -2e38, NEG, ALU.is_gt, ALU.mult))

    for t in range(NT):
        select(t)
    wait(dve, V.now())
    wait(act, V.now())

    jobs = [(t, h) for t in range(NT) for h in range(AH)]
    got = {}

    def scores(i, job):
        t, h = job
        w = (t + 1) * P
        S = scratch[0][i % 4][:, 0:w]
        k = spare_bank()
        mm = pe.matmul(bank[k][:, 0:w], Y[:, h, t * P:(t + 1) * P], dkT[:, 0:w], start=True, stop=True)
        token = full.mark(mm)
        wait(dve, token)
        v = V.mark(dve.scalar_tensor_tensor(out=S, in0=const[:, K_DIST + 512 - w:K_DIST + 512],
                                            scalar=const[:, K_SLOPE + h:K_SLOPE + h + 1],
                                            in1=sel[:, sel_at[t]:sel_at[t] + w], op0=ALU.mult, op1=ALU.add))
        wait(dve, v)
        got[i] = softmax(i, k, w, P ** -0.5, token, mask=S, normal=True)

    def turn(i, job):
        got[i] = turn_probabilities(i, (job[0] + 1) * P, got[i])

    def values(i, job):
        t, h = job
        wait(pe, got[i])
        k = spare_bank()
        for c in range(t + 1):
            mm = pe.matmul(bank[k][:, 0:P], d_val[:, c, :], scratch[1][i % 4][:, c * P:(c + 1) * P],
                           start=c == 0, stop=c == t)
        wait(act, full.mark(mm))
        free[k].mark(act.activation(Y[:, h, t * P:(t + 1) * P], bank[k][:, 0:P], ACT.Copy))

    pipeline(jobs, [scores, turn, values])
    second_out(True, R_BPG, R_BPB)

    wait(act, V.now())
    stored = sig("stored")
    wait(act, stored.mark(act.dma_start(out[0].rearrange("(t p) d -> p t d", p=P), x_res[:, :, :]), 16))


def pack_weights(a):
    units = []

    def add(block):
        flat = block.reshape(P, -1)
        unit = np.zeros((P, UNIT), np.float32)
        unit[:, :flat.shape[1]] = flat
        units.append(unit)

    def rows_of(w):
        return w.reshape(-1, P, w.shape[1]).transpose(1, 0, 2)

    def token_chunks(w, n, per_unit=4):
        r = rows_of(w)
        for c in range(0, w.shape[1], n):
            for k in range(0, r.shape[1], per_unit):
                add(r[:, k:k + per_unit, c:c + n])

    def feature_blocks(w, pairs):
        r = rows_of(w)
        for p in pairs:
            both = np.zeros((P, KB, 256), np.float32)
            at = 0
            for c, n in p:
                both[:, :, at:at + n] = r[:, :, c:c + n]
                at += n
            add(both)

    def run(start, blocks):
        return [((start + 2 * P * i, P), (start + 2 * P * i + P, P)) for i in range(blocks // 2)]

    def first(layer):
        feature_blocks(a["w_mem_kv"][layer], run(0, 2))
        token_chunks(a["w_mem_kv"][layer][:, 256:], 256, per_unit=8)
        if layer == 0:
            token_chunks(a["w_in_a"][0], A_CHUNK)
        else:
            token_chunks(a["w_in_b"][0], 512)
        token_chunks(a["w_out"][layer], 512)
        feature_blocks(a["w_ffn_in"][layer], [((j * P, P), (DFF + j * P, P)) for j in range(FB)])
        token_chunks(a["w_ffn_out"][layer], 512)

    first(0)
    token_chunks(a["w_kv"], 512)
    first(1)
    feature_blocks(a["a_w_mkv_2"][0], run(0, 4))
    token_chunks(a["a_w_mkv_2"][0][:, 512:], 512)
    w = a["a_w_in_2"][0]
    feature_blocks(w, run(2 * CONVW, 4))
    feature_blocks(w, [((j * P, P), (CONVW + j * P, P)) for j in range(CB)])
    feature_blocks(w, run(2 * CONVW + 512, MIXB))
    token_chunks(a["a_w_out_2"][0], 512)
    feature_blocks(a["b_w_mkv_2"][0], run(0, 4))
    token_chunks(a["b_w_mkv_2"][0][:, 512:], 512)
    w = a["b_w_in_2"][0]
    at_kv = AH * P
    at_qi = at_kv + 2 * P
    at_ki = at_qi + IH * IHD
    at_mq = at_ki + IHD + IH
    feature_blocks(w, run(at_mq, 4))
    feature_blocks(w, run(0, AH))
    feature_blocks(w, run(at_kv, 2))
    feature_blocks(w, run(at_qi, 4))
    feature_blocks(w, [((at_ki, IHD), (at_ki + IHD, IH))])
    feature_blocks(w, run(at_mq + 512, MIXB))
    token_chunks(a["b_w_out_2"][0], 512)
    return np.stack(units)


def kernel(**inputs):
    from concourse import bacc
    from concourse.bass_utils import run_bass_kernel_spmd

    a = {k: np.asarray(v) for k, v in inputs.items()}

    def by_feature(v):
        return v.reshape(-1, P).T

    taps = a["a_conv_w_2"][0].reshape(TAPS, CB, P).transpose(2, 1, 0).reshape(P, CB * TAPS)
    cols = np.concatenate(
        [by_feature(v) for v in (a["g_mix_pre"][0], a["g_mix_pre"][1], a["g_ffn_pre"][0], a["g_ffn_pre"][1],
                                 a["g_kv"], a["g_mem"][0], a["g_mem"][1], a["mem_ln_g_2"], a["mem_ln_b_2"])]
        + [taps] + [by_feature(v) for v in (a["a_conv_b_2"][0], a["a_ln_g_2"][0], a["a_ln_b_2"][0])], axis=1)
    rows = np.concatenate(
        [a["g_mix_post"][0], a["g_ffn_post"][0], a["g_mix_post"][1], a["g_ffn_post"][1],
         a["a_post_g_2"][0], a["a_post_b_2"][0], a["b_post_g_2"][0], a["b_post_b_2"][0],
         a["g_mlstm_out"][0], a["b_gates_a"][0], a["sinks_b"][0]])
    arrays = {
        "x": a["x"], "mem": a["mem"], "mem_2": a["mem_2"],
        "positions": np.ascontiguousarray(a["positions"].reshape(NT, P).T),
        "cols": np.ascontiguousarray(cols), "rows": rows, "constants": constants(),
        "weights": pack_weights(a),
    }
    nc = bacc.Bacc("TRN2", target_bir_lowering=False, num_devices=1)
    args = [nc.dram_tensor(n, v.shape, mybir.dt.from_np(v.dtype), kind="ExternalInput").ap()
            for n, v in arrays.items()]
    out = nc.dram_tensor("out", (1, SEQ, D), F32, kind="ExternalOutput").ap()
    build(nc, *args, out)
    r = run_bass_kernel_spmd(nc, [arrays], core_ids=[0])
    return r.results[0]["out"]
```

```python
import math
from contextlib import contextmanager

import numpy as np

import concourse.bass as bass
from concourse import mybir

F32 = mybir.dt.float32
F32R = mybir.dt.float32r
I32 = mybir.dt.int32
ALU = mybir.AluOpType
ACT = mybir.ActivationFunctionType
AX = mybir.AxisListType
ENG = mybir.EngineType

P = 128
D = 1024
KB = D // P
SEQ = 512
NT = SEQ // P
MEMT = 2
MEM = MEMT * P
EPS = 1e-6
LN_EPS = 1e-5
NEG = -1e30
UNIT = 2048

LH, LQK, LV = 4, 96, 192
A_IN = 2 * LH * LQK + 2 * LH * LV + 2 * LH + 256
A_CHUNK = A_IN // 6
COL_V, COL_O = 2 * LH * LQK, 2 * LH * LQK + LH * LV
COL_GATE = COL_O + LH * LV
COL_MQ = COL_GATE + 2 * LH
SOFTCAP = 15.0
SH, SKV, HD = 12, 4, 64
DFF = 2816
FB = DFF // P

CONVW, TAPS = 1536, 31
CB = CONVW // P
AH = 12
IH, IHD = 8, 64
TOPK = SEQ // 4
MIXB = 2048 // P
ALPHA = 4.0 ** 0.25

GC_MIX, GC_FFN, GC_KV, GC_MEM, GC_LNG, GC_LNB = (0, 8), (16, 24), 32, (40, 48), 56, 64
GC_TAP = 72
GC_CB = GC_TAP + CB * TAPS
GC_CG, GC_CBETA = GC_CB + CB, GC_CB + 2 * CB
N_COLS = GC_CB + 3 * CB

R_MIXPOST, R_FFNPOST = (0, 2048), (1024, 3072)
R_APG, R_APB, R_BPG, R_BPB = 4096, 5120, 6144, 7168
R_MLSTM = 8192
R_GATE = R_MLSTM + LH * LV
R_SINK = R_GATE + 2 * LH
N_ROWS = R_SINK + SH

K_ID, K_ONE = 0, 128
K_BLOCK = 256
K_TRI, K_SWA, K_CAUS, K_INV = K_BLOCK, K_BLOCK + 128, K_BLOCK + 384, K_BLOCK + 896
K_END_1 = K_INV + 32
K_ADM, K_DIST, K_SLOPE = K_BLOCK, K_BLOCK + 896, K_BLOCK + 1408
N_CONST = K_SLOPE + AH


def alibi_slopes(n):
    p = 2 ** int(math.floor(math.log2(n)))
    return [2.0 ** (-8.0 * (i + 1) / p) for i in range(p)] + \
           [2.0 ** (-4.0 * (2 * i + 1) / p) for i in range(n - p)]


def constants():
    c = np.zeros((P, N_CONST), np.float32)
    c2 = np.zeros((P, N_CONST), np.float32)
    q = np.arange(P)[:, None]
    k = np.arange(P)[None, :]
    c[:, K_ID:K_ID + P] = np.eye(P)
    c[:, K_ONE:K_ONE + P] = 1.0
    c[:, K_TRI:K_TRI + P] = q <= k
    causal = np.where(k <= q, 0.0, NEG)
    c[:, K_SWA:K_SWA + P] = np.where(k > q, 0.0, NEG)
    c[:, K_SWA + P:K_SWA + 2 * P] = causal
    c[:, K_CAUS + 384:K_CAUS + 512] = causal
    c2[:, K_ADM + 384:K_ADM + 512] = np.where((k >= 64) & (q < 64), NEG, 0.0)
    c2[:, K_ADM + 512:K_ADM + 896] = NEG
    c2[:, K_DIST:K_DIST + 512] = np.abs(q - np.arange(512)[None, :] + 384)
    inv = np.float32(1.0) / np.power(np.float32(10000.0), np.arange(0, 64, 2, dtype=np.float32) / np.float32(64))
    c[:, K_INV:K_INV + 32] = inv[None, :]
    c2[:, K_SLOPE:K_SLOPE + AH] = -np.asarray(alibi_slopes(AH), np.float32)[None, :] * P ** 0.5
    return np.concatenate([c[:, :K_END_1], c2[:, K_BLOCK:]], axis=1)


class Signal:

    every = []

    def __init__(self, nc, name):
        self.sem, self.n, self.trip = nc.alloc_semaphore(name), 0, None
        Signal.every.append(self)

    def value(self, more=0):
        n = self.n + more
        return n if self.trip is None else self.trip + n

    def now(self, more=0):
        return self.sem, self.value(more)

    def mark(self, ins, by=1):
        ins.then_inc(self.sem, by)
        return self.expect(by)

    def expect(self, by):
        self.n += by
        return self.now()


@contextmanager
def loop(nc, trips, engines, per_trip):
    before = {s: s.n for s in Signal.every}
    with nc.Fori(0, trips, engines=engines) as i:
        for s, by in per_trip.items():
            s.trip = i * by
        yield i
    real = {s: s.n - before[s] for s in Signal.every if s.n != before[s]}
    assert real == {s: b for s, b in per_trip.items() if b}, {s.sem.name: b for s, b in real.items()}
    for s, by in per_trip.items():
        s.trip, s.n = None, before[s] + trips * by


def weave(*lists):
    at = [((i + 0.5) / len(steps), n, i) for n, steps in enumerate(lists) for i in range(len(steps))]
    for _, n, i in sorted(at):
        lists[n][i]()


def wait(engine, *tokens):
    for sem, value in tokens:
        if isinstance(value, int) and value <= 0:
            continue
        engine.wait_ge(sem, value)


PER_TWO_UNITS = {"split_hi": 2, "split_lo": 2, "unit_used": 2, "raw_even": 16, "raw_odd": 16,
                 "bank0_read": 1, "bank1_read": 1, "bank2_read": 1, "bank3_read": 1}
PER_CONV = {**PER_TWO_UNITS, "group_full": 2, "dve_done": 32}
PER_GATE3 = {**PER_TWO_UNITS, "group_full": 14, "bank4_read": 3, "bank5_read": 3, "bank6_read": 3,
             "bank7_read": 3, "dve_done": 112, "pool_done": 4}
PER_SELECT = {**PER_TWO_UNITS, "group_full": 10, "bank4_read": 2, "bank5_read": 2, "bank6_read": 2,
              "bank7_read": 2, "dve_done": 42, "pool_done": 1}
PER_GATE4 = {**PER_TWO_UNITS, "group_full": 50, "bank4_read": 12, "bank5_read": 12, "bank6_read": 12,
             "bank7_read": 12, "act_done": 12, "dve_done": 64, "pool_done": 16}


def build(nc, x_in, mem_in, mem2_in, pos_in, cols_in, rows_in, const_in, weights_in, out):
    pe, act, dve, pool, sp = nc.tensor, nc.scalar, nc.vector, nc.gpsimd, nc.sync
    Signal.every = []
    sig = lambda name: Signal(nc, name)
    loaded = sig("loaded")
    parked = sig("parked")
    mem_park = nc.dram_tensor("mem_park", (2, P, 2048), F32, kind="Internal").ap()
    pooled = sig("pool_loads")
    rows = sig("rows")
    raw = [sig("raw_even"), sig("raw_odd")]
    hi, lo = sig("split_hi"), sig("split_lo")
    used = sig("unit_used")
    full = sig("group_full")
    free = [sig(f"bank{b}_read") for b in range(8)]
    A, V, G = sig("act_done"), sig("dve_done"), sig("pool_done")
    n_units = weights_in.shape[0]

    at = [16512]

    def place(name, shape, dtype=F32, offset=None):
        size = 4 * int(np.prod(shape[1:]))
        if offset is None:
            offset, at[0] = at[0], at[0] + (size + 31) // 32 * 32
        return nc.alloc_sbuf_tensor_at(name, shape, dtype, offset=offset)

    const = place("const", [P, N_CONST])
    cols = place("cols", [P, N_COLS])
    row_a = place("row_a", [P, D])
    row_b = place("row_b", [P, D])
    small = place("small", [P, 256])
    rotary = place("rotary", [P, 2, NT, 32])
    minus_half = small[:, 240:256]
    small_rows = place("small_rows", [P, 32])
    x_res = place("x_res", [P, NT, D])
    x_base = at[0]
    XH = place("XH", [P, KB, SEQ], F32R)
    XL = place("XL", [P, KB, SEQ], F32R)
    RAW = [place(f"RAW{j}", [P, UNIT]) for j in range(2)]
    WH = [place(f"WH{j}", [P, UNIT], F32R) for j in range(2)]
    WL = [place(f"WL{j}", [P, UNIT], F32R) for j in range(2)]
    big = at[0]
    BIG = (229344 - big) // 32 * 32
    assert BIG >= 2 * FB * SEQ * 4, BIG
    S_buf = [place(f"S{j}", [P, SEQ], offset=x_base + 2048 * j) for j in range(4)]
    T_buf = [place(f"T{j}", [P, SEQ], offset=x_base + 8192 + 2048 * j) for j in range(4)]
    scratch = [S_buf, T_buf]
    c_row = place("c_row", [P, LH, SEQ], offset=x_base + 16384)
    scr = place("scr", [P, 2048], offset=x_base + 24576)
    mix_x = place("mix_x", [P, NT, D], offset=x_base)
    HH = place("HH", [P, FB, SEQ], F32R, offset=big)
    HL = place("HL", [P, FB, SEQ], F32R, offset=big + FB * SEQ * 4)
    xn = place("xn", [P, NT, D], offset=big + 73728)
    mix_b = place("mix_b", [P, NT, D], offset=big)
    proj = place("proj", [P, NT, A_IN], offset=big)
    mem_kv1 = [place("mem_kv1_0", [P, 2, 2, 256], offset=big + 41088),
               place("mem_kv1_1", [P, 2, 2, 256], offset=big + 2 * FB * SEQ * 4)]
    assert BIG >= 2 * FB * SEQ * 4 + 4096
    mem_kv2 = [place(f"mem_kv2_{l}", [P, 2048], offset=big + 8192 * l) for l in range(2)]
    qkT = place("qkT", [P, 2 * LH, SEQ], offset=big + 45184)
    mixed = place("mixed", [P, NT, D], offset=big + 61568)
    mqT = place("mqT", [P, 2, SEQ], offset=big + 77952)
    q_tok = place("q_tok", [P, NT, D], offset=big)
    kv_tok = place("kv_tok", [P, NT, 2 * SKV * HD], offset=big + 16384)
    kT = place("kT", [P, 2, SEQ], offset=big + 24576)
    kT_swapped = place("kT_swapped", [P, 2, SEQ], offset=big + 28672)
    qT = place("qT", [P, KB, SEQ], offset=big + 45184)
    Y = place("Y", [P, MIXB, SEQ], offset=big)
    gate = place("gate", [P, MIXB, SEQ], offset=big + 32768)
    YH = place("YH", [P, KB, SEQ], F32R, offset=big + 32768)
    YL = place("YL", [P, KB, SEQ], F32R, offset=big + 49152)
    misc = big + 65536
    PAD = TAPS - 1
    CH = CB // 2
    conv_in = [place("conv_in_0", [P, CH, SEQ + PAD], offset=big + 32768),
               place("conv_in_1", [P, CH, SEQ + PAD], offset=misc)]
    kv2 = [place("kv2_0", [P, 2048], offset=misc + 13056), place("kv2_1", [P, 2048], offset=misc + 12288)]
    S_mem = [place(f"Sm{j}", [P, MEM], offset=misc + 21248 + 1024 * j) for j in range(3)]
    T_mem = [place(f"Tm{j}", [P, MEM], offset=misc + 24320 + 1024 * j) for j in range(4)]
    assert 65536 + 28416 <= BIG
    row_at = 16512 + 4 * N_CONST // 32 * 32 + 32 * (4 * N_CONST % 32 > 0) + (4 * N_COLS + 31) // 32 * 32
    q_now = [place(f"q_now{j}", [P, P], offset=row_at + 512 * j) for j in range(4)]
    odd_taps = place("odd_taps", [P, SEQ], offset=row_at + 2048)
    dkT = place("dkT", [P, SEQ], offset=misc)
    d_val = place("d_val", [P, NT, P], offset=misc + 2048)
    sel = place("sel", [P, NT, SEQ], offset=misc + 4096)
    qiT = place("qiT", [P, 4, SEQ], offset=misc + 20480)
    wi = place("wi", [P, NT, IH], offset=misc + 28672)
    top8 = place("top8", [P, 8], offset=misc + 28800)
    ranking = place("ranking", [P, SEQ], offset=big + 32768)
    assert 65536 + 28832 <= BIG
    kiT = place("kiT", [P, SEQ], offset=row_at)
    wiT = place("wiT", [P, SEQ], offset=row_at + 2048)
    qi_now = place("qi_now", [P, 4, P], offset=row_at + 2048)
    dvT = place("dvT", [P, SEQ], offset=row_at + 4096)
    relu = [place(f"relu{j}", [P, SEQ], offset=row_at + 4096 + 2048 * j) for j in range(2)]
    S_dsa = [place(f"Sd{j}", [P, SEQ], offset=misc + 20480 + 2048 * j) for j in range(3)]
    q_dsa = [place(f"q_dsa{j}", [P, P], offset=misc + 26624 + 512 * j) for j in range(4)]
    T_dsa = [place(f"Td{j}", [P, SEQ], offset=row_at + 2048 * j) for j in range(4)]

    bank = [nc.alloc_psum_tensor(f"bank{b}", [P, SEQ], F32) for b in range(8)]
    ring = [0, 0]

    def product_bank():
        b = ring[0] % 4
        ring[0] += 1
        wait(pe, free[b].now())
        return b

    spare = [4, 4]

    def spare_bank():
        b = spare[0] + ring[1] % spare[1]
        ring[1] += 1
        wait(pe, free[b].now())
        return b

    ident = const[:, K_ID:K_ID + P]
    ones = const[:, K_ONE:K_ONE + P]

    def col(base, k):
        return cols[:, base + k:base + k + 1]

    wait(pool, G.mark(pool.memset(minus_half, -0.5)))

    loaded.mark(sp.dma_start(const[:, 0:K_END_1], const_in[:, 0:K_END_1]), 16)
    loaded.mark(sp.dma_start(cols[:, :], cols_in), 16)
    pos = place("pos", [P, NT], I32, offset=x_base)
    t_pos = loaded.mark(sp.dma_start(pos[:, :], pos_in), 16)
    mem_tok = [place(f"mem_tok{m}", [P, MEMT, D], offset=big + 57344 + 8192 * m) for m in range(2)]
    for m, src in enumerate((mem_in, mem2_in)):
        loaded.mark(sp.dma_start(mem_tok[m][:, :, :], src[0].rearrange("(t p) d -> p t d", p=P)), 16)
    t_x = loaded.mark(act.dma_start(x_res[:, :, :], x_in[0].rearrange("(t p) d -> p t d", p=P)), 16)
    t_loaded = loaded.now()
    t_rows = pooled.mark(pool.dma_start(
        small_rows[:, 0:2 * LH + SH],
        rows_in[R_GATE:N_ROWS].rearrange("(a n) -> a n", a=1).partition_broadcast(P)), 16)

    def quiet():
        return [s.now() for s in (A, V, G, full, used, lo, *free)]

    def load_row(dst, start, n=D):
        wait(pool, *quiet())
        src = rows_in[start:start + n].rearrange("(a n) -> a n", a=1).partition_broadcast(P)
        return rows.mark(pool.dma_start(dst[:, 0:n], src), 16)

    for j in range(2):
        sp.dma_start(RAW[j][:, :], weights_in[j]).then_inc(raw[j].sem, 16)
    with nc.Fori(1, n_units // 2, engines=[ENG.SP]) as i:
        for j in range(2):
            sp.wait_ge(lo.sem, i * 2 + (j - 1))
            sp.dma_start(RAW[j][:, :], weights_in[i * 2 + j]).then_inc(raw[j].sem, 16)

    rest_by = [dve]

    def low_parts_on(engine):
        rest_by[0] = engine
        wait(engine, lo.now())

    def split_next():
        j = hi.n % 2
        if hi.trip is None and hi.n >= n_units:
            return
        wait(act, raw[j].expect(16), used.now())
        t = hi.mark(act.activation(WH[j][:, :], RAW[j][:, :], ACT.Copy))
        wait(rest_by[0], t)
        lo.mark(rest_by[0].tensor_tensor(WL[j][:, :], RAW[j][:, :], WH[j][:, :].bitcast(F32), ALU.subtract))

    def three_passes(ps, ah, al, bh, bl, first, last):
        pe.matmul(ps, ah, bh, start=first, stop=False)
        pe.matmul(ps, ah, bl, start=False, stop=False)
        return pe.matmul(ps, al, bh, start=False, stop=last)

    def unit_steps(n, epilogue, widths=(P, P), first=0):
        state, results, steps = {}, [], []

        def begin():
            state["slot"] = used.n % 2
            wait(pe, (lo.sem, used.value(1)))

        def block(c, w, at, kb):
            if kb == 0:
                state["bank"] = product_bank()
            j, b = state["slot"], state["bank"]
            s = slice(kb * 256 + at, kb * 256 + at + w)
            mm = three_passes(bank[b][0:w, 0:n], WH[j][:, s], WL[j][:, s], XH[:, kb, first:first + n],
                              XL[:, kb, first:first + n], kb == 0, kb == KB - 1)
            if kb == KB - 1:
                results.append((b, (used if c == len(widths) - 1 else full).mark(mm)))

        def end():
            epilogue(results)
            split_next()

        at = 0
        steps.append(begin)
        for c, w in enumerate(widths):
            steps += [lambda c=c, w=w, at=at, kb=kb: block(c, w, at, kb) for kb in range(KB)]
            at += w
        steps.append(end)
        return steps

    def unit_features(n, epilogue, widths=(P, P), first=0):
        for step in unit_steps(n, epilogue, widths, first):
            step()

    def chunk_tokens(n, k_blocks, tiles, tokens, epilogue, per_unit=4, first=0, ready=None):
        banks, results = [], []
        for k0 in range(0, k_blocks, per_unit):
            ks = range(k0, min(k0 + per_unit, k_blocks))
            end = ks[-1] == k_blocks - 1
            j = used.n % 2
            wait(pe, (lo.sem, used.value(1)))
            if ready is not None:
                wait(pe, ready[ks[-1]])
            for t in range(tiles):
                if k0 == 0:
                    banks.append(product_bank())
                for kb in ks:
                    th, tl, k = tokens(kb)
                    tt = slice(first + t * P, first + (t + 1) * P)
                    s = slice((kb - k0) * n, (kb - k0 + 1) * n)
                    mm = three_passes(bank[banks[t]][:, 0:n], th[:, k, tt], tl[:, k, tt],
                                      WH[j][:, s], WL[j][:, s], kb == 0, kb == k_blocks - 1)
                if t == tiles - 1:
                    token = used.mark(mm)
                elif end:
                    token = full.mark(mm)
                if end:
                    results.append((banks[t], token))
            if end:
                epilogue(results)
            split_next()

    from_x = lambda kb: (XH, XL, kb)
    from_y = lambda kb: (XH, XL, kb) if kb < KB else (YH, YL, kb - KB)
    from_h = lambda kb: (HH, HL, kb)

    def settle():
        dve.tensor_copy(small[:, 204:205], ident[:, 0:1])

    def inverse_root(v, eps):
        t = V.mark(dve.tensor_scalar(v, v, eps, None, ALU.add))
        wait(pool, t)
        t = G.mark(pool.tensor_tensor(v, v, minus_half[:, 0:v.shape[-1]], ALU.pow))
        wait(dve, t)

    def rms_scale(src, tiles, ready, junk=None):
        wait(act, *ready)
        wait(dve, *ready)
        junk = junk or (scr[:, 0:D], scr[:, D:2 * D])
        for t in range(tiles):
            if t % 2:
                A.mark(act.activation(junk[0], src[:, t, :], ACT.Square, scale=1.0 / 32,
                                      accum_out=small[:, t:t + 1]))
            else:
                V.mark(dve.tensor_tensor_reduce(junk[1], src[:, t, :], src[:, t, :], 1.0 / D, 0.0,
                                                ALU.mult, ALU.add, small[:, t:t + 1]))
            wait(act, A.now())
            wait(dve, V.now())
        wait(dve, A.now())
        inverse_root(small[:, 0:tiles], EPS)

    def turn_split(src, tiles, ready, g=None, b=None, first=0):
        n = tiles * P
        wait(pe, *ready)
        for kb in range(KB):
            k = spare_bank()
            for t in range(tiles):
                mm = pe.transpose(bank[k][:, t * P:(t + 1) * P], src[:, t, kb * P:(kb + 1) * P], ident)
            token = full.mark(mm)
            ps = bank[k][:, 0:n]
            high, low = XH[:, kb, first:first + n], XL[:, kb, first:first + n]
            wait(act, token)
            wait(dve, token)
            if b is not None:
                plain = scr2[kb % 2][:, 0:n]
                wait(act, V.now())
                u = A.mark(act.activation(plain, ps, ACT.Identity, scale=col(g, kb), bias=col(b, kb)))
                wait(act, u)
                h = free[k].mark(act.activation(high, plain, ACT.Copy))
                wait(dve, h)
                V.mark(dve.tensor_tensor(low, plain, high.bitcast(F32), ALU.subtract))
            else:
                scale = 1.0 if g is None else col(g, kb)
                h = A.mark(act.activation(high, ps, ACT.Copy, scale=scale))
                wait(dve, h)
                free[k].mark(dve.scalar_tensor_tensor(out=low, in0=ps, scalar=scale, in1=high.bitcast(F32),
                                                      op0=ALU.mult, op1=ALU.subtract))
        wait(pe, V.now(), *[f.now() for f in free[4:]])

    scr2 = [place(f"scr2_{j}", [P, MEM], offset=big + 53248 + 1024 * j) for j in range(2)]

    def rms_turn(src, g, ready):
        rms_scale(src, NT, ready)
        for t in range(NT):
            token = V.mark(dve.tensor_scalar(xn[:, t, :], src[:, t, :], small[:, t:t + 1], None, ALU.mult))
        turn_split(xn, NT, [token], g=g)

    def post_norm_add(mix, ready, row):
        rms_scale(mix, NT, ready)
        wait(dve, row)
        for t in range(NT):
            token = V.mark(dve.scalar_tensor_tensor(out=mix[:, t, :], in0=mix[:, t, :], scalar=small[:, t:t + 1],
                                                    in1=row_a[:, :], op0=ALU.mult, op1=ALU.mult))
            wait(dve, token)
            token = V.mark(dve.tensor_tensor(x_res[:, t, :], x_res[:, t, :], mix[:, t, :], ALU.add))
        return token

    def copy_out(dst):
        def epilogue(results):
            for t, (b, token) in enumerate(results):
                wait(act, token)
                free[b].mark(act.activation(dst(t), bank[b][:, 0:dst(t).shape[-1]], ACT.Copy))
        return epilogue

    compute = [ENG.PE, ENG.Activation, ENG.DVE]

    def signals(per):
        return {s: per[s.sem.name] for s in Signal.every if s.sem.name in per}

    def weights_per_trip(units, more):
        per = {hi: units, lo: units, used: units, raw[0]: 8 * units, raw[1]: 8 * units}
        for s, by in more.items():
            per[s] = per.get(s, 0) + by
        return per

    def chunks(count, n, k_blocks, tokens, dst, per_unit=4, rolled=True, ready=None):
        units = -(-k_blocks // per_unit)
        if rolled:
            with loop(nc, count, compute, weights_per_trip(
                    units, {full: NT - 1, free[0]: 1, free[1]: 1, free[2]: 1, free[3]: 1})) as i:
                chunk_tokens(n, k_blocks, NT, tokens, copy_out(lambda t: dst(t, i * n)), per_unit, ready=ready)
        else:
            for i in range(count):
                chunk_tokens(n, k_blocks, NT, tokens, copy_out(lambda t: dst(t, i * n)), per_unit, ready=ready)

    bank_tokens = lambda: [f.now() for f in free]

    def pipeline(jobs, stages, distance=1):
        spare[:] = [0, 8]
        for step in range(len(jobs) + distance * (len(stages) - 1)):
            for s, stage in reversed(list(enumerate(stages))):
                i = step - s * distance
                if 0 <= i < len(jobs):
                    stage(i, jobs[i])
        spare[:] = [4, 4]

    stat = lambda kind, i: small[:, 16 + 8 * kind + i % 8:17 + 8 * kind + i % 8]

    def turn_probabilities(i, width, ready):
        wait(pe, ready)
        k = spare_bank()
        for c in range(width // P):
            mm = pe.transpose(bank[k][:, c * P:(c + 1) * P], scratch[0][i % len(scratch[0])][:, c * P:(c + 1) * P], ident)
        token = full.mark(mm)
        wait(act, token)
        return free[k].mark(act.activation(scratch[1][i % len(scratch[1])][:, 0:width], bank[k][:, 0:width], ACT.Copy))

    def softmax(i, k, width, scale, token, mask=None, sink=None):
        S = scratch[0][i % len(scratch[0])][:, 0:width]
        ps = bank[k][:, 0:width]
        wait(dve, token)
        if mask is not None:
            start = NEG if sink is None else sink
            if not isinstance(V.now()[1], int):
                settle()
            v = free[k].mark(dve.tensor_tensor_reduce(S, ps, mask, scale, start, ALU.add, ALU.max, stat(0, i)))
        else:
            v = V.mark(dve.tensor_reduce(stat(0, i), ps, AX.X, ALU.max))
        wait(dve, v)
        v = V.mark(dve.tensor_scalar(stat(1, i), stat(0, i), -1.0 if mask is not None else -scale, None, ALU.mult))
        wait(act, v)
        if mask is not None:
            a = A.mark(act.activation(S, S, ACT.Exp, bias=stat(1, i), accum_out=stat(2, i)))
        else:
            a = free[k].mark(act.activation(S, ps, ACT.Exp, bias=stat(1, i), scale=scale, accum_out=stat(2, i)))
        if sink is not None:
            a = A.mark(act.activation(stat(3, i), sink, ACT.Exp, bias=stat(1, i)))
        return a

    def reciprocal_of_sum(i, ready, sink=False, width=0):
        wait(dve, ready)
        if sink:
            wait(dve, V.mark(dve.tensor_tensor(stat(2, i), stat(2, i), stat(3, i), ALU.add)))
        v = V.mark(dve.reciprocal(stat(4, i), stat(2, i)))
        if width:
            wait(dve, v)
            S = scratch[0][i % len(scratch[0])][:, 0:width]
            v = V.mark(dve.tensor_scalar(S, S, stat(4, i), None, ALU.mult))
        return v

    def memory_first(layer, qb, ready):
        wait(pe, *ready)
        jobs = [(t, h) for t in range(NT) for h in range(4)]
        got = {}

        def scores(i, job):
            t, h = job
            r = slice(64 * (h % 2), 64 * (h % 2) + 64)
            k = spare_bank()
            mm = pe.matmul(bank[k][:, 0:MEM], qb(h // 2)[r, t * P:(t + 1) * P], mem_kv1[layer][r, 0, h // 2, :],
                           start=True, stop=True)
            got[i] = softmax(i, k, MEM, HD ** -0.5, full.mark(mm))

        def divide(i, job):
            got[i] = got[i], reciprocal_of_sum(i, got[i])

        def turn(i, job):
            got[i] = got[i][1], turn_probabilities(i, MEM, got[i][0])

        def values(i, job):
            t, h = job
            recip, token = got[i]
            wait(pe, token)
            k = spare_bank()
            for c in range(MEMT):
                mm = pe.matmul(bank[k][:, 0:64], scratch[1][i % len(scratch[1])][:, c * P:(c + 1) * P],
                               mem_kv1[layer][:, 1, c, h * 64:(h + 1) * 64], start=c == 0, stop=c == MEMT - 1)
            wait(dve, full.mark(mm), recip)
            free[k].mark(dve.tensor_scalar(mixed[:, t, 768 + h * 64:832 + h * 64], bank[k][:, 0:64],
                                           stat(4, i), None, ALU.mult))

        pipeline(jobs, [scores, divide, turn, values])

    def memory_keys():
        junk = (row_a[:, :], row_b[:, :])
        m1, m2 = mem_tok
        rms_scale(m1, MEMT, [t_loaded], junk)
        for t in range(MEMT):
            token = V.mark(dve.tensor_scalar(m1[:, t, :], m1[:, t, :], small[:, t:t + 1], None, ALU.mult))
        turn_split(m1, MEMT, [token], g=GC_MEM[0])
        turn_split(m1, MEMT, [], g=GC_MEM[1], first=MEM)

        def keys(dst):
            def epilogue(results):
                for c, (b, token) in enumerate(results):
                    wait(act, token)
                    free[b].mark(act.activation(dst(c), bank[b][:, 0:MEM], ACT.Copy))
            return epilogue

        for layer in range(2):
            unit_features(MEM, keys(lambda c: mem_kv1[layer][:, 0, c, :]), first=MEM * layer)
            chunk_tokens(256, KB, MEMT, from_x, copy_out(lambda t: mem_kv1[layer][:, 1, t, :]), per_unit=8,
                         first=MEM * layer)
        for t in range(MEMT):
            layer_norm_stats(m2[:, t, :], t)
            token = V.mark(dve.tensor_scalar(m2[:, t, :], m2[:, t, :], small[:, 100 + 2 * t:101 + 2 * t],
                                             small[:, 101 + 2 * t:102 + 2 * t], ALU.subtract, ALU.mult))
        turn_split(m2, MEMT, [token], g=GC_LNG, b=GC_LNB)
        for layer in range(2):
            kv = mem_kv2[layer]
            for u in range(2):
                unit_features(MEM, keys(lambda c: kv[:, (2 * u + c) * MEM:(2 * u + c + 1) * MEM]))
            chunk_tokens(512, KB, MEMT, from_x, copy_out(lambda t: kv[:, 1024 + 512 * t:1536 + 512 * t]))
            wait(act, *bank_tokens())
            parked.mark(act.dma_start(mem_park[layer], kv[:, :]), 16)

    def fetch_memory(layer):
        wait(pool, parked.now(), *quiet())
        return pooled.mark(pool.dma_start(kv2[layer][:, :], mem_park[layer]), 16)

    def layer_norm_stats(src, t):
        for c in range(2):
            v = V.mark(dve.bn_stats(small[:, 108 + 12 * t + 6 * c:114 + 12 * t + 6 * c], src[:, 512 * c:512 * c + 512]))
        wait(dve, v)
        v = V.mark(dve.bn_aggr(small[:, 100 + 2 * t:102 + 2 * t], small[:, 108 + 12 * t:120 + 12 * t]))
        wait(dve, v)
        inverse_root(small[:, 101 + 2 * t:102 + 2 * t], LN_EPS)

    def mlstm():
        wait(dve, *bank_tokens())
        gates = scr[:, 0:32].rearrange("p (t g) -> p t g", g=8)
        nlf = scr[:, 64:80].rearrange("p (t h) -> p t h", h=4)
        nb = scr[:, 96:112].rearrange("p (t h) -> p t h", h=4)
        cc = scr[:, 128:144].rearrange("p (t h) -> p t h", h=4)
        e_f = scr[:, 160:176].rearrange("p (t h) -> p t h", h=4)
        for t in range(NT):
            v = V.mark(dve.tensor_tensor(gates[:, t, :], proj[:, t, COL_GATE:COL_GATE + 8], small_rows[:, 0:8], ALU.add))
        wait(act, v)
        a = A.mark(act.activation(gates, gates, ACT.Tanh, scale=1.0 / SOFTCAP))
        wait(act, a)
        a = A.mark(act.activation(e_f, gates[:, :, 4:8], ACT.Exp, scale=-SOFTCAP))
        wait(act, a)
        a = A.mark(act.activation(nlf, e_f, ACT.Ln, bias=1.0))
        wait(pe, a)
        k = spare_bank()
        for t in range(NT):
            for s in range(t + 1):
                mm = pe.matmul(bank[k][:, t * 4:t * 4 + 4], const[:, K_TRI:K_TRI + P] if s == t else ones,
                               nlf[:, s, :], start=s == 0, stop=s == t)
        wait(dve, full.mark(mm))
        v = free[k].mark(dve.tensor_copy(scr[:, 96:112], bank[k][:, 0:16]))
        wait(dve, v)
        v = V.mark(dve.scalar_tensor_tensor(out=cc, in0=gates[:, :, 0:4], scalar=SOFTCAP, in1=nb,
                                            op0=ALU.mult, op1=ALU.add))
        wait(dve, v)
        diag = scr[:, 512:2048].rearrange("p (j s) -> p j s", j=3)
        for h in range(LH):
            if h:
                wait(dve, full.now())
            for t in range(NT):
                v = V.mark(dve.tensor_scalar(diag[:, h % 3, t * P:(t + 1) * P], ident, cc[:, t, h:h + 1], None, ALU.mult))
            wait(pe, v)
            k = spare_bank()
            token = full.mark(pe.matmul(bank[k][:, :], ones, diag[:, h % 3, :], start=True, stop=True))
            wait(act, token)
            free[k].mark(act.activation(c_row[:, h, :], bank[k][:, :], ACT.Copy))
        for h in range(2 * LH):
            k = spare_bank()
            for t in range(NT):
                mm = pe.transpose(bank[k][0:LQK, t * P:(t + 1) * P], proj[:, t, h * LQK:(h + 1) * LQK], ident)
            wait(act, full.mark(mm))
            free[k].mark(act.activation(qkT[0:LQK, h, :], bank[k][0:LQK, :], ACT.Copy,
                                        scale=1.0 if h < LH else LQK ** -0.5))
        for c in range(2):
            k = spare_bank()
            for t in range(NT):
                mm = pe.transpose(bank[k][:, t * P:(t + 1) * P],
                                  proj[:, t, COL_MQ + c * P:COL_MQ + (c + 1) * P], ident)
            wait(act, full.mark(mm))
            free[k].mark(act.activation(mqT[:, c, :], bank[k][:, :], ACT.Copy))
        wait(dve, *bank_tokens())
        wait(pe, *bank_tokens())
        jobs = [(t, h) for t in range(NT) for h in range(LH)]
        got = {}

        def scores(i, job):
            t, h = job
            w = (t + 1) * P
            E = scratch[1][i % len(scratch[1])][:, 0:w]
            k = spare_bank()
            token = full.mark(pe.matmul(bank[k][:, 0:w], qkT[0:LQK, h, t * P:(t + 1) * P], qkT[0:LQK, LH + h, 0:w],
                                        start=True, stop=True))
            wait(dve, full.now())
            v = V.mark(dve.tensor_tensor_reduce(E, c_row[:, h, 0:w], const[:, K_CAUS + 512 - w:K_CAUS + 512],
                                                1.0, NEG, ALU.add, ALU.max, stat(0, i)))
            wait(dve, v)
            v = V.mark(dve.tensor_scalar(stat(1, i), stat(0, i), -1.0, None, ALU.mult))
            wait(act, v)
            A.mark(act.activation(E, E, ACT.Exp, bias=stat(1, i)))
            got[i] = k, token, A.mark(act.activation(stat(3, i), nb[:, t, h:h + 1], ACT.Exp, bias=stat(1, i)))

        def divide(i, job):
            w = (job[0] + 1) * P
            k, token, a = got[i]
            wait(dve, a, token)
            v = free[k].mark(dve.tensor_tensor_reduce(scratch[0][i % len(scratch[0])][:, 0:w], bank[k][:, 0:w],
                                                      scratch[1][i % len(scratch[1])][:, 0:w], 1.0, 0.0,
                                                      ALU.mult, ALU.add, stat(2, i)))
            wait(dve, v)
            d = V.mark(dve.scalar_tensor_tensor(out=stat(2, i), in0=stat(2, i), scalar=-1.0, in1=stat(2, i),
                                                op0=ALU.mult, op1=ALU.max))
            wait(dve, d)
            d = V.mark(dve.tensor_scalar(stat(2, i), stat(2, i), stat(3, i), None, ALU.max))
            wait(dve, d)
            r = V.mark(dve.reciprocal(stat(4, i), stat(2, i)))
            got[i] = v, r

        def turn(i, job):
            got[i] = got[i][1], turn_probabilities(i, (job[0] + 1) * P, got[i][0])

        def values(i, job):
            t, h = job
            recip, token = got[i]
            wait(pe, token)
            k = spare_bank()
            for s in range(t + 1):
                mm = pe.matmul(bank[k][:, 0:LV], scratch[1][i % len(scratch[1])][:, s * P:(s + 1) * P],
                               proj[:, s, COL_V + h * LV:COL_V + (h + 1) * LV], start=s == 0, stop=s == t)
            wait(act, full.mark(mm), recip)
            m = free[k].mark(act.activation(mixed[:, t, h * LV:(h + 1) * LV], bank[k][:, 0:LV], ACT.Copy,
                                            scale=stat(4, i)))

        pipeline(jobs, [scores, divide, turn, values])
        wait(act, *bank_tokens())
        for i, (t, h) in enumerate(jobs):
            a = A.mark(act.activation(scr[:, 512:512 + LV], mixed[:, t, h * LV:(h + 1) * LV], ACT.Square,
                                      scale=LV ** -0.5, accum_out=small[:, 64 + i:65 + i]))
            wait(act, a)
        wait(dve, a, rows.now())
        inverse_root(small[:, 64:80], EPS)
        for t in range(NT):
            a = A.mark(act.activation(proj[:, t, COL_O:COL_O + 768], proj[:, t, COL_O:COL_O + 768], ACT.Sigmoid))
            for h in range(LH):
                s = slice(h * LV, (h + 1) * LV)
                v = V.mark(dve.scalar_tensor_tensor(out=mixed[:, t, s], in0=mixed[:, t, s],
                                                    scalar=small[:, 64 + 4 * t + h:65 + 4 * t + h],
                                                    in1=row_b[:, s], op0=ALU.mult, op1=ALU.mult))
            wait(dve, v, a)
            V.mark(dve.tensor_tensor(mixed[:, t, 0:768], mixed[:, t, 0:768], proj[:, t, COL_O:COL_O + 768], ALU.mult))

    def rotary_tables():
        two_pi = 2 * math.pi
        c1 = float(np.float32(6.28125))
        c2 = float(np.float32(two_pi - c1))
        c3 = float(two_pi - c1 - c2)
        magic = 12582912.0
        ang, turns, r = scr[:, 0:128], scr[:, 128:256], scr[:, 256:384]
        pf = small[:, 8:12]
        wait(dve, t_loaded)
        v = V.mark(dve.tensor_copy(pf, pos[:, :]))
        wait(dve, v)
        for t in range(NT):
            v = V.mark(dve.tensor_scalar(ang[:, t * 32:(t + 1) * 32], const[:, K_INV:K_INV + 32], pf[:, t:t + 1],
                                         None, ALU.mult))
        for kind, shift in ((1, 0.0), (0, 0.25)):
            wait(dve, v)
            v = V.mark(dve.tensor_scalar(turns, ang, 1.0 / two_pi, shift, ALU.mult, ALU.add))
            wait(dve, v)
            v = V.mark(dve.tensor_scalar(turns, turns, magic, None, ALU.add))
            wait(dve, v)
            v = V.mark(dve.tensor_scalar(turns, turns, -magic, None, ALU.add))
            src = ang
            for c in (c1, c2, c3):
                wait(dve, v)
                v = V.mark(dve.scalar_tensor_tensor(out=r, in0=turns, scalar=-c, in1=src, op0=ALU.mult, op1=ALU.add))
                src = r
            wait(dve, v)
            v = V.mark(dve.tensor_scalar(r, r, shift * two_pi, math.pi, ALU.add, ALU.min))
            wait(dve, v)
            v = V.mark(dve.tensor_scalar(r, r, -math.pi, None, ALU.max))
            wait(act, v)
            a = A.mark(act.activation(rotary[:, kind, :, :], r.rearrange("p (t f) -> p t f", t=NT), ACT.Sin))
            wait(dve, a)

    def rotate(buf, heads, ready):
        wait(dve, *ready)
        n = heads * 32
        for t in range(NT):
            v4 = buf[:, t, 0:heads * HD].rearrange("p (h two f) -> p h two f", two=2, f=32)
            x1, x2 = v4[:, :, 0, :], v4[:, :, 1, :]
            cos = rotary[:, 0, t, :].rearrange("p (a f) -> p a f", a=1).to_broadcast([P, heads, 32])
            sin = rotary[:, 1, t, :].rearrange("p (a f) -> p a f", a=1).to_broadcast([P, heads, 32])
            s1 = scr[:, 0:n].rearrange("p (h f) -> p h f", f=32)
            s2 = scr[:, 512:512 + n].rearrange("p (h f) -> p h f", f=32)
            V.mark(dve.tensor_tensor(s1, x1, sin, ALU.mult))
            v = V.mark(dve.tensor_tensor(s2, x2, sin, ALU.mult))
            wait(dve, v)
            V.mark(dve.tensor_tensor(x1, x1, cos, ALU.mult))
            v = V.mark(dve.tensor_tensor(x2, x2, cos, ALU.mult))
            wait(dve, v)
            V.mark(dve.tensor_tensor(x1, x1, s2, ALU.subtract))
            v = V.mark(dve.tensor_tensor(x2, x2, s1, ALU.add))
            wait(dve, v)

    def sliding():
        rotate(q_tok, SH, bank_tokens())
        wait(pe, V.now(), *bank_tokens())
        for src, blocks, dst in ((q_tok, KB, qT), (kv_tok, 2, kT)):
            for c in range(blocks):
                k = spare_bank()
                for t in range(NT):
                    mm = pe.transpose(bank[k][:, t * P:(t + 1) * P], src[:, t, c * P:(c + 1) * P], ident)
                wait(act, full.mark(mm))
                free[k].mark(act.activation(dst[:, c, :], bank[k][:, :], ACT.Copy))
        wait(pe, *bank_tokens())
        wait(dve, *bank_tokens())
        for c in range(2):
            for r in range(2):
                v = V.mark(dve.tensor_copy(kT_swapped[64 * r:64 * r + 64, c, :], kT[64 - 64 * r:128 - 64 * r, c, :]))
        wait(pe, v)
        jobs = [(t, h) for t in range(NT) for h in range(SH)]
        got = {}

        def scores(i, job):
            t, h = job
            g = h // 3
            r = slice(64 * (h % 2), 64 * (h % 2) + 64)
            keys = kT if h % 2 == g % 2 else kT_swapped
            w = P if t == 0 else 2 * P
            k = spare_bank()
            mm = pe.matmul(bank[k][:, 0:w], qT[r, h // 2, t * P:(t + 1) * P],
                           keys[r, g // 2, (t + 1) * P - w:(t + 1) * P], start=True, stop=True)
            got[i] = softmax(i, k, w, HD ** -0.5, full.mark(mm), mask=const[:, K_SWA + 256 - w:K_SWA + 256],
                             sink=small_rows[:, 8 + h:9 + h])

        def divide(i, job):
            got[i] = got[i], reciprocal_of_sum(i, got[i], sink=True)

        def turn(i, job):
            got[i] = got[i][1], turn_probabilities(i, P if job[0] == 0 else 2 * P, got[i][0])

        def values(i, job):
            t, h = job
            recip, token = got[i]
            wait(pe, token)
            k = spare_bank()
            n = 1 if t == 0 else 2
            for c in range(n):
                mm = pe.matmul(bank[k][:, 0:HD], scratch[1][i % len(scratch[1])][:, c * P:(c + 1) * P],
                               kv_tok[:, t - n + 1 + c, 256 + (h // 3) * HD:256 + (h // 3 + 1) * HD],
                               start=c == 0, stop=c == n - 1)
            wait(dve, full.mark(mm), recip)
            free[k].mark(dve.tensor_scalar(mixed[:, t, h * HD:(h + 1) * HD], bank[k][:, 0:HD],
                                           stat(4, i), None, ALU.mult))

        pipeline(jobs, [scores, divide, turn, values])

    silu = [row_b[:, 0:512], row_b[:, 512:1024]]

    def feed_forward(layer):
        rms_turn(x_res, GC_FFN[layer], [V.now()])
        row = load_row(row_a, R_FFNPOST[layer])
        per = weights_per_trip(2, {A: 2, V: 2, full: 2, free[0]: 1, free[1]: 1, free[2]: 1, free[3]: 1})
        with loop(nc, FB // 2, compute, per) as i:
            for j in range(2):
                def hidden(results):
                    (bg, tg), (bu, tu) = results
                    wait(act, tg, V.now())
                    a = free[bg].mark(act.activation(silu[j], bank[bg][:, :], ACT.Silu))
                    wait(dve, a, tu, A.now())
                    v = free[bu].mark(dve.tensor_tensor(silu[j], silu[j], bank[bu][:, :], ALU.mult))
                    wait(act, v)
                    a = A.mark(act.activation(HH[:, i * 2 + j, :], silu[j], ACT.Copy))
                    wait(dve, a)
                    V.mark(dve.tensor_tensor(HL[:, i * 2 + j, :], silu[j],
                                             HH[:, i * 2 + j, :].bitcast(F32), ALU.subtract))
                unit_features(SEQ, hidden)
        wait(pe, V.now(), A.now())
        chunks(2, 512, FB, from_h, lambda t, c: mix_x[:, t, bass.ds(c, 512)])
        return post_norm_add(mix_x, bank_tokens(), row)

    def out_first(layer, row):
        turn_split(mixed, NT, [V.now(), A.now(), *bank_tokens()])
        chunks(2, 512, KB, from_x, lambda t, c: mix_b[:, t, bass.ds(c, 512)])
        return post_norm_add(mix_b, bank_tokens(), row)

    split_next()
    split_next()
    for e in (pe, act, dve):
        wait(e, t_loaded, t_rows)
    rotary_tables()
    memory_keys()

    rms_turn(x_res, GC_MIX[0], [V.now(), A.now()])
    wait(act, parked.now())
    chunks(6, A_CHUNK, KB, from_x, lambda t, c: proj[:, t, bass.ds(c, A_CHUNK)])
    load_row(row_b, R_MLSTM, LH * LV)
    row = load_row(row_a, R_MIXPOST[0])
    mlstm()
    wait(act, V.now())
    memory_first(0, lambda c: mqT[:, c, :], bank_tokens())
    out_first(0, row)
    feed_forward(0)

    rms_turn(x_res, GC_KV, [V.now()])
    chunk_tokens(512, KB, NT, from_x, copy_out(lambda t: kv_tok[:, t, :]))
    rotate(kv_tok, SKV, bank_tokens())

    rms_turn(x_res, GC_MIX[1], [V.now()])
    chunks(2, 512, KB, from_x, lambda t, c: q_tok[:, t, bass.ds(c, 512)])
    row = load_row(row_a, R_MIXPOST[1])
    sliding()
    memory_first(1, lambda c: qT[:, 6 + c, :], bank_tokens())
    out_first(1, row)
    feed_forward(1)

    def feature_units(units, epilogue_of, more, pairs=True):
        per = weights_per_trip(2, {full: 2, free[0]: 1, free[1]: 1, free[2]: 1, free[3]: 1, **more})
        with loop(nc, units // 2, compute, per) as i:
            for j in range(2):
                unit_features(SEQ, epilogue_of(i * 2 + j))

    def to_feature(dst, first, func=ACT.Copy):
        def of(unit):
            def epilogue(results):
                for c, (b, token) in enumerate(results):
                    wait(act, token)
                    free[b].mark(act.activation(dst[:, unit * 2 + (first + c), :], bank[b][:, :], func))
            return epilogue
        return of

    def second_out(last, g_row, b_row):
        wait(dve, *quiet())
        ready = {}
        for c in range(MIXB):
            v = V.mark(dve.tensor_tensor(Y[:, c, :], Y[:, c, :], gate[:, c, :], ALU.mult))
            ready[c] = v
        for c in range(MIXB):
            h, l, k = (XH, XL, c) if c < KB else (YH, YL, c - KB)
            wait(act, ready[c] if c < KB else ready[MIXB - 1])
            a = A.mark(act.activation(h[:, k, :], Y[:, c, :], ACT.Copy))
            wait(dve, a)
            ready[c] = V.mark(dve.tensor_tensor(l[:, k, :], Y[:, c, :], h[:, k, :].bitcast(F32), ALU.subtract))
        load_row(row_a, g_row)
        row = load_row(row_b, b_row)
        chunks(2, 512, MIXB, from_y, lambda t, c: mix_b[:, t, bass.ds(c, 512)] if not isinstance(c, int)
               else mix_b[:, t, c:c + 512], rolled=not last, ready=ready)
        wait(dve, *bank_tokens(), row)
        for t in range(NT):
            v = V.mark(dve.scalar_tensor_tensor(out=x_res[:, t, :], in0=x_res[:, t, :], scalar=ALPHA,
                                                in1=mix_b[:, t, :], op0=ALU.mult, op1=ALU.add))
            wait(dve, v)
            layer_norm_stats(x_res[:, t, :], t)
            v = V.mark(dve.tensor_scalar(x_res[:, t, :], x_res[:, t, :], small[:, 100 + 2 * t:101 + 2 * t],
                                         small[:, 101 + 2 * t:102 + 2 * t], ALU.subtract, ALU.mult))
            wait(dve, v)
            v = V.mark(dve.tensor_tensor(x_res[:, t, :], x_res[:, t, :], row_a[:, :], ALU.mult))
            wait(dve, v)
            v = V.mark(dve.tensor_tensor(x_res[:, t, :], x_res[:, t, :], row_b[:, :], ALU.add))

    def staged_jobs(jobs, q_ring, S_ring, T_ring):
        got, steps = {}, []

        def stage_query(i, job):
            wait(pool, full.now())
            got[i] = G.mark(pool.tensor_copy(q_ring[i % 4][:, :], job["query"]))

        def scores(i, job):
            wait(pe, got[i])
            w = job["width"]
            k = spare_bank()
            token = full.mark(pe.matmul(bank[k][:, 0:w], q_ring[i % 4][:, :], job["keys"], start=True, stop=True))
            mask = None
            if job["bias"] is not None:
                S = S_ring[i % len(S_ring)][:, 0:w]
                wait(dve, token)
                wait(dve, job["bias"](S))
                mask = S
            scratch[:] = [S_ring, T_ring]
            got[i] = softmax(i, k, w, P ** -0.5, token, mask=mask)

        def divide(i, job):
            scratch[:] = [S_ring, T_ring]
            got[i] = reciprocal_of_sum(i, got[i], width=job["width"])

        def turn(i, job):
            scratch[:] = [S_ring, T_ring]
            got[i] = turn_probabilities(i, job["width"], got[i])

        def values(i, job):
            wait(pe, got[i])
            k = spare_bank()
            n = job["width"] // P
            for c in range(n):
                mm = pe.matmul(bank[k][:, 0:P], job["value"](c), T_ring[i % len(T_ring)][:, c * P:(c + 1) * P],
                               start=c == 0, stop=c == n - 1)
            wait(act, full.mark(mm))
            free[k].mark(act.activation(job["out"], bank[k][:, 0:P], ACT.Copy))

        stages = [stage_query, scores, divide, turn, values]
        for step in range(len(jobs) + len(stages) - 1):
            for s, stage in reversed(list(enumerate(stages))):
                i = step - s
                if 0 <= i < len(jobs):
                    steps.append(lambda stage=stage, i=i: stage(i, jobs[i]))
        return steps

    def memory_jobs(t, layer):
        kv = kv2[layer]
        return [{"query": Y[:, AH + h, bass.ds(t * P, P)], "keys": kv[:, h * MEM:(h + 1) * MEM], "width": MEM,
                 "bias": None, "value": lambda c, h=h: kv[:, 1024 + 512 * c + h * P:1024 + 512 * c + (h + 1) * P],
                 "out": Y[:, AH + h, bass.ds(t * P, P)]} for h in range(4)]

    def gate_units(i):
        return unit_steps(SEQ, to_feature(gate, 0, ACT.Silu)(i * 2)) + \
            unit_steps(SEQ, to_feature(gate, 0, ACT.Silu)(i * 2 + 1))

    everyone = [ENG.PE, ENG.Activation, ENG.DVE, ENG.Pool]

    t_kv = fetch_memory(0)
    t_const = pooled.mark(pool.dma_start(const[:, K_BLOCK:N_CONST], const_in[:, K_END_1:]), 16)
    turn_split(x_res, NT, quiet())
    for e in (pe, act, dve):
        wait(e, t_const)
    unit_features(SEQ, to_feature(Y, AH)(0))
    unit_features(SEQ, to_feature(Y, AH + 2)(0))
    wait(dve, *quiet())
    for half in conv_in:
        v = V.mark(dve.memset(half[:, :, 0:PAD], 0.0))

    def convolve(out, src, c, n):
        def pair(k):
            for tap in range(k, min(k + 2, TAPS)):
                w = cols[:, bass.ds(c * TAPS + (GC_TAP + tap), 1)]
                acc = odd_taps[:, 0:n] if tap % 2 else out
                if tap == 0:
                    V.mark(dve.tensor_scalar(acc, src(tap), w, cols[:, bass.ds(c + GC_CB, 1)], ALU.mult, ALU.add))
                elif tap == 1:
                    V.mark(dve.tensor_scalar(acc, src(tap), w, None, ALU.mult))
                else:
                    wait(dve, V.now(-1))
                    V.mark(dve.scalar_tensor_tensor(out=acc, in0=src(tap), scalar=w, in1=acc,
                                                    op0=ALU.mult, op1=ALU.add))

        def both():
            wait(dve, V.now())
            V.mark(dve.tensor_tensor(out, out, odd_taps[:, 0:n], ALU.add))
            wait(dve, V.now())

        return [lambda k=k: pair(k) for k in range(0, TAPS, 2)] + [both]

    low_parts_on(pool)
    for half in range(2):
        with loop(nc, CH // 2, everyone, signals(PER_CONV)) as i:
            made = {}

            def glu(j):
                def epilogue(results):
                    (ba, ta), (bg, tg) = results
                    wait(act, tg)
                    a = free[bg].mark(act.activation(silu[j], bank[bg][:, :], ACT.Sigmoid))
                    wait(dve, a, ta)
                    made[j] = free[ba].mark(dve.tensor_tensor(conv_in[half][:, i * 2 + j, PAD:PAD + SEQ], silu[j],
                                                              bank[ba][:, :], ALU.mult))
                return epilogue
            c = i + 3 * half
            first_unit, second_unit = unit_steps(SEQ, glu(0)), unit_steps(SEQ, glu(1))
            taps = convolve(Y[:, c, :], lambda k: conv_in[0][:, c, k:k + SEQ], c, SEQ)
            for step in first_unit:
                step()
            wait(dve, made[0])
            weave(second_unit, taps)

    wait(pe, *quiet())
    wait(act, V.now())
    wait(pool, *quiet())
    with loop(nc, NT, everyone, signals(PER_GATE3)) as i:
        whole = convolve(Y[:, i + CH, :], lambda k: conv_in[1][:, i, k:k + SEQ], i + CH, SEQ)
        quarters = []
        for j in range(2):
            quarters += convolve(Y[:, CB - 2 + j, bass.ds(i * P, P)],
                                 lambda k, j=j: conv_in[1][:, CH - 2 + j, bass.ds(i * P + k, P)], CB - 2 + j, P)
        weave(gate_units(i), staged_jobs(memory_jobs(i, 0), q_now, S_mem, T_mem), whole + quarters)
    low_parts_on(dve)
    scratch[:] = [S_buf, T_buf]

    mean, dev = scr[:, 0:SEQ], scr[:, SEQ:2 * SEQ]
    wait(pe, V.now())
    wait(dve, *quiet())
    wait(act, *quiet())
    k = spare_bank()
    for c in range(CB):
        mm = pe.matmul(bank[k][:, :], ones, Y[:, c, :], start=c == 0, stop=c == CB - 1)
    wait(dve, full.mark(mm))
    v = free[k].mark(dve.tensor_scalar(mean, bank[k][:, :], 1.0 / CONVW, None, ALU.mult))
    wait(dve, v)
    k = spare_bank()
    squares = {}
    for c in range(CB):
        v = V.mark(dve.tensor_tensor(Y[:, c, :], Y[:, c, :], mean, ALU.subtract))
        wait(act, v)
        if c >= 4:
            wait(act, squares[c - 4])
        a = A.mark(act.activation(S_buf[c % 4][:, :], Y[:, c, :], ACT.Square))
        wait(pe, a)
        squares[c] = full.mark(pe.matmul(bank[k][:, :], ones, S_buf[c % 4][:, :], start=c == 0, stop=c == CB - 1))
    wait(dve, squares[CB - 1])
    v = free[k].mark(dve.tensor_scalar(dev, bank[k][:, :], 1.0 / CONVW, LN_EPS, ALU.mult, ALU.add))
    wait(act, v)
    a = A.mark(act.activation(dev, dev, ACT.Sqrt))
    wait(dve, a)
    v = V.mark(dve.reciprocal(dev, dev))
    wait(dve, v, A.now())
    for c in range(CB):
        v = V.mark(dve.tensor_tensor(Y[:, c, :], Y[:, c, :], dev, ALU.mult))
        wait(act, v)
        A.mark(act.activation(Y[:, c, :], Y[:, c, :], ACT.Silu, scale=col(GC_CG, c), bias=col(GC_CBETA, c)))
    second_out(False, R_APG, R_APB)

    t_kv = fetch_memory(1)
    turn_split(x_res, NT, quiet())
    for e in (pe, act, dve):
        wait(e, t_kv)

    def into(targets):
        def epilogue(results):
            for (dst, w), (b, token) in zip(targets, results):
                wait(act, token)
                free[b].mark(act.activation(dst, bank[b][0:w, :], ACT.Copy))
        return epilogue

    unit_features(SEQ, into([(kiT[0:IHD, :], IHD), (wiT[0:IH, :], IH)]), widths=(IHD, IH))
    for u in range(2):
        unit_features(SEQ, into([(qiT[:, 2 * u, :], P), (qiT[:, 2 * u + 1, :], P)]))
    unit_features(SEQ, into([(dkT[:, :], P), (dvT[:, :], P)]))
    unit_features(SEQ, to_feature(Y, AH)(0))
    unit_features(SEQ, to_feature(Y, AH + 2)(0))
    low_parts_on(pool)
    wait(pe, *bank_tokens())
    wait(dve, *bank_tokens())
    k = spare_bank()
    for t in range(NT):
        mm = pe.transpose(bank[k][:, t * P:(t + 1) * P], dvT[:, t * P:(t + 1) * P], ident)
    wait(act, full.mark(mm))
    free[k].mark(act.activation(d_val[:, :, :], bank[k][:, :].rearrange("p (t d) -> p t d", t=NT), ACT.Copy))
    k = spare_bank()
    for t in range(NT):
        mm = pe.transpose(bank[k][:, t * IH:(t + 1) * IH], wiT[0:IH, t * P:(t + 1) * P], const[0:IH, K_ID:K_ID + IH])
    wait(dve, full.mark(mm))
    free[k].mark(dve.tensor_copy(wi[:, :, :], bank[k][:, 0:NT * IH].rearrange("p (t h) -> p t h", t=NT)))
    V.mark(dve.tensor_copy(kiT[IHD:2 * IHD, :], kiT[0:IHD, :]))
    V.mark(dve.tensor_copy(sel[:, 0, :], const[:, K_ADM + 384:K_ADM + 896]))
    for e in (pe, dve, act, pool):
        wait(e, *bank_tokens(), V.now())

    def select(t):
        s = ranking[:, :]

        def stage_queries():
            wait(pool, V.now(), full.now())
            G.mark(pool.tensor_copy(qi_now[:, :, :], qiT[:, :, bass.ds(t * P, P)]))
            wait(pe, G.now())

        def index_head(h):
            r = slice(IHD * (h % 2), IHD * (h % 2) + IHD)
            k = spare_bank()
            token = full.mark(pe.matmul(bank[k][:, :], qi_now[r, h // 2, :], kiT[r, :], start=True, stop=True))
            wait(act, token, V.now(-1))
            a = free[k].mark(act.activation(relu[h % 2][:, :], bank[k][:, :], ACT.Relu))
            wait(dve, a, V.now())
            weight = wi[:, bass.ds(t, 1), h:h + 1].rearrange("p a h -> p (a h)")
            if h == 0:
                V.mark(dve.tensor_scalar(s, relu[0][:, :], weight, None, ALU.mult))
            else:
                V.mark(dve.scalar_tensor_tensor(out=s, in0=relu[h % 2][:, :], scalar=weight, in1=s,
                                                op0=ALU.mult, op1=ALU.add))

        def admissible():
            wait(dve, V.now())
            V.mark(dve.tensor_tensor(s, s, const[:, bass.ds(t * -P + (K_ADM + 384), SEQ)], ALU.add))

        def take8():
            wait(dve, V.now())
            settle()
            v = V.mark(dve.max(top8[:, :], s))
            wait(dve, v)
            settle()
            V.mark(dve.match_replace(s, top8[:, :], s, -3e38))

        def to_mask():
            wait(dve, V.now())
            V.mark(dve.tensor_scalar(sel[:, bass.ds(t, 1), :].rearrange("p a k -> p (a k)"), s, -2e38, NEG,
                                     ALU.is_gt, ALU.mult))

        return [stage_queries] + [lambda h=h: index_head(h) for h in range(IH)] + [admissible] + \
            [take8] * (TOPK // 8) + [to_mask]

    with loop(nc, AH // 4, everyone, signals(PER_SELECT)) as i:
        both = unit_steps(SEQ, to_feature(Y, 0)(i * 2)) + unit_steps(SEQ, to_feature(Y, 0)(i * 2 + 1))
        weave(both, select(i + 1))

    for e in (pe, act, dve, pool):
        wait(e, *quiet())
    with loop(nc, AH // 3, everyone, signals(PER_GATE4)) as i:
        jobs = []
        memory = memory_jobs(i, 1)
        for g in range(3):
            h = i * 3 + g
            for t in range(NT):
                w = (t + 1) * P

                def bias(S, h=h, t=t, w=w):
                    return V.mark(dve.scalar_tensor_tensor(
                        out=S, in0=const[:, K_DIST + 512 - w:K_DIST + 512],
                        scalar=const[:, bass.ds(h + K_SLOPE, 1)], in1=sel[:, t, 0:w],
                        op0=ALU.mult, op1=ALU.add))
                jobs.append({"query": Y[:, h, t * P:(t + 1) * P], "keys": dkT[:, 0:w], "width": w, "bias": bias,
                             "value": lambda c: d_val[:, c, :], "out": Y[:, h, t * P:(t + 1) * P]})
            jobs.append(memory[g])
        jobs.append(memory[3])
        weave(gate_units(i), staged_jobs(jobs, q_dsa, S_dsa, T_dsa))
    low_parts_on(dve)
    scratch[:] = [S_buf, T_buf]
    second_out(True, R_BPG, R_BPB)

    wait(act, V.now())
    stored = sig("stored")
    wait(act, stored.mark(act.dma_start(out[0].rearrange("(t p) d -> p t d", p=P), x_res[:, :, :]), 16))


def pack_weights(a):
    units = []

    def add(block):
        flat = block.reshape(P, -1)
        unit = np.zeros((P, UNIT), np.float32)
        unit[:, :flat.shape[1]] = flat
        units.append(unit)

    def rows_of(w):
        return w.reshape(-1, P, w.shape[1]).transpose(1, 0, 2)

    def token_chunks(w, n, per_unit=4):
        r = rows_of(w)
        for c in range(0, w.shape[1], n):
            for k in range(0, r.shape[1], per_unit):
                add(r[:, k:k + per_unit, c:c + n])

    def feature_blocks(w, pairs):
        r = rows_of(w)
        for p in pairs:
            both = np.zeros((P, KB, 256), np.float32)
            at = 0
            for c, n in p:
                both[:, :, at:at + n] = r[:, :, c:c + n]
                at += n
            add(both)

    def run(start, blocks):
        return [((start + 2 * P * i, P), (start + 2 * P * i + P, P)) for i in range(blocks // 2)]

    for layer in range(2):
        feature_blocks(a["w_mem_kv"][layer], run(0, 2))
        token_chunks(a["w_mem_kv"][layer][:, 256:], 256, per_unit=8)
    for w in (a["a_w_mkv_2"][0], a["b_w_mkv_2"][0]):
        feature_blocks(w, run(0, 4))
        token_chunks(w[:, 512:], 512)

    def first(layer):
        if layer == 0:
            token_chunks(a["w_in_a"][0], A_CHUNK)
        else:
            token_chunks(a["w_in_b"][0], 512)
        token_chunks(a["w_out"][layer], 512)
        feature_blocks(a["w_ffn_in"][layer], [((j * P, P), (DFF + j * P, P)) for j in range(FB)])
        token_chunks(a["w_ffn_out"][layer], 512)

    first(0)
    token_chunks(a["w_kv"], 512)
    first(1)
    w = a["a_w_in_2"][0]
    feature_blocks(w, run(2 * CONVW, 4))
    feature_blocks(w, [((j * P, P), (CONVW + j * P, P)) for j in range(CB)])
    feature_blocks(w, run(2 * CONVW + 512, MIXB))
    token_chunks(a["a_w_out_2"][0], 512)
    w = a["b_w_in_2"][0]
    at_kv = AH * P
    at_qi = at_kv + 2 * P
    at_ki = at_qi + IH * IHD
    at_mq = at_ki + IHD + IH
    feature_blocks(w, [((at_ki, IHD), (at_ki + IHD, IH))])
    feature_blocks(w, run(at_qi, 4))
    feature_blocks(w, run(at_kv, 2))
    feature_blocks(w, run(at_mq, 4))
    feature_blocks(w, run(0, AH))
    feature_blocks(w, run(at_mq + 512, MIXB))
    token_chunks(a["b_w_out_2"][0], 512)
    return np.stack(units)


def kernel(**inputs):
    from concourse import bacc
    from concourse.bass_utils import run_bass_kernel_spmd

    a = {k: np.asarray(v) for k, v in inputs.items()}

    def by_feature(v):
        return v.reshape(-1, P).T

    taps = a["a_conv_w_2"][0].reshape(TAPS, CB, P).transpose(2, 1, 0).reshape(P, CB * TAPS)
    cols = np.concatenate(
        [by_feature(v) for v in (a["g_mix_pre"][0], a["g_mix_pre"][1], a["g_ffn_pre"][0], a["g_ffn_pre"][1],
                                 a["g_kv"], a["g_mem"][0], a["g_mem"][1], a["mem_ln_g_2"], a["mem_ln_b_2"])]
        + [taps] + [by_feature(v) for v in (a["a_conv_b_2"][0], a["a_ln_g_2"][0], a["a_ln_b_2"][0])], axis=1)
    rows = np.concatenate(
        [a["g_mix_post"][0], a["g_ffn_post"][0], a["g_mix_post"][1], a["g_ffn_post"][1],
         a["a_post_g_2"][0], a["a_post_b_2"][0], a["b_post_g_2"][0], a["b_post_b_2"][0],
         a["g_mlstm_out"][0], a["b_gates_a"][0], a["sinks_b"][0]])
    arrays = {
        "x": a["x"], "mem": a["mem"], "mem_2": a["mem_2"],
        "positions": np.ascontiguousarray(a["positions"].reshape(NT, P).T),
        "cols": np.ascontiguousarray(cols), "rows": rows, "constants": constants(),
        "weights": pack_weights(a),
    }
    nc = bacc.Bacc("TRN2", target_bir_lowering=False, num_devices=1)
    args = [nc.dram_tensor(n, v.shape, mybir.dt.from_np(v.dtype), kind="ExternalInput").ap()
            for n, v in arrays.items()]
    out = nc.dram_tensor("out", (1, SEQ, D), F32, kind="ExternalOutput").ap()
    build(nc, *args, out)
    r = run_bass_kernel_spmd(nc, [arrays], core_ids=[0])
    return r.results[0]["out"]
```

```python
import math
from contextlib import contextmanager

import numpy as np

import concourse.bass as bass
from concourse import mybir

F32 = mybir.dt.float32
F32R = mybir.dt.float32r
I32 = mybir.dt.int32
ALU = mybir.AluOpType
ACT = mybir.ActivationFunctionType
AX = mybir.AxisListType
ENG = mybir.EngineType

P = 128
D = 1024
KB = D // P
SEQ = 512
NT = SEQ // P
MEMT = 2
MEM = MEMT * P
EPS = 1e-6
LN_EPS = 1e-5
NEG = -1e30
UNIT = 2048

LH, LQK, LV = 4, 96, 192
A_IN = 2 * LH * LQK + 2 * LH * LV + 2 * LH + 256
A_CHUNK = A_IN // 6
COL_V, COL_O = 2 * LH * LQK, 2 * LH * LQK + LH * LV
COL_GATE = COL_O + LH * LV
COL_MQ = COL_GATE + 2 * LH
SOFTCAP = 15.0
SH, SKV, HD = 12, 4, 64
DFF = 2816
FB = DFF // P

CONVW, TAPS = 1536, 31
CB = CONVW // P
AH = 12
IH, IHD = 8, 64
TOPK = SEQ // 4
MIXB = 2048 // P
ALPHA = 4.0 ** 0.25

GC_MEM, GC_LNG, GC_LNB = (0, 8), 16, 24
GC_TAP = 32
GC_CB = GC_TAP + CB * TAPS
GC_CG, GC_CBETA = GC_CB + CB, GC_CB + 2 * CB
N_COLS = GC_CB + 3 * CB

R_MIXPOST, R_FFNPOST = (0, 2048), (1024, 3072)
R_APG, R_APB, R_BPG, R_BPB = 4096, 5120, 6144, 7168
R_MIXPRE, R_FFNPRE, R_KV = (8192, 9216), (10240, 11264), 12288
R_MLSTM = 13312
R_GATE = R_MLSTM + LH * LV
R_SINK = R_GATE + 2 * LH
N_ROWS = R_SINK + SH

K_ID, K_ONE = 0, 128
K_BLOCK = 256
K_TRI, K_SWA, K_CAUS, K_INV = K_BLOCK, K_BLOCK + 128, K_BLOCK + 384, K_BLOCK + 896
K_END_1 = K_INV + 32
K_ADM, K_DIST, K_SLOPE = K_BLOCK, K_BLOCK + 512, K_BLOCK + 1024
N_CONST = K_SLOPE + AH


def alibi_slopes(n):
    p = 2 ** int(math.floor(math.log2(n)))
    return [2.0 ** (-8.0 * (i + 1) / p) for i in range(p)] + \
           [2.0 ** (-4.0 * (2 * i + 1) / p) for i in range(n - p)]


def constants():
    c = np.zeros((P, N_CONST), np.float32)
    c2 = np.zeros((P, N_CONST), np.float32)
    q = np.arange(P)[:, None]
    k = np.arange(P)[None, :]
    c[:, K_ID:K_ID + P] = np.eye(P)
    c[:, K_ONE:K_ONE + P] = 1.0
    c[:, K_TRI:K_TRI + P] = q <= k
    causal = np.where(k <= q, 0.0, NEG)
    c[:, K_SWA:K_SWA + P] = np.where(k > q, 0.0, NEG)
    c[:, K_SWA + P:K_SWA + 2 * P] = causal
    c[:, K_CAUS + 384:K_CAUS + 512] = causal
    c2[:, K_ADM + 384:K_ADM + 512] = np.where((k >= 64) & (q < 64), NEG, 0.0)
    c2[:, K_DIST:K_DIST + 512] = np.abs(q - np.arange(512)[None, :] + 384)
    inv = np.float32(1.0) / np.power(np.float32(10000.0), np.arange(0, 64, 2, dtype=np.float32) / np.float32(64))
    c[:, K_INV:K_INV + 32] = inv[None, :]
    c2[:, K_SLOPE:K_SLOPE + AH] = -np.asarray(alibi_slopes(AH), np.float32)[None, :] * P ** 0.5
    return np.concatenate([c[:, :K_END_1], c2[:, K_BLOCK:]], axis=1)


class Signal:

    every = []

    def __init__(self, nc, name):
        self.sem, self.n, self.trip = nc.alloc_semaphore(name), 0, None
        Signal.every.append(self)

    def value(self, more=0):
        n = self.n + more
        return n if self.trip is None else self.trip + n

    def now(self, more=0):
        return self.sem, self.value(more)

    def mark(self, ins, by=1):
        ins.then_inc(self.sem, by)
        return self.expect(by)

    def expect(self, by):
        self.n += by
        return self.now()


@contextmanager
def loop(nc, trips, engines, per_trip):
    before = {s: s.n for s in Signal.every}
    with nc.Fori(0, trips, engines=engines) as i:
        for s, by in per_trip.items():
            s.trip = i * by
        yield i
    real = {s: s.n - before[s] for s in Signal.every if s.n != before[s]}
    assert real == {s: b for s, b in per_trip.items() if b}, {s.sem.name: b for s, b in real.items()}
    for s, by in per_trip.items():
        s.trip, s.n = None, before[s] + trips * by


def weave(*lists):
    at = [((i + 0.5) / len(steps), n, i) for n, steps in enumerate(lists) for i in range(len(steps))]
    for _, n, i in sorted(at):
        lists[n][i]()


def wait(engine, *tokens):
    for sem, value in tokens:
        if isinstance(value, int) and value <= 0:
            continue
        engine.wait_ge(sem, value)


APART_CONV, APART_GATE = 7, 13

PER_TWO_UNITS = {"split_hi": 2, "split_lo": 2, "unit_used": 2, "raw_even": 16, "raw_odd": 16,
                 "bank0_read": 1, "bank1_read": 1, "bank2_read": 1, "bank3_read": 1}
PER_CONV = {**PER_TWO_UNITS, "group_full": 2, "dve_done": 33 - APART_CONV, "act_done": APART_CONV,
            "pool_done": APART_CONV - 1}
PER_GATE3 = {**PER_TWO_UNITS, "group_full": 14, "bank4_read": 3, "bank5_read": 3, "bank6_read": 3,
             "bank7_read": 3, "dve_done": 113 - APART_GATE, "act_done": APART_GATE, "pool_done": 3 + APART_GATE}
PER_GATE4 = {**PER_TWO_UNITS, "group_full": 50, "bank4_read": 12, "bank5_read": 12, "bank6_read": 12,
             "bank7_read": 12, "act_done": 18, "dve_done": 70, "pool_done": 16}


def build(nc, x_in, mem_in, mem2_in, pos_in, cols_in, rows_in, const_in, weights_in, out):
    pe, act, dve, pool, sp = nc.tensor, nc.scalar, nc.vector, nc.gpsimd, nc.sync
    Signal.every = []
    sig = lambda name: Signal(nc, name)
    loaded = sig("loaded")
    mem_there = [sig("mem_there"), sig("mem2_there")]
    x_there = sig("x_there")
    parked = sig("parked")
    mem_park = nc.dram_tensor("mem_park", (2, P, 2048), F32, kind="Internal").ap()
    stored = sig("stored")
    pooled = sig("pool_loads")
    in_row_a, in_row_b = sig("in_row_a"), sig("in_row_b")
    raw = [sig("raw_even"), sig("raw_odd")]
    hi, lo = sig("split_hi"), sig("split_lo")
    used = sig("unit_used")
    full = sig("group_full")
    free = [sig(f"bank{b}_read") for b in range(8)]
    A, V, G = sig("act_done"), sig("dve_done"), sig("pool_done")
    n_units = weights_in.shape[0]

    at = [16512]

    def place(name, shape, dtype=F32, offset=None):
        size = 4 * int(np.prod(shape[1:]))
        if offset is None:
            offset, at[0] = at[0], at[0] + (size + 31) // 32 * 32
        return nc.alloc_sbuf_tensor_at(name, shape, dtype, offset=offset)

    const = place("const", [P, N_CONST])
    cols = place("cols", [P, N_COLS])
    row_a = place("row_a", [P, D])
    row_b = place("row_b", [P, D])
    small = place("small", [P, 256])
    rotary = place("rotary", [P, 2, NT, 32])
    minus_half = small[:, 240:256]
    rms_eps, ln_eps = small[:, 224:228], small[:, 228:232]
    mix_squares, mix_root = small[:, 80:88], small[:, 88:92]
    x_root = small[:, 0:4]
    small_rows = place("small_rows", [P, 32])
    x_res = place("x_res", [P, NT, D])
    x_base = at[0]
    XH = place("XH", [P, KB, SEQ], F32R)
    XL = place("XL", [P, KB, SEQ], F32R)
    RAW = [place(f"RAW{j}", [P, UNIT]) for j in range(2)]
    WH = [place(f"WH{j}", [P, UNIT], F32R) for j in range(2)]
    WL = [place(f"WL{j}", [P, UNIT], F32R) for j in range(2)]
    big = at[0]
    BIG = (229344 - big) // 32 * 32
    assert BIG >= 2 * FB * SEQ * 4, BIG
    S_buf = [place(f"S{j}", [P, SEQ], offset=x_base + 2048 * j) for j in range(4)]
    T_buf = [place(f"T{j}", [P, SEQ], offset=x_base + 8192 + 2048 * j) for j in range(4)]
    scratch = [S_buf, T_buf]
    c_row = place("c_row", [P, LH, SEQ], offset=x_base + 16384)
    scr = place("scr", [P, 2048], offset=x_base + 24576)
    angles = place("angles", [P, 384], offset=big + 32768)
    mix_x = place("mix_x", [P, NT, D], offset=x_base)
    HH = place("HH", [P, FB, SEQ], F32R, offset=big)
    HL = place("HL", [P, FB, SEQ], F32R, offset=big + FB * SEQ * 4)
    xn = place("xn", [P, NT, D], offset=big + 73728)
    mix_b = place("mix_b", [P, NT, D], offset=big)
    proj = place("proj", [P, NT, A_IN], offset=big)
    mem_kv1 = [place("mem_kv1_0", [P, 2, 2, 256], offset=big + 41088),
               place("mem_kv1_1", [P, 2, 2, 256], offset=big + 2 * FB * SEQ * 4)]
    assert BIG >= 2 * FB * SEQ * 4 + 4096
    m2_parts = [place(f"m2_{part}", [P, KB, MEM], F32R, offset=big + 16384 + 8192 * j)
                for j, part in enumerate(("high", "low"))]
    mem_kv2 = [place(f"mem_kv2_{l}", [P, 2048], offset=big + 8192 * l) for l in range(2)]
    qkT = place("qkT", [P, 2 * LH, SEQ], offset=big + 45184)
    mixed = place("mixed", [P, NT, D], offset=big + 61568)
    mqT = place("mqT", [P, 2, SEQ], offset=big + 77952)
    q_tok = place("q_tok", [P, NT, D], offset=big)
    kv_tok = place("kv_tok", [P, NT, 2 * SKV * HD], offset=big + 16384)
    kT = place("kT", [P, 2, SEQ], offset=big + 24576)
    kT_swapped = place("kT_swapped", [P, 2, SEQ], offset=big + 28672)
    qT = place("qT", [P, KB, SEQ], offset=big + 45184)
    Y = place("Y", [P, MIXB, SEQ], offset=big)
    gate = place("gate", [P, MIXB, SEQ], offset=big + 32768)
    YH = place("YH", [P, KB, SEQ], F32R, offset=big + 32768)
    misc = big + 65536
    YL = place("YL", [P, KB, SEQ], F32R, offset=misc)
    squared = [place(f"squared{j}", [P, SEQ], offset=misc + 16384 + 2048 * j) for j in range(4)]
    mean = place("mean", [P, SEQ], offset=misc + 24576)[:, :]
    dev = place("dev", [P, SEQ], offset=misc + 26624)[:, :]
    PAD = TAPS - 1
    CH = CB // 2
    conv_in = [place("conv_in_0", [P, CH, SEQ + PAD], offset=big + 32768),
               place("conv_in_1", [P, CH, SEQ + PAD], offset=misc)]
    kv2 = [place("kv2_0", [P, 2048], offset=misc + 13056), place("kv2_1", [P, 2048], offset=misc + 12288)]
    S_mem = [place(f"Sm{j}", [P, MEM], offset=misc + 21248 + 1024 * j) for j in range(4)]
    T_mem = [place(f"Tm{j}", [P, MEM], offset=misc + 25344 + 1024 * j) for j in range(3)]
    assert 65536 + 28416 + 2048 <= BIG
    row_at = 16512 + 4 * N_CONST // 32 * 32 + 32 * (4 * N_CONST % 32 > 0) + (4 * N_COLS + 31) // 32 * 32
    q_now = [place(f"q_now{j}", [P, P], offset=row_at + 512 * j) for j in range(4)]
    apart_taps = place("apart_taps", [P, SEQ], offset=misc + 28416)
    products = [place(f"product{j}", [P, SEQ], offset=misc + 21248 + 2048 * j) for j in range(2)]
    odd_taps = place("odd_taps", [P, SEQ], offset=row_at + 2048)
    dkT = place("dkT", [P, SEQ], offset=misc)
    d_val = place("d_val", [P, NT, P], offset=misc + 2048)
    sel = place("sel", [P, NT, SEQ], offset=misc + 4096)
    qiT = place("qiT", [P, 4, SEQ], offset=misc + 20480)
    wi = place("wi", [P, NT, IH], offset=misc + 28672)
    top8 = place("top8", [P, 8], offset=misc + 28800)
    ranking = [place(f"ranking{j}", [P, SEQ], offset=big + 32768 + 2048 * j) for j in range(2)]
    assert 65536 + 28832 <= BIG
    kiT = place("kiT", [P, SEQ], offset=row_at)
    wiT = place("wiT", [P, SEQ], offset=row_at + 2048)
    dvT = place("dvT", [P, SEQ], offset=row_at + 4096)
    relu = [place(f"relu{j}", [P, SEQ], offset=row_at + 4096 + 2048 * j) for j in range(2)]
    S_dsa = [place(f"Sd{j}", [P, SEQ], offset=o) for j, o in enumerate(
        (misc + 20480, misc + 22528, misc + 24576, row_at + 6144))]
    q_dsa = [place(f"q_dsa{j}", [P, P], offset=misc + 26624 + 512 * j) for j in range(4)]
    T_dsa = [place(f"Td{j}", [P, SEQ], offset=row_at + 2048 * j) for j in range(3)]

    bank = [nc.alloc_psum_tensor(f"bank{b}", [P, SEQ], F32) for b in range(8)]
    ring = [0, 0]

    def product_bank():
        b = ring[0] % 4
        ring[0] += 1
        wait(pe, free[b].now())
        return b

    spare = [4, 4]

    def spare_bank():
        b = spare[0] + ring[1] % spare[1]
        ring[1] += 1
        wait(pe, free[b].now())
        return b

    ident = const[:, K_ID:K_ID + P]
    ones = const[:, K_ONE:K_ONE + P]

    def col(base, k):
        return cols[:, base + k:base + k + 1]

    G.mark(pool.memset(minus_half, -0.5))
    G.mark(pool.memset(rms_eps, EPS))
    wait(pool, G.mark(pool.memset(ln_eps, LN_EPS)))

    pos = place("pos", [P, NT], I32, offset=big + 36864)
    mem_tok = [place(f"mem_tok{m}", [P, MEMT, D], offset=big + 57344 + 8192 * m) for m in range(2)]
    load_memory = lambda m, src: mem_there[m].mark(
        sp.dma_start(mem_tok[m][:, :, :], src[0].rearrange("(t p) d -> p t d", p=P)), 16)
    t_mem = [load_memory(0, mem_in)]
    loaded.mark(sp.dma_start(const[:, 0:K_END_1], const_in[:, 0:K_END_1]), 16)
    loaded.mark(sp.dma_start(cols[:, :], cols_in), 16)
    t_loaded = loaded.mark(sp.dma_start(pos[:, :], pos_in), 16)
    t_rows = pooled.mark(pool.dma_start(
        small_rows[:, 0:2 * LH + SH],
        rows_in[R_GATE:N_ROWS].rearrange("(a n) -> a n", a=1).partition_broadcast(P)), 16)

    def quiet():
        return [s.now() for s in (A, V, G, full, used, lo, *free)]

    def load_row(dst, start, n=D):
        wait(pool, *quiet())
        src = rows_in[start:start + n].rearrange("(a n) -> a n", a=1).partition_broadcast(P)
        return (in_row_a if dst is row_a else in_row_b).mark(pool.dma_start(dst[:, 0:n], src), 16)

    for j in range(2):
        sp.dma_start(RAW[j][:, :], weights_in[j]).then_inc(raw[j].sem, 16)
    t_mem.append(load_memory(1, mem2_in))
    t_x = x_there.mark(sp.dma_start(x_res[:, :, :], x_in[0].rearrange("(t p) d -> p t d", p=P)), 16)
    with nc.Fori(1, n_units // 2, engines=[ENG.SP]) as i:
        for j in range(2):
            sp.wait_ge(lo.sem, i * 2 + (j - 1))
            sp.dma_start(RAW[j][:, :], weights_in[i * 2 + j]).then_inc(raw[j].sem, 16)

    rest_by = [dve]

    def low_parts_on(engine):
        rest_by[0] = engine
        wait(engine, lo.now())

    def split_next():
        j = hi.n % 2
        if hi.trip is None and hi.n >= n_units:
            return
        wait(act, raw[j].expect(16), used.now())
        t = hi.mark(act.activation(WH[j][:, :], RAW[j][:, :], ACT.Copy))
        wait(rest_by[0], t)
        lo.mark(rest_by[0].tensor_tensor(WL[j][:, :], RAW[j][:, :], WH[j][:, :].bitcast(F32), ALU.subtract))

    def split_pieces():
        state = {}

        def piece(q):
            if q == 0:
                state["slot"] = hi.n % 2
                wait(act, raw[state["slot"]].expect(16), used.now())
            j, s, last = state["slot"], slice(q * UNIT // 4, (q + 1) * UNIT // 4), q == 3
            t = (hi if last else A).mark(act.activation(WH[j][:, s], RAW[j][:, s], ACT.Copy))
            wait(dve, t)
            (lo if last else V).mark(dve.tensor_tensor(WL[j][:, s], RAW[j][:, s], WH[j][:, s].bitcast(F32),
                                                       ALU.subtract))
        return [lambda q=q: piece(q) for q in range(4)]

    def three_passes(ps, ah, al, bh, bl, first, last):
        pe.matmul(ps, ah, bh, start=first, stop=False)
        pe.matmul(ps, ah, bl, start=False, stop=False)
        return pe.matmul(ps, al, bh, start=False, stop=last)

    def unit_steps(n, epilogue, widths=(P, P), first=0, source=(XH, XL), split=True, spread=False):
        state, results, steps = {}, [], []

        def begin():
            state["slot"] = used.n % 2
            wait(pe, (lo.sem, used.value(1)))

        def block(c, w, at, kb):
            if kb == 0:
                state["bank"] = product_bank()
            j, b = state["slot"], state["bank"]
            s = slice(kb * 256 + at, kb * 256 + at + w)
            mm = three_passes(bank[b][0:w, 0:n], WH[j][:, s], WL[j][:, s], source[0][:, kb, first:first + n],
                              source[1][:, kb, first:first + n], kb == 0, kb == KB - 1)
            if kb == KB - 1:
                results.append((b, (used if c == len(widths) - 1 else full).mark(mm)))

        def end():
            epilogue(results)
            if split and not spread:
                split_next()

        at = 0
        steps.append(begin)
        for c, w in enumerate(widths):
            steps += [lambda c=c, w=w, at=at, kb=kb: block(c, w, at, kb) for kb in range(KB)]
            at += w
        if spread:
            for q, piece in enumerate(split_pieces()):
                steps[4 * q + 2] = lambda piece=piece, step=steps[4 * q + 2]: (step(), piece())
        steps.append(end)
        return steps

    def unit_features(n, epilogue, widths=(P, P), first=0):
        for step in unit_steps(n, epilogue, widths, first):
            step()

    def chunk_steps(n, k_blocks, tiles, tokens, epilogue, per_unit=4, first=0, ready=None):
        banks, results = [], []

        def unit(k0, split=True):
            ks = range(k0, min(k0 + per_unit, k_blocks))
            end = ks[-1] == k_blocks - 1
            j = used.n % 2
            wait(pe, (lo.sem, used.value(1)))
            if ready is not None:
                wait(pe, ready[ks[-1]])
            for t in range(tiles):
                if k0 == 0:
                    banks.append(product_bank())
                for kb in ks:
                    th, tl, k = tokens(kb)
                    tt = slice(first + t * P, first + (t + 1) * P)
                    s = slice((kb - k0) * n, (kb - k0 + 1) * n)
                    mm = three_passes(bank[banks[t]][:, 0:n], th[:, k, tt], tl[:, k, tt],
                                      WH[j][:, s], WL[j][:, s], kb == 0, kb == k_blocks - 1)
                if t == tiles - 1:
                    token = used.mark(mm)
                elif end:
                    token = full.mark(mm)
                if end:
                    results.append((banks[t], token))
            if end:
                epilogue(results)
            if split:
                split_next()

        return [lambda k0=k0, **more: unit(k0, **more) for k0 in range(0, k_blocks, per_unit)]

    def chunk_tokens(*args, **more):
        for step in chunk_steps(*args, **more):
            step()

    from_x = lambda kb: (XH, XL, kb)
    from_y = lambda kb: (XH, XL, kb) if kb < KB else (YH, YL, kb - KB)
    from_h = lambda kb: (HH, HL, kb)

    def settle():
        dve.tensor_copy(small[:, 204:205], ident[:, 0:1])

    def inverse_root(v, eps):
        t = V.mark(dve.tensor_scalar(v, v, eps, None, ALU.add))
        wait(pool, t)
        t = G.mark(pool.tensor_tensor(v, v, minus_half[:, 0:v.shape[-1]], ALU.pow))
        wait(dve, t)

    def rms_scale(src, tiles, ready, junk=None):
        wait(act, *ready)
        wait(dve, *ready)
        junk = junk or (scr[:, 0:D], scr[:, D:2 * D])
        for t in range(tiles):
            if t % 2:
                A.mark(act.activation(junk[0], src[:, t, :], ACT.Square, scale=1.0 / 32,
                                      accum_out=small[:, t:t + 1]))
            else:
                V.mark(dve.tensor_tensor_reduce(junk[1], src[:, t, :], src[:, t, :], 1.0 / D, 0.0,
                                                ALU.mult, ALU.add, small[:, t:t + 1]))
            wait(act, A.now())
            wait(dve, V.now())
        wait(dve, A.now())
        inverse_root(small[:, 0:tiles], EPS)

    def turn_split(src, tiles, ready, g=None, b=None, first=0, target=(XH, XL)):
        n = tiles * P
        wait(pe, *ready)
        for kb in range(KB):
            k = spare_bank()
            for t in range(tiles):
                mm = pe.transpose(bank[k][:, t * P:(t + 1) * P], src[:, t, kb * P:(kb + 1) * P], ident)
            token = full.mark(mm)
            ps = bank[k][:, 0:n]
            high, low = (part[:, kb, first:first + n] for part in target)
            wait(act, token)
            wait(dve, token)
            if b is not None:
                plain = scr2[kb % 2][:, 0:n]
                h = A.mark(act.activation(high, ps, ACT.Identity, scale=col(g, kb), bias=col(b, kb)))
                wait(dve, h)
                v = free[k].mark(dve.tensor_scalar(plain, ps, col(g, kb), col(b, kb), ALU.mult, ALU.add))
                wait(dve, v)
                V.mark(dve.tensor_tensor(low, plain, high.bitcast(F32), ALU.subtract))
            else:
                scale = 1.0 if g is None else col(g, kb)
                h = A.mark(act.activation(high, ps, ACT.Copy, scale=scale))
                wait(dve, h)
                free[k].mark(dve.scalar_tensor_tensor(out=low, in0=ps, scalar=scale, in1=high.bitcast(F32),
                                                      op0=ALU.mult, op1=ALU.subtract))
        wait(pe, V.now(), *[f.now() for f in free[4:]])

    scr2 = [place(f"scr2_{j}", [P, MEM], offset=big + 53248 + 1024 * j) for j in range(2)]

    def root_on_pool(v, eps, ready):
        wait(pool, *ready)
        wait(pool, G.mark(pool.tensor_tensor(v, v, eps[:, 0:v.shape[-1]], ALU.add)))
        return G.mark(pool.tensor_tensor(v, v, minus_half[:, 0:v.shape[-1]], ALU.pow))

    def turn_tile(src, t, ready):
        wait(pe, *ready)
        banks = []
        for half in range(2):
            k = spare_bank()
            for q in range(4):
                kb = 4 * half + q
                mm = pe.transpose(bank[k][:, q * P:(q + 1) * P], src[:, t, kb * P:(kb + 1) * P], ident)
            banks.append((k, full.mark(mm)))
        return banks

    def parts_of_tile(t, banks):
        for half, (k, token) in enumerate(banks):
            ps = bank[k][:, :].rearrange("p (q n) -> p q n", q=4)
            high = XH[:, 4 * half:4 * half + 4, t * P:(t + 1) * P]
            low = XL[:, 4 * half:4 * half + 4, t * P:(t + 1) * P]
            wait(act, token)
            h = A.mark(act.activation(high, ps, ACT.Copy))
            wait(dve, h)
            free[k].mark(dve.tensor_tensor(low, ps, high.bitcast(F32), ALU.subtract))

    def norm_steps(mix=None, row=None, pre=None):
        if mix is not None:
            wait(pool, *bank_tokens())
            two = mix_squares.rearrange("p (t c) -> p t c", c=2)
            total = G.mark(pool.tensor_tensor(mix_root, two[:, :, 0], two[:, :, 1], ALU.add))
            t_root = root_on_pool(mix_root, rms_eps, [total])
        for e in (act, dve):
            wait(e, *[s.now() for s in (A, V, full, used, *free)])
        rooted, turned = {}, {}

        def square(t, ready):
            if pre is None:
                rooted[t] = ready
                return
            wait(act, *ready)
            root = x_root[:, t:t + 1]
            a = A.mark(act.activation(xn[:, t, :], x_res[:, t, :], ACT.Square, scale=1.0 / 32, accum_out=root))
            rooted[t] = [root_on_pool(root, rms_eps, [a])]

        if mix is None:
            for t in range(NT):
                square(t, [])
        else:
            wait(dve, t_root, row)
            for t in range(NT):
                scaled = V.mark(dve.scalar_tensor_tensor(out=mix_b[:, t, :], in0=mix[:, t, :],
                                                         scalar=mix_root[:, t:t + 1], in1=row_a[:, :],
                                                         op0=ALU.mult, op1=ALU.mult))
                engine, done = (pool, G) if t == 2 else (dve, V)
                wait(engine, scaled)
                added = done.mark(engine.tensor_tensor(x_res[:, t, :], x_res[:, t, :], mix_b[:, t, :], ALU.add))
                square(t, [added])
            wait(act, V.now())

        def scale_and_turn(t):
            if pre is None:
                turned[t] = turn_tile(x_res, t, rooted[t])
                return
            wait(dve, pre, *rooted[t])
            v = V.mark(dve.scalar_tensor_tensor(out=xn[:, t, :], in0=x_res[:, t, :], scalar=x_root[:, t:t + 1],
                                                in1=row_b[:, :], op0=ALU.mult, op1=ALU.mult))
            turned[t] = turn_tile(xn, t, [v])

        def both(step):
            if step < NT:
                scale_and_turn(step)
            if step:
                parts_of_tile(step - 1, turned[step - 1])

        return [lambda step=step: both(step) for step in range(NT + 1)]

    def norm_and_turn(*args, **more):
        for step in norm_steps(*args, **more):
            step()
        wait(pe, *[f.now() for f in free[4:]])

    def copy_out(dst, sums=None):
        def epilogue(results):
            for t, (b, token) in enumerate(results):
                wait(act, token)
                ps = bank[b][:, 0:dst(t).shape[-1]]
                copied = act.activation(dst(t), ps, ACT.Copy)
                if sums is None:
                    free[b].mark(copied)
                else:
                    wait(act, A.mark(copied))
                    free[b].mark(act.activation(ps, ps, ACT.Square, scale=1.0 / 32, accum_out=sums(t)))
        return epilogue

    compute = [ENG.PE, ENG.Activation, ENG.DVE]

    def signals(per):
        return {s: per[s.sem.name] for s in Signal.every if s.sem.name in per}

    def weights_per_trip(units, more):
        per = {hi: units, lo: units, used: units, raw[0]: 8 * units, raw[1]: 8 * units}
        for s, by in more.items():
            per[s] = per.get(s, 0) + by
        return per

    def chunks(count, n, k_blocks, tokens, dst, sums=None):
        per = {full: NT - 1, free[0]: 1, free[1]: 1, free[2]: 1, free[3]: 1, A: NT if sums else 0}
        with loop(nc, count, compute, weights_per_trip(-(-k_blocks // 4), per)) as i:
            chunk_tokens(n, k_blocks, NT, tokens,
                         copy_out(lambda t: dst(t, i * n), sums and (lambda t: sums(t, i))))

    squares_of_mix = lambda t, chunk: mix_squares[:, bass.ds(chunk + 2 * t, 1)]

    bank_tokens = lambda: [f.now() for f in free]

    def staggered(count, stages, delays):
        for step in range(count + delays[-1]):
            yield [(stage, step - d) for stage, d in reversed(list(zip(stages, delays))) if 0 <= step - d < count]

    def pipeline(jobs, delays=(0, 2, 3, 4), beside=()):
        def emit(step):
            for s, i in step:
                job, stages = jobs[i]
                stages[s](i, job)

        spare[:] = [0, 8]
        weave([lambda step=step: emit(step) for step in staggered(len(jobs), range(4), delays)], beside)
        spare[:] = [4, 4]

    stat = lambda kind, i: small[:, 16 + 8 * kind + i % 8:17 + 8 * kind + i % 8]

    def turn_probabilities(i, width, ready):
        wait(pe, ready)
        k = spare_bank()
        for c in range(width // P):
            mm = pe.transpose(bank[k][:, c * P:(c + 1) * P], scratch[0][i % len(scratch[0])][:, c * P:(c + 1) * P], ident)
        token = full.mark(mm)
        wait(act, token)
        return free[k].mark(act.activation(scratch[1][i % len(scratch[1])][:, 0:width], bank[k][:, 0:width], ACT.Copy))

    def softmax(i, k, width, scale, token, mask=None, sink=None):
        S = scratch[0][i % len(scratch[0])][:, 0:width]
        ps = bank[k][:, 0:width]
        wait(dve, token)
        if mask is not None:
            start = NEG if sink is None else sink
            if not isinstance(V.now()[1], int):
                settle()
            v = free[k].mark(dve.tensor_tensor_reduce(S, ps, mask, scale, start, ALU.add, ALU.max, stat(0, i)))
        else:
            v = V.mark(dve.tensor_reduce(stat(0, i), ps, AX.X, ALU.max))
        wait(dve, v)
        v = V.mark(dve.tensor_scalar(stat(1, i), stat(0, i), -1.0 if mask is not None else -scale, None, ALU.mult))
        wait(act, v)
        if mask is not None:
            a = A.mark(act.activation(S, S, ACT.Exp, bias=stat(1, i), accum_out=stat(2, i)))
        else:
            a = free[k].mark(act.activation(S, ps, ACT.Exp, bias=stat(1, i), scale=scale, accum_out=stat(2, i)))
        if sink is not None:
            a = A.mark(act.activation(stat(3, i), sink, ACT.Exp, bias=stat(1, i)))
        return a

    def reciprocal_of_sum(i, ready, sink=False, width=0):
        wait(dve, ready)
        if sink:
            wait(dve, V.mark(dve.tensor_tensor(stat(2, i), stat(2, i), stat(3, i), ALU.add)))
        v = V.mark(dve.reciprocal(stat(4, i), stat(2, i)))
        if width:
            wait(dve, v)
            S = scratch[0][i % len(scratch[0])][:, 0:width]
            v = V.mark(dve.tensor_scalar(S, S, stat(4, i), None, ALU.mult))
        return v

    def memory_first(layer, qb):
        got = {}

        def scores(i, job):
            t, h = job
            r = slice(64 * (h % 2), 64 * (h % 2) + 64)
            k = spare_bank()
            mm = pe.matmul(bank[k][:, 0:MEM], qb(h // 2)[r, t * P:(t + 1) * P], mem_kv1[layer][r, 0, h // 2, :],
                           start=True, stop=True)
            got[i] = softmax(i, k, MEM, HD ** -0.5, full.mark(mm))

        def divide(i, job):
            got[i] = got[i], reciprocal_of_sum(i, got[i])

        def turn(i, job):
            got[i] = got[i][1], turn_probabilities(i, MEM, got[i][0])

        def values(i, job):
            t, h = job
            recip, token = got[i]
            wait(pe, token)
            k = spare_bank()
            for c in range(MEMT):
                mm = pe.matmul(bank[k][:, 0:64], scratch[1][i % len(scratch[1])][:, c * P:(c + 1) * P],
                               mem_kv1[layer][:, 1, c, h * 64:(h + 1) * 64], start=c == 0, stop=c == MEMT - 1)
            wait(dve, full.mark(mm), recip)
            free[k].mark(dve.tensor_scalar(mixed[:, t, 768 + h * 64:832 + h * 64], bank[k][:, 0:64],
                                           stat(4, i), None, ALU.mult))

        return [((t, h), [scores, divide, turn, values]) for t in range(NT) for h in range(4)]

    def memory_keys():
        junk = (row_a[:, :], row_b[:, :])
        m1, m2 = mem_tok
        rms_scale(m1, MEMT, [t_mem[0]], junk)
        for t in range(MEMT):
            token = V.mark(dve.tensor_scalar(m1[:, t, :], m1[:, t, :], small[:, t:t + 1], None, ALU.mult))
        turn_split(m1, MEMT, [token, t_loaded], g=GC_MEM[0])
        turn_split(m1, MEMT, [], g=GC_MEM[1], first=MEM)
        pre = load_row(row_b, R_MIXPRE[0])

        def keys(dst):
            def epilogue(results):
                for c, (b, token) in enumerate(results):
                    wait(act, token)
                    free[b].mark(act.activation(dst(c), bank[b][:, 0:MEM], ACT.Copy))
            return epilogue

        def first_block(layer):
            unit_features(MEM, keys(lambda c: mem_kv1[layer][:, 0, c, :]), first=MEM * layer)
            chunk_tokens(256, KB, MEMT, from_x, copy_out(lambda t: mem_kv1[layer][:, 1, t, :]), per_unit=8,
                         first=MEM * layer)

        wait(dve, t_mem[1])
        for t in range(MEMT):
            layer_norm_stats(m2[:, t, :], t)
            token = V.mark(dve.tensor_scalar(m2[:, t, :], m2[:, t, :], small[:, 100 + 2 * t:101 + 2 * t],
                                             small[:, 101 + 2 * t:102 + 2 * t], ALU.subtract, ALU.mult))
        first_block(0)
        turn_split(m2, MEMT, [token], g=GC_LNG, b=GC_LNB, target=m2_parts)
        first_block(1)
        for e in (act, dve):
            wait(e, t_x)
        turns = norm_steps(pre=pre)
        from_m2 = lambda kb: (*m2_parts, kb)
        products = []
        for layer in range(2):
            kv = mem_kv2[layer]
            for u in range(2):
                products += unit_steps(MEM, keys(lambda c, kv=kv, u=u: kv[:, (2 * u + c) * MEM:(2 * u + c + 1) * MEM]),
                                       source=m2_parts)
            products += chunk_steps(512, KB, MEMT, from_m2,
                                    copy_out(lambda t, kv=kv: kv[:, 1024 + 512 * t:1536 + 512 * t]))

            def park(layer=layer, kv=kv):
                wait(act, *bank_tokens())
                parked.mark(act.dma_start(mem_park[layer], kv[:, :]), 16)
            products.append(park)
        weave(products[:2 * KB + 10], turns)
        turned = [f.now() for f in free[4:]]
        rotary_tables()
        for step in products[2 * KB + 10:]:
            step()
        wait(pe, *turned)

    def fetch_memory(layer):
        wait(pool, parked.now(), *quiet())
        return pooled.mark(pool.dma_start(kv2[layer][:, :], mem_park[layer]), 16)

    def layer_norm_stats(src, t):
        for c in range(2):
            v = V.mark(dve.bn_stats(small[:, 108 + 12 * t + 6 * c:114 + 12 * t + 6 * c], src[:, 512 * c:512 * c + 512]))
        wait(dve, v)
        v = V.mark(dve.bn_aggr(small[:, 100 + 2 * t:102 + 2 * t], small[:, 108 + 12 * t:120 + 12 * t]))
        wait(dve, v)
        inverse_root(small[:, 101 + 2 * t:102 + 2 * t], LN_EPS)

    def mlstm():
        wait(dve, *bank_tokens())
        gates = scr[:, 0:32].rearrange("p (t g) -> p t g", g=8)
        nlf = scr[:, 64:80].rearrange("p (t h) -> p t h", h=4)
        nb = scr[:, 96:112].rearrange("p (t h) -> p t h", h=4)
        cc = scr[:, 128:144].rearrange("p (t h) -> p t h", h=4)
        e_f = scr[:, 160:176].rearrange("p (t h) -> p t h", h=4)
        for t in range(NT):
            v = V.mark(dve.tensor_tensor(gates[:, t, :], proj[:, t, COL_GATE:COL_GATE + 8], small_rows[:, 0:8], ALU.add))
        wait(act, v)
        a = A.mark(act.activation(gates, gates, ACT.Tanh, scale=1.0 / SOFTCAP))
        wait(act, a)
        a = A.mark(act.activation(e_f, gates[:, :, 4:8], ACT.Exp, scale=-SOFTCAP))
        wait(act, a)
        logs = A.mark(act.activation(nlf, e_f, ACT.Ln, bias=1.0))
        for h in range(2 * LH):
            k = spare_bank()
            for t in range(NT):
                mm = pe.transpose(bank[k][0:LQK, t * P:(t + 1) * P], proj[:, t, h * LQK:(h + 1) * LQK], ident)
            wait(act, full.mark(mm))
            free[k].mark(act.activation(qkT[0:LQK, h, :], bank[k][0:LQK, :], ACT.Copy,
                                        scale=1.0 if h < LH else LQK ** -0.5))
        for c in range(2):
            k = spare_bank()
            for t in range(NT):
                mm = pe.transpose(bank[k][:, t * P:(t + 1) * P],
                                  proj[:, t, COL_MQ + c * P:COL_MQ + (c + 1) * P], ident)
            wait(act, full.mark(mm))
            free[k].mark(act.activation(mqT[:, c, :], bank[k][:, :], ACT.Copy))
        wait(pe, logs)
        k = spare_bank()
        for t in range(NT):
            for s in range(t + 1):
                mm = pe.matmul(bank[k][:, t * 4:t * 4 + 4], const[:, K_TRI:K_TRI + P] if s == t else ones,
                               nlf[:, s, :], start=s == 0, stop=s == t)
        wait(dve, full.mark(mm))
        v = free[k].mark(dve.tensor_copy(scr[:, 96:112], bank[k][:, 0:16]))
        wait(dve, v)
        v = V.mark(dve.scalar_tensor_tensor(out=cc, in0=gates[:, :, 0:4], scalar=SOFTCAP, in1=nb,
                                            op0=ALU.mult, op1=ALU.add))
        wait(dve, v)
        diag = scr[:, 512:2048].rearrange("p (j s) -> p j s", j=3)
        for h in range(LH):
            if h:
                wait(dve, full.now())
            for t in range(NT):
                v = V.mark(dve.tensor_scalar(diag[:, h % 3, t * P:(t + 1) * P], ident, cc[:, t, h:h + 1], None, ALU.mult))
            wait(pe, v)
            k = spare_bank()
            token = full.mark(pe.matmul(bank[k][:, :], ones, diag[:, h % 3, :], start=True, stop=True))
            wait(act, token)
            free[k].mark(act.activation(c_row[:, h, :], bank[k][:, :], ACT.Copy))
        wait(dve, *bank_tokens())
        wait(pe, *bank_tokens())
        got = {}

        def scores(i, job):
            t, h = job
            w = (t + 1) * P
            E = scratch[1][i % len(scratch[1])][:, 0:w]
            k = spare_bank()
            token = full.mark(pe.matmul(bank[k][:, 0:w], qkT[0:LQK, h, t * P:(t + 1) * P], qkT[0:LQK, LH + h, 0:w],
                                        start=True, stop=True))
            wait(dve, full.now())
            v = V.mark(dve.tensor_tensor_reduce(E, c_row[:, h, 0:w], const[:, K_CAUS + 512 - w:K_CAUS + 512],
                                                1.0, NEG, ALU.add, ALU.max, stat(0, i)))
            wait(dve, v)
            v = V.mark(dve.tensor_scalar(stat(1, i), stat(0, i), -1.0, None, ALU.mult))
            wait(act, v)
            A.mark(act.activation(E, E, ACT.Exp, bias=stat(1, i)))
            got[i] = k, token, A.mark(act.activation(stat(3, i), nb[:, t, h:h + 1], ACT.Exp, bias=stat(1, i)))

        def divide(i, job):
            w = (job[0] + 1) * P
            k, token, a = got[i]
            wait(dve, a, token)
            v = free[k].mark(dve.tensor_tensor_reduce(scratch[0][i % len(scratch[0])][:, 0:w], bank[k][:, 0:w],
                                                      scratch[1][i % len(scratch[1])][:, 0:w], 1.0, 0.0,
                                                      ALU.mult, ALU.add, stat(2, i)))
            wait(dve, v)
            d = V.mark(dve.scalar_tensor_tensor(out=stat(2, i), in0=stat(2, i), scalar=-1.0, in1=stat(2, i),
                                                op0=ALU.mult, op1=ALU.max))
            wait(dve, d)
            d = V.mark(dve.tensor_scalar(stat(2, i), stat(2, i), stat(3, i), None, ALU.max))
            wait(dve, d)
            r = V.mark(dve.reciprocal(stat(4, i), stat(2, i)))
            got[i] = v, r

        def turn(i, job):
            got[i] = got[i][1], turn_probabilities(i, (job[0] + 1) * P, got[i][0])

        def values(i, job):
            t, h = job
            recip, token = got[i]
            wait(pe, token)
            k = spare_bank()
            for s in range(t + 1):
                mm = pe.matmul(bank[k][:, 0:LV], scratch[1][i % len(scratch[1])][:, s * P:(s + 1) * P],
                               proj[:, s, COL_V + h * LV:COL_V + (h + 1) * LV], start=s == 0, stop=s == t)
            wait(act, full.mark(mm), recip)
            m = free[k].mark(act.activation(mixed[:, t, h * LV:(h + 1) * LV], bank[k][:, 0:LV], ACT.Copy,
                                            scale=stat(4, i)))

        pipeline([((t, h), [scores, divide, turn, values]) for t in range(NT) for h in range(LH)])

    def head_norm():
        squares = small[:, 64:80]
        done = {}
        before = bank_tokens()

        def square(i):
            t, h = divmod(i, LH)
            junk = scr[:, 512 + 256 * (i % 2):512 + 256 * (i % 2) + LV]
            wait(act, *(before if i < 2 else [done[i - 2]]))
            done[i] = A.mark(act.activation(junk, mixed[:, t, h * LV:(h + 1) * LV], ACT.Square,
                                            scale=LV ** -0.5, accum_out=squares[:, i:i + 1]))

        def root():
            wait(pool, done[NT * LH - 1])
            v = G.mark(pool.tensor_scalar(squares, squares, EPS, None, ALU.add))
            wait(pool, v)
            done["root"] = G.mark(pool.tensor_tensor(squares, squares, minus_half, ALU.pow))

        def sigmoid():
            for t in range(NT):
                o = proj[:, t, COL_O:COL_O + 768]
                done["gate", t] = A.mark(act.activation(o, o, ACT.Sigmoid))

        def scale(t):
            wait(dve, done["root"], in_row_b.now())
            for h in range(LH):
                s = slice(h * LV, (h + 1) * LV)
                v = V.mark(dve.scalar_tensor_tensor(out=mixed[:, t, s], in0=mixed[:, t, s],
                                                    scalar=squares[:, 4 * t + h:4 * t + h + 1],
                                                    in1=row_b[:, s], op0=ALU.mult, op1=ALU.mult))
            wait(dve, v, done["gate", t])
            V.mark(dve.tensor_tensor(mixed[:, t, 0:768], mixed[:, t, 0:768], proj[:, t, COL_O:COL_O + 768], ALU.mult))

        return [lambda i=i: square(i) for i in range(NT * LH)] + [root, sigmoid] + \
            [lambda t=t: scale(t) for t in range(NT)]

    def rotary_tables():
        two_pi = 2 * math.pi
        c1 = float(np.float32(6.28125))
        c2 = float(np.float32(two_pi - c1))
        c3 = float(two_pi - c1 - c2)
        magic = 12582912.0
        ang, turns, r = (angles[:, 128 * j:128 * j + 128] for j in range(3))
        pf = small[:, 8:12]
        wait(dve, t_loaded)
        v = V.mark(dve.tensor_copy(pf, pos[:, :]))
        wait(dve, v)
        for t in range(NT):
            v = V.mark(dve.tensor_scalar(ang[:, t * 32:(t + 1) * 32], const[:, K_INV:K_INV + 32], pf[:, t:t + 1],
                                         None, ALU.mult))
        for kind, shift in ((1, 0.0), (0, 0.25)):
            wait(dve, v)
            v = V.mark(dve.tensor_scalar(turns, ang, 1.0 / two_pi, shift, ALU.mult, ALU.add))
            wait(dve, v)
            v = V.mark(dve.tensor_scalar(turns, turns, magic, None, ALU.add))
            wait(dve, v)
            v = V.mark(dve.tensor_scalar(turns, turns, -magic, None, ALU.add))
            src = ang
            for c in (c1, c2, c3):
                wait(dve, v)
                v = V.mark(dve.scalar_tensor_tensor(out=r, in0=turns, scalar=-c, in1=src, op0=ALU.mult, op1=ALU.add))
                src = r
            wait(dve, v)
            v = V.mark(dve.tensor_scalar(r, r, shift * two_pi, math.pi, ALU.add, ALU.min))
            wait(dve, v)
            v = V.mark(dve.tensor_scalar(r, r, -math.pi, None, ALU.max))
            wait(act, v)
            a = A.mark(act.activation(rotary[:, kind, :, :], r.rearrange("p (t f) -> p t f", t=NT), ACT.Sin))
            wait(dve, a)

    def rotate(buf, heads, ready, first=0):
        wait(dve, *ready)
        n = heads * 32
        for t in range(NT):
            v4 = buf[:, t, first * HD:(first + heads) * HD].rearrange("p (h two f) -> p h two f", two=2, f=32)
            x1, x2 = v4[:, :, 0, :], v4[:, :, 1, :]
            cos = rotary[:, 0, t, :].rearrange("p (a f) -> p a f", a=1).to_broadcast([P, heads, 32])
            sin = rotary[:, 1, t, :].rearrange("p (a f) -> p a f", a=1).to_broadcast([P, heads, 32])
            s1 = qT[:, 0, 0:n].rearrange("p (h f) -> p h f", f=32)
            s2 = qT[:, 1, 0:n].rearrange("p (h f) -> p h f", f=32)
            V.mark(dve.tensor_tensor(s1, x1, sin, ALU.mult))
            v = V.mark(dve.tensor_tensor(s2, x2, sin, ALU.mult))
            wait(dve, v)
            V.mark(dve.tensor_tensor(x1, x1, cos, ALU.mult))
            v = V.mark(dve.tensor_tensor(x2, x2, cos, ALU.mult))
            wait(dve, v)
            V.mark(dve.tensor_tensor(x1, x1, s2, ALU.subtract))
            v = V.mark(dve.tensor_tensor(x2, x2, s1, ALU.add))
            wait(dve, v)

    def turn_all(src, blocks, dst):
        for c in range(blocks):
            k = spare_bank()
            for t in range(NT):
                mm = pe.transpose(bank[k][:, t * P:(t + 1) * P], src[:, t, c * P:(c + 1) * P], ident)
            wait(act, full.mark(mm))
            free[k].mark(act.activation(dst[:, c, :], bank[k][:, :], ACT.Copy))

    def sliding_keys():
        wait(pe, V.now())
        turn_all(kv_tok, 2, kT)
        wait(dve, *bank_tokens())
        for c in range(2):
            for r in range(2):
                V.mark(dve.tensor_copy(kT_swapped[64 * r:64 * r + 64, c, :], kT[64 - 64 * r:128 - 64 * r, c, :]))

    def sliding():
        wait(pe, V.now(), *bank_tokens())
        turn_all(q_tok, KB, qT)
        wait(pe, *bank_tokens())
        wait(dve, *bank_tokens())
        got = {}

        def scores(i, job):
            t, h = job
            g = h // 3
            r = slice(64 * (h % 2), 64 * (h % 2) + 64)
            keys = kT if h % 2 == g % 2 else kT_swapped
            w = P if t == 0 else 2 * P
            k = spare_bank()
            mm = pe.matmul(bank[k][:, 0:w], qT[r, h // 2, t * P:(t + 1) * P],
                           keys[r, g // 2, (t + 1) * P - w:(t + 1) * P], start=True, stop=True)
            got[i] = softmax(i, k, w, HD ** -0.5, full.mark(mm), mask=const[:, K_SWA + 256 - w:K_SWA + 256],
                             sink=small_rows[:, 8 + h:9 + h])

        def divide(i, job):
            got[i] = got[i], reciprocal_of_sum(i, got[i], sink=True)

        def turn(i, job):
            got[i] = got[i][1], turn_probabilities(i, P if job[0] == 0 else 2 * P, got[i][0])

        def values(i, job):
            t, h = job
            recip, token = got[i]
            wait(pe, token)
            k = spare_bank()
            n = 1 if t == 0 else 2
            for c in range(n):
                mm = pe.matmul(bank[k][:, 0:HD], scratch[1][i % len(scratch[1])][:, c * P:(c + 1) * P],
                               kv_tok[:, t - n + 1 + c, 256 + (h // 3) * HD:256 + (h // 3 + 1) * HD],
                               start=c == 0, stop=c == n - 1)
            wait(dve, full.mark(mm), recip)
            free[k].mark(dve.tensor_scalar(mixed[:, t, h * HD:(h + 1) * HD], bank[k][:, 0:HD],
                                           stat(4, i), None, ALU.mult))

        own = [((t, h), [scores, divide, turn, values]) for t in range(NT) for h in range(SH)]
        pipeline(own + memory_first(1, lambda c: qT[:, 6 + c, :]), (0, 2, 3, 5))

    silu = [row_b[:, 0:512], row_b[:, 512:1024]]

    def feed_forward(layer, next_row):
        row = load_row(row_a, R_FFNPOST[layer])
        per = weights_per_trip(2, {A: 2, V: 2, full: 2, free[0]: 1, free[1]: 1, free[2]: 1, free[3]: 1})
        with loop(nc, FB // 2, compute, per) as i:
            for j in range(2):
                def hidden(results):
                    (bg, tg), (bu, tu) = results
                    wait(act, tg, V.now())
                    a = free[bg].mark(act.activation(silu[j], bank[bg][:, :], ACT.Silu))
                    wait(dve, a, tu, A.now())
                    v = free[bu].mark(dve.tensor_tensor(silu[j], silu[j], bank[bu][:, :], ALU.mult))
                    wait(act, v)
                    a = A.mark(act.activation(HH[:, i * 2 + j, :], silu[j], ACT.Copy))
                    wait(dve, a)
                    V.mark(dve.tensor_tensor(HL[:, i * 2 + j, :], silu[j],
                                             HH[:, i * 2 + j, :].bitcast(F32), ALU.subtract))
                unit_features(SEQ, hidden)
        pre = next_row and load_row(row_b, next_row)
        wait(pe, V.now(), A.now())
        chunks(2, 512, FB, from_h, lambda t, c: mix_x[:, t, bass.ds(c, 512)], squares_of_mix)
        norm_and_turn(mix_x, row, pre)

    def out_first(layer, row):
        turn_split(mixed, NT, [V.now(), A.now(), *bank_tokens()])
        pre = load_row(row_b, R_FFNPRE[layer])
        chunks(2, 512, KB, from_x, lambda t, c: mix_b[:, t, bass.ds(c, 512)], squares_of_mix)
        norm_and_turn(mix_b, row, pre)

    split_next()
    split_next()
    wait(dve, t_rows)
    memory_keys()

    wait(act, parked.now())
    chunks(6, A_CHUNK, KB, from_x, lambda t, c: proj[:, t, bass.ds(c, A_CHUNK)])
    load_row(row_b, R_MLSTM, LH * LV)
    row = load_row(row_a, R_MIXPOST[0])
    mlstm()
    wait(act, V.now())
    wait(pe, *bank_tokens())
    pipeline(memory_first(0, lambda c: mqT[:, c, :]), (0, 2, 3, 5), beside=head_norm())
    out_first(0, row)
    feed_forward(0, R_KV)

    wait(dve, load_row(row_b, R_MIXPRE[1]))
    scaled = [V.mark(dve.scalar_tensor_tensor(out=xn[:, t, :], in0=x_res[:, t, :], scalar=x_root[:, t:t + 1],
                                              in1=row_b[:, :], op0=ALU.mult, op1=ALU.mult)) for t in range(NT)]
    chunk_tokens(512, KB, NT, from_x, copy_out(lambda t: kv_tok[:, t, :]))

    turned = [turn_tile(xn, 0, scaled[:1])]
    for t in range(NT):
        if t + 1 < NT:
            turned.append(turn_tile(xn, t + 1, scaled[t + 1:t + 2]))
        parts_of_tile(t, turned[t])
    wait(pe, *[f.now() for f in free[4:]])
    rotate(kv_tok, SKV, bank_tokens())
    for c in range(2):
        chunk_tokens(512, KB, NT, from_x, copy_out(lambda t: q_tok[:, t, 512 * c:512 * c + 512]))
        if c == 0:
            sliding_keys()
        rotate(q_tok, (KB, SH - KB)[c], bank_tokens(), first=KB * c)
    row = load_row(row_a, R_MIXPOST[1])
    sliding()
    out_first(1, row)
    feed_forward(1, None)

    def to_feature(dst, first, func=ACT.Copy):
        def of(unit):
            def epilogue(results):
                for c, (b, token) in enumerate(results):
                    wait(act, token)
                    free[b].mark(act.activation(dst[:, unit * 2 + (first + c), :], bank[b][:, :], func))
            return epilogue
        return of

    order = [*range(AH, MIXB), *range(AH)]
    ready = {}

    def gated(p):
        c = order[p]
        v = V.mark(dve.tensor_tensor(Y[:, c, :], Y[:, c, :], gate[:, c, :], ALU.mult))
        wait(act, v)
        h, _, k = from_y(p)
        ready[p] = A.mark(act.activation(h[:, k, :], Y[:, c, :], ACT.Copy))

    def low_part(p):
        h, l, k = from_y(p)
        wait(dve, ready[p])
        ready[p] = V.mark(dve.tensor_tensor(l[:, k, :], Y[:, order[p], :], h[:, k, :].bitcast(F32), ALU.subtract))

    def out_chunk(c):
        def epilogue(results):
            for t, (b, token) in enumerate(results):
                x = x_res[:, t, c * 512:(c + 1) * 512]
                wait(dve, token)
                v = free[b].mark(dve.scalar_tensor_tensor(out=x, in0=x, scalar=ALPHA, in1=bank[b][:, :],
                                                          op0=ALU.mult, op1=ALU.add))
                wait(dve, v)
                V.mark(dve.bn_stats(small[:, 108 + 12 * t + 6 * c:114 + 12 * t + 6 * c], x))
        return chunk_steps(512, MIXB, NT, from_y, epilogue, ready=ready)

    def second_norm(gain_and_bias, store):
        wait(dve, V.now())
        for t in range(NT):
            v = V.mark(dve.bn_aggr(small[:, 100 + 2 * t:102 + 2 * t], small[:, 108 + 12 * t:120 + 12 * t]))
        spread = small[:, 100:108].rearrange("p (t s) -> p t s", s=2)[:, :, 1]
        wait(dve, root_on_pool(spread, ln_eps, [v]), *gain_and_bias)
        turned = {}

        def finish(t):
            x = x_res[:, t, :]
            v = V.mark(dve.scalar_tensor_tensor(out=x, in0=x, scalar=small[:, 100 + 2 * t:101 + 2 * t],
                                                in1=row_a[:, :], op0=ALU.subtract, op1=ALU.mult))
            wait(dve, v)
            return V.mark(dve.scalar_tensor_tensor(out=x, in0=x, scalar=small[:, 101 + 2 * t:102 + 2 * t],
                                                   in1=row_b[:, :], op0=ALU.mult, op1=ALU.add))

        if store:
            for t in range(NT):
                wait(act, finish(t))
                stored.mark(act.dma_start(out[0, t * P:(t + 1) * P, :], x_res[:, t, :]), 16)
            return
        for step in range(NT + 1):
            if step < NT:
                turned[step] = turn_tile(x_res, step, [finish(step)])
            if step:
                parts_of_tile(step - 1, turned[step - 1])
        wait(pe, *[f.now() for f in free[4:]])

    def staged_jobs(jobs, q_ring, S_ring, T_ring):
        got, read, steps = {}, {}, []

        def stage_query(i, job):
            wait(pool, read[i - 4] if i >= 4 else full.now())
            got[i] = G.mark(pool.tensor_copy(q_ring[i % 4][:, :], job["query"]))

        def scores(i, job):
            wait(pe, got[i])
            w = job["width"]
            k = spare_bank()
            token = read[i] = full.mark(pe.matmul(bank[k][:, 0:w], q_ring[i % 4][:, :], job["keys"], start=True, stop=True))
            mask = None
            if job["bias"] is not None:
                S = S_ring[i % len(S_ring)][:, 0:w]
                wait(dve, token)
                wait(dve, job["bias"](S))
                mask = S
            scratch[:] = [S_ring, T_ring]
            got[i] = softmax(i, k, w, P ** -0.5, token, mask=mask)

        def divide(i, job):
            scratch[:] = [S_ring, T_ring]
            got[i] = reciprocal_of_sum(i, got[i], width=job["width"])

        def turn(i, job):
            scratch[:] = [S_ring, T_ring]
            got[i] = turn_probabilities(i, job["width"], got[i])

        def values(i, job):
            wait(pe, got[i])
            k = spare_bank()
            n = job["width"] // P
            for c in range(n):
                mm = pe.matmul(bank[k][:, 0:P], job["value"](c), T_ring[i % len(T_ring)][:, c * P:(c + 1) * P],
                               start=c == 0, stop=c == n - 1)
            wait(act, full.mark(mm))
            free[k].mark(act.activation(job["out"], bank[k][:, 0:P], ACT.Copy))

        for step in staggered(len(jobs), [stage_query, scores, divide, turn, values], (0, 2, 4, 5, 6)):
            def emit(step=step):
                for stage, i in step:
                    stage(i, jobs[i])
            steps += [emit] + [lambda: None] * (len(step) < 5)
        return steps

    def memory_jobs(t, layer):
        kv = kv2[layer]
        return [{"query": Y[:, AH + h, bass.ds(t * P, P)], "keys": kv[:, h * MEM:(h + 1) * MEM], "width": MEM,
                 "bias": None, "value": lambda c, h=h: kv[:, 1024 + 512 * c + h * P:1024 + 512 * c + (h + 1) * P],
                 "out": Y[:, AH + h, bass.ds(t * P, P)]} for h in range(4)]

    def gate_units(i, spread=False):
        return [step for j in range(2)
                for step in unit_steps(SEQ, to_feature(gate, 0, ACT.Silu)(i * 2 + j), spread=spread)]

    everyone = [ENG.PE, ENG.Activation, ENG.DVE, ENG.Pool]

    fetch_memory(0)
    t_const = pooled.mark(pool.dma_start(const[:, K_BLOCK:N_CONST], const_in[:, K_END_1:]), 16)
    unit_features(SEQ, to_feature(Y, AH)(0))
    unit_features(SEQ, to_feature(Y, AH + 2)(0))
    wait(dve, *quiet())
    for half in conv_in:
        v = V.mark(dve.memset(half[:, :, 0:PAD], 0.0))

    def convolve(out, src, c, n, apart=0, products=None):
        own = TAPS - apart
        before = V.now(), G.now()
        added = {}

        def weight(tap):
            return cols[:, bass.ds(c * TAPS + (GC_TAP + tap), 1)]

        def pair(k):
            for tap in range(k, min(k + 2, own)):
                acc = odd_taps[:, 0:n] if tap % 2 else out
                if tap == 0:
                    V.mark(dve.tensor_scalar(acc, src(tap), weight(tap), cols[:, bass.ds(c + GC_CB, 1)],
                                             ALU.mult, ALU.add))
                elif tap == 1:
                    V.mark(dve.tensor_scalar(acc, src(tap), weight(tap), None, ALU.mult))
                else:
                    wait(dve, V.now(-1))
                    V.mark(dve.scalar_tensor_tensor(out=acc, in0=src(tap), scalar=weight(tap), in1=acc,
                                                    op0=ALU.mult, op1=ALU.add))

        def other(m):
            product = products[m % 2] if m else apart_taps
            wait(act, before[0] if m == 0 else before[1] if m < 3 else added[m - 2])
            added[m] = A.mark(act.activation(product[:, 0:n], src(own + m), ACT.Copy, scale=weight(own + m)))
            if m:
                wait(pool, added[m - 1], added[m])
                added[m] = G.mark(pool.tensor_tensor(apart_taps[:, 0:n], apart_taps[:, 0:n], product[:, 0:n], ALU.add))

        def both():
            wait(dve, V.now())
            v = V.mark(dve.tensor_tensor(out, out, odd_taps[:, 0:n], ALU.add))
            wait(dve, v)
            if apart:
                wait(dve, added[apart - 1])
                wait(dve, V.mark(dve.tensor_tensor(out, out, apart_taps[:, 0:n], ALU.add)))

        return [lambda k=k: pair(k) for k in range(0, own, 2)] + [both], \
            [lambda m=m: other(m) for m in range(apart)]

    low_parts_on(pool)
    for half in range(2):
        with loop(nc, CH // 2, everyone, signals(PER_CONV)) as i:
            made = {}

            def glu(j):
                def epilogue(results):
                    (ba, ta), (bg, tg) = results
                    wait(act, tg)
                    a = free[bg].mark(act.activation(silu[j], bank[bg][:, :], ACT.Sigmoid))
                    wait(dve, a, ta)
                    made[j] = free[ba].mark(dve.tensor_tensor(conv_in[half][:, i * 2 + j, PAD:PAD + SEQ], silu[j],
                                                              bank[ba][:, :], ALU.mult))
                return epilogue
            c = i + 3 * half
            first_unit, second_unit = unit_steps(SEQ, glu(0)), unit_steps(SEQ, glu(1))
            taps = convolve(Y[:, c, :], lambda k: conv_in[0][:, c, k:k + SEQ], c, SEQ, APART_CONV, products)
            for step in first_unit:
                step()
            wait(dve, made[0])
            wait(act, made[0])
            weave(second_unit, *taps)

    wait(pe, t_const, *quiet())
    for e in (act, dve, pool):
        wait(e, *quiet())
    with loop(nc, NT, everyone, signals(PER_GATE3)) as i:
        whole, others = convolve(Y[:, i + CH, :], lambda k: conv_in[1][:, i, k:k + SEQ], i + CH, SEQ,
                                 APART_GATE, silu)
        quarters = []
        for j in range(2):
            quarters += convolve(Y[:, CB - 2 + j, bass.ds(i * P, P)],
                                 lambda k, j=j: conv_in[1][:, CH - 2 + j, bass.ds(i * P + k, P)], CB - 2 + j, P)[0]
        weave(gate_units(i), staged_jobs(memory_jobs(i, 0), q_now, S_mem, T_mem), quarters + whole, others)
    low_parts_on(dve)
    scratch[:] = [S_buf, T_buf]

    for e in (pe, dve, act):
        wait(e, *quiet())
    gain_and_bias = load_row(row_a, R_APG), load_row(row_b, R_APB)
    for p in range(4):
        gated(p)
    for p in range(4):
        low_part(p)
    k = spare_bank()
    for c in range(CB):
        mm = pe.matmul(bank[k][:, :], ones, Y[:, c, :], start=c == 0, stop=c == CB - 1)
    wait(dve, full.mark(mm))
    v = free[k].mark(dve.tensor_scalar(mean, bank[k][:, :], 1.0 / CONVW, None, ALU.mult))
    wait(dve, v)
    chunk = out_chunk(0)
    chunk[0](split=False)
    k = spare_bank()
    squares = {}
    for c in range(CB):
        v = V.mark(dve.tensor_tensor(Y[:, c, :], Y[:, c, :], mean, ALU.subtract))
        wait(act, v)
        if c >= 4:
            wait(act, squares[c - 4])
        a = A.mark(act.activation(squared[c % 4][:, :], Y[:, c, :], ACT.Square))
        wait(pe, a)
        squares[c] = full.mark(pe.matmul(bank[k][:, :], ones, squared[c % 4][:, :], start=c == 0, stop=c == CB - 1))
    split_next()
    wait(dve, squares[CB - 1])
    v = free[k].mark(dve.tensor_scalar(dev, bank[k][:, :], 1.0 / CONVW, LN_EPS, ALU.mult, ALU.add))
    wait(act, v)
    a = A.mark(act.activation(dev, dev, ACT.Sqrt))
    wait(dve, a)
    v = V.mark(dve.reciprocal(dev, dev))
    wait(dve, v)
    smooth = {}

    def normalized(p):
        c = order[p]
        wait(act, V.mark(dve.tensor_tensor(Y[:, c, :], Y[:, c, :], dev, ALU.mult)))
        smooth[p] = A.mark(act.activation(Y[:, c, :], Y[:, c, :], ACT.Silu, scale=col(GC_CG, c), bias=col(GC_CBETA, c)))

    def gated_after(p):
        wait(dve, smooth[p])
        gated(p)

    for step in staggered(CB, [normalized, gated_after, low_part], (0, 2, 3)):
        for stage, i in step:
            stage(MIXB - CB + i)
    for step in chunk[1:] + out_chunk(1):
        step()
    second_norm(gain_and_bias, False)

    t_kv = fetch_memory(1)

    def into(targets):
        def epilogue(results):
            for (dst, w), (b, token) in zip(targets, results):
                wait(act, token)
                free[b].mark(act.activation(dst, bank[b][0:w, :], ACT.Copy))
        return epilogue

    unit_features(SEQ, into([(kiT[0:IHD, :], IHD), (wiT[0:IH, :], IH)]), widths=(IHD, IH))
    for u in range(2):
        unit_features(SEQ, into([(qiT[:, 2 * u, :], P), (qiT[:, 2 * u + 1, :], P)]))
    unit_features(SEQ, into([(dkT[:, :], P), (dvT[:, :], P)]))
    wait(pe, *bank_tokens())
    wait(dve, *bank_tokens())
    k = spare_bank()
    for t in range(NT):
        mm = pe.transpose(bank[k][:, t * P:(t + 1) * P], dvT[:, t * P:(t + 1) * P], ident)
    wait(act, full.mark(mm))
    free[k].mark(act.activation(d_val[:, :, :], bank[k][:, :].rearrange("p (t d) -> p t d", t=NT), ACT.Copy))
    k = spare_bank()
    for t in range(NT):
        mm = pe.transpose(bank[k][:, t * IH:(t + 1) * IH], wiT[0:IH, t * P:(t + 1) * P], const[0:IH, K_ID:K_ID + IH])
    wait(dve, full.mark(mm))
    free[k].mark(dve.tensor_copy(wi[:, :, :], bank[k][:, 0:NT * IH].rearrange("p (t h) -> p t h", t=NT)))
    V.mark(dve.tensor_copy(kiT[IHD:2 * IHD, :], kiT[0:IHD, :]))
    wait(dve, t_const)
    V.mark(dve.tensor_copy(sel[:, 0, 0:P], const[:, K_ADM + 384:K_ADM + 512]))
    for e in (pe, dve, act, pool):
        wait(e, *bank_tokens(), V.now())

    last_sum = [(V.sem, 0)] * 2
    summed = {}

    def index_scores(t):
        w = (t + 1) * P
        s = ranking[t % 2][:, 0:w]

        def index_head(h):
            r = slice(IHD * (h % 2), IHD * (h % 2) + IHD)
            k = spare_bank()
            token = full.mark(pe.matmul(bank[k][:, 0:w], qiT[r, h // 2, t * P:(t + 1) * P], kiT[r, 0:w],
                                        start=True, stop=True))
            wait(act, token, last_sum[h % 2])
            a = free[k].mark(act.activation(relu[h % 2][:, 0:w], bank[k][:, 0:w], ACT.Relu))
            wait(dve, a, last_sum[(h + 1) % 2])
            if h == 0:
                v = V.mark(dve.tensor_scalar(s, relu[0][:, 0:w], wi[:, t, h:h + 1], None, ALU.mult))
            else:
                v = V.mark(dve.scalar_tensor_tensor(out=s, in0=relu[h % 2][:, 0:w], scalar=wi[:, t, h:h + 1],
                                                    in1=s, op0=ALU.mult, op1=ALU.add))
            last_sum[h % 2] = v

        def admissible():
            wait(dve, last_sum[1])
            summed[t] = V.mark(dve.tensor_tensor(s, s, const[:, K_ADM + 512 - w:K_ADM + 512], ALU.add))

        return [lambda h=h: index_head(h) for h in range(IH)] + [admissible]

    def select(t):
        w = (t + 1) * P
        s = ranking[t % 2][:, 0:w]

        def take8():
            wait(dve, summed[t])
            v = V.mark(dve.max(top8[:, :], s))
            wait(dve, v)
            summed[t] = V.mark(dve.match_replace(s, top8[:, :], s, -3e38))

        def to_mask():
            wait(dve, summed[t])
            V.mark(dve.tensor_scalar(sel[:, t, 0:w], s, -2e38, NEG, ALU.is_gt, ALU.mult))

        return [take8] * (TOPK // 8) + [to_mask]

    weave(unit_steps(SEQ, to_feature(Y, AH)(0)) + unit_steps(SEQ, to_feature(Y, AH + 2)(0)), index_scores(1))
    for t in range(1, NT):
        both = unit_steps(SEQ, to_feature(Y, 4 * (t - 1))(0)) + \
            unit_steps(SEQ, to_feature(Y, 4 * t - 2)(0), split=t < NT - 1)
        weave(both, select(t), *([index_scores(t + 1)] if t + 1 < NT else []))

    for e in (pe, act, dve, pool):
        wait(e, t_kv, *quiet())
    with loop(nc, AH // 3, everyone, signals(PER_GATE4)) as i:
        jobs = []
        memory = memory_jobs(i, 1)
        for g in range(3):
            h = i * 3 + g
            for t in range(NT):
                w = (t + 1) * P

                def bias(S, h=h, t=t, w=w):
                    return V.mark(dve.scalar_tensor_tensor(
                        out=S, in0=const[:, K_DIST + 512 - w:K_DIST + 512],
                        scalar=const[:, bass.ds(h + K_SLOPE, 1)], in1=sel[:, t, 0:w],
                        op0=ALU.mult, op1=ALU.add))
                jobs.append({"query": Y[:, h, t * P:(t + 1) * P], "keys": dkT[:, 0:w], "width": w, "bias": bias,
                             "value": lambda c: d_val[:, c, :], "out": Y[:, h, t * P:(t + 1) * P]})
            jobs.append(memory[g])
        jobs.append(memory[3])
        weave(gate_units(i, spread=True), staged_jobs(jobs, q_dsa, S_dsa, T_dsa))
    split_next()
    scratch[:] = [S_buf, T_buf]
    gain_and_bias = load_row(row_a, R_BPG), load_row(row_b, R_BPB)
    for e in (dve, act):
        wait(e, *quiet())
    for step in staggered(MIXB, [gated, low_part], (0, 1)):
        for stage, p in step:
            stage(p)
    for step in out_chunk(0) + out_chunk(1):
        step()
    second_norm(gain_and_bias, True)
    wait(act, stored.now())


def pack_weights(a):
    units = []

    def add(block):
        flat = block.reshape(P, -1)
        unit = np.zeros((P, UNIT), np.float32)
        unit[:, :flat.shape[1]] = flat
        units.append(unit)

    def rows_of(w):
        return w.reshape(-1, P, w.shape[1]).transpose(1, 0, 2)

    def token_chunks(w, n, per_unit=4):
        r = rows_of(w)
        for c in range(0, w.shape[1], n):
            for k in range(0, r.shape[1], per_unit):
                add(r[:, k:k + per_unit, c:c + n])

    def feature_blocks(w, pairs):
        r = rows_of(w)
        for p in pairs:
            both = np.zeros((P, KB, 256), np.float32)
            at = 0
            for c, n in p:
                both[:, :, at:at + n] = r[:, :, c:c + n]
                at += n
            add(both)

    def memory_first(w):
        return np.concatenate([w[AH * P:], w[:AH * P]])

    def run(start, blocks):
        return [((start + 2 * P * i, P), (start + 2 * P * i + P, P)) for i in range(blocks // 2)]

    for layer in range(2):
        feature_blocks(a["w_mem_kv"][layer], run(0, 2))
        token_chunks(a["w_mem_kv"][layer][:, 256:], 256, per_unit=8)
    for w in (a["a_w_mkv_2"][0], a["b_w_mkv_2"][0]):
        feature_blocks(w, run(0, 4))
        token_chunks(w[:, 512:], 512)

    def first(layer):
        if layer == 0:
            token_chunks(a["w_in_a"][0], A_CHUNK)
        else:
            token_chunks(a["w_in_b"][0], 512)
        token_chunks(a["w_out"][layer], 512)
        feature_blocks(a["w_ffn_in"][layer], [((j * P, P), (DFF + j * P, P)) for j in range(FB)])
        token_chunks(a["w_ffn_out"][layer], 512)

    first(0)
    token_chunks(a["w_kv"], 512)
    first(1)
    w = a["a_w_in_2"][0]
    feature_blocks(w, run(2 * CONVW, 4))
    feature_blocks(w, [((j * P, P), (CONVW + j * P, P)) for j in range(CB)])
    feature_blocks(w, run(2 * CONVW + 512, MIXB))
    token_chunks(memory_first(a["a_w_out_2"][0]), 512)
    w = a["b_w_in_2"][0]
    at_kv = AH * P
    at_qi = at_kv + 2 * P
    at_ki = at_qi + IH * IHD
    at_mq = at_ki + IHD + IH
    feature_blocks(w, [((at_ki, IHD), (at_ki + IHD, IH))])
    feature_blocks(w, run(at_qi, 4))
    feature_blocks(w, run(at_kv, 2))
    feature_blocks(w, run(at_mq, 4))
    feature_blocks(w, run(0, AH))
    feature_blocks(w, run(at_mq + 512, MIXB))
    token_chunks(memory_first(a["b_w_out_2"][0]), 512)
    return np.stack(units)


def kernel(**inputs):
    from concourse import bacc
    from concourse.bass_utils import run_bass_kernel_spmd

    a = {k: np.asarray(v) for k, v in inputs.items()}

    def by_feature(v):
        return v.reshape(-1, P).T

    taps = a["a_conv_w_2"][0].reshape(TAPS, CB, P).transpose(2, 1, 0).reshape(P, CB * TAPS)
    cols = np.concatenate(
        [by_feature(v) for v in (a["g_mem"][0], a["g_mem"][1], a["mem_ln_g_2"], a["mem_ln_b_2"])]
        + [taps] + [by_feature(v) for v in (a["a_conv_b_2"][0], a["a_ln_g_2"][0], a["a_ln_b_2"][0])], axis=1)
    rows = np.concatenate(
        [a["g_mix_post"][0], a["g_ffn_post"][0], a["g_mix_post"][1], a["g_ffn_post"][1],
         a["a_post_g_2"][0], a["a_post_b_2"][0], a["b_post_g_2"][0], a["b_post_b_2"][0],
         a["g_mix_pre"][0], a["g_mix_pre"][1], a["g_ffn_pre"][0], a["g_ffn_pre"][1], a["g_kv"],
         a["g_mlstm_out"][0], a["b_gates_a"][0], a["sinks_b"][0]])
    arrays = {
        "x": a["x"], "mem": a["mem"], "mem_2": a["mem_2"],
        "positions": np.ascontiguousarray(a["positions"].reshape(NT, P).T),
        "cols": np.ascontiguousarray(cols), "rows": rows, "constants": constants(),
        "weights": pack_weights(a),
    }
    nc = bacc.Bacc("TRN2", target_bir_lowering=False, num_devices=1)
    args = [nc.dram_tensor(n, v.shape, mybir.dt.from_np(v.dtype), kind="ExternalInput").ap()
            for n, v in arrays.items()]
    out = nc.dram_tensor("out", (1, SEQ, D), F32, kind="ExternalOutput").ap()
    build(nc, *args, out)
    r = run_bass_kernel_spmd(nc, [arrays], core_ids=[0])
    return r.results[0]["out"]
```
